# Optimizing a Trainium2 kernel written in Bass

```python
import jax, jax.numpy as jnp
from jax import lax
import numpy as np

D_MODEL = 1024
BATCH = 1
SEQ = 512
DEPTH = 1

D_MIX = D_MODEL
D_A = D_MIX // 2
D_B = D_MIX - D_A
HEAD_A = 64
G_A = D_A // HEAD_A
HEAD_B = 64
H_B = D_B // HEAD_B
CHUNK = 128
DECAY_RANK = 64
ICLR_RANK = 64
LN_EPS = 1e-5
GN_EPS = 64e-5
ALPHA = (2 * DEPTH) ** 0.25
BETA = (8 * DEPTH) ** -0.25

N_COLS_A = 3 * D_A
N_COLS_B = 4 * D_B + DECAY_RANK + ICLR_RANK
N_COLS = N_COLS_A + N_COLS_B


def _layer_norm(x, g, b, eps):
    xf = x.astype(jnp.float32)
    mu = jnp.mean(xf, axis=-1, keepdims=True)
    var = jnp.mean(jnp.square(xf - mu), axis=-1, keepdims=True)
    y = (xf - mu) * lax.rsqrt(var + eps)
    return (y * g.astype(jnp.float32) + b.astype(jnp.float32)).astype(x.dtype)

def _token_shift(p, mu):
    prev = jnp.pad(p, ((0, 0), (1, 0), (0, 0)))[:, :-1]
    return p + mu * (prev - p)

def _rwkv7_scan(r, w, k, v, a, b):
    Bsz, T, H, N = r.shape
    seq_first = lambda z: jnp.swapaxes(z, 0, 1)
    xs = tuple(seq_first(z) for z in (r, w, k, v, a, b))

    def step(S, inp):
        r_t, w_t, k_t, v_t, a_t, b_t = inp
        sa = jnp.einsum('bhij,bhj->bhi', S, a_t)
        S = S * w_t[:, :, None, :] + sa[..., None] * b_t[:, :, None, :] + v_t[..., None] * k_t[:, :, None, :]
        y = jnp.einsum('bhij,bhj->bhi', S, r_t)
        return S, y

    S0 = jnp.zeros((Bsz, H, N, N), jnp.float32)
    _, ys = lax.scan(step, S0, xs)
    return jnp.swapaxes(ys, 0, 1)

def _gmlp_branch(p_a, ln_v_g, ln_v_b, w_spatial, b_spatial):
    Bsz, T, _ = p_a.shape
    u = jax.nn.gelu(p_a[..., :D_A])
    v = jax.nn.gelu(p_a[..., D_A:2 * D_A])
    gate = p_a[..., 2 * D_A:]
    v = v.reshape(Bsz, T, G_A, HEAD_A)
    v = _layer_norm(v, ln_v_g, ln_v_b, LN_EPS)
    v = v.reshape(Bsz, T // CHUNK, CHUNK, G_A, HEAD_A)
    causal = jnp.tril(jnp.ones((CHUNK, CHUNK), dtype=bool))
    w_m = jnp.where(causal[None], w_spatial, jnp.zeros((), w_spatial.dtype))
    v = jnp.einsum('gts,bcsgd->bctgd', w_m, v) + jnp.swapaxes(b_spatial, 0, 1)[None, None, :, :, None]
    v = v.reshape(Bsz, T, D_A)
    return u * v * jax.nn.silu(gate)

def _rwkv7_branch(p_b, mu_b, w0, w_up, a0, a_up, k_k, k_a, r_k, gn_g, gn_b):
    Bsz, T, _ = p_b.shape
    p_b = _token_shift(p_b, mu_b)
    o = 0
    r = p_b[..., o:o + D_B]; o += D_B
    k = p_b[..., o:o + D_B]; o += D_B
    v = p_b[..., o:o + D_B]; o += D_B
    gate = p_b[..., o:o + D_B]; o += D_B
    wd = p_b[..., o:o + DECAY_RANK]; o += DECAY_RANK
    ad = p_b[..., o:o + ICLR_RANK]

    w_raw = -jax.nn.softplus(-(w0 + jnp.tanh(wd) @ w_up)) - 0.5
    a = jax.nn.sigmoid(a0 + ad @ a_up)

    heads = lambda z: z.reshape(Bsz, T, H_B, HEAD_B).astype(jnp.float32)
    kk = heads(k * k_k)
    kk = kk * lax.rsqrt(jnp.sum(kk * kk, axis=-1, keepdims=True) + 1e-12)
    k = k * (1 + (a - 1) * k_a)
    rh, kh, vh, ah = heads(r), heads(k), heads(v), heads(a)
    decay = jnp.exp(-jnp.exp(heads(w_raw)))

    y = _rwkv7_scan(rh, decay, kh, vh, -kk, kk * ah)
    y = _layer_norm(y, gn_g, gn_b, GN_EPS)
    bonus = jnp.sum(rh * kh * r_k.astype(jnp.float32), axis=-1, keepdims=True) * vh
    y = (y + bonus).reshape(Bsz, T, D_B).astype(p_b.dtype)
    return y * jax.nn.silu(gate)

def first_inputs(seed: int = 0) -> dict:
    key = jax.random.key(seed)
    ks = jax.random.split(key, 24)
    f32 = jnp.float32
    nrm = lambda k, s, sc: jax.random.normal(k, s, f32) * sc
    return {
        "x": nrm(ks[0], (BATCH, SEQ, D_MODEL), 1.0),
        "c": nrm(ks[1], (BATCH, D_MODEL), 1.0),
        "w_ada": nrm(ks[2], (D_MODEL, 3 * D_MODEL), D_MODEL ** -0.5),
        "b_ada": nrm(ks[3], (3 * D_MODEL,), 0.02),
        "w_in": nrm(ks[4], (D_MODEL, N_COLS), D_MODEL ** -0.5),
        "mu_b": jax.random.uniform(ks[5], (N_COLS_B,), f32),
        "ln_v_g": 1.0 + nrm(ks[6], (G_A, HEAD_A), 0.05),
        "ln_v_b": nrm(ks[7], (G_A, HEAD_A), 0.02),
        "w_spatial": nrm(ks[8], (G_A, CHUNK, CHUNK), CHUNK ** -0.5),
        "b_spatial": 1.0 + nrm(ks[9], (G_A, CHUNK), 0.1),
        "w0": jax.random.uniform(ks[10], (D_B,), f32, -4.0, 1.0),
        "w_up": nrm(ks[11], (DECAY_RANK, D_B), 0.5 * DECAY_RANK ** -0.5),
        "a0": nrm(ks[12], (D_B,), 0.5),
        "a_up": nrm(ks[13], (ICLR_RANK, D_B), 0.5 * ICLR_RANK ** -0.5),
        "k_k": 0.85 + nrm(ks[14], (D_B,), 0.05),
        "k_a": 1.0 + nrm(ks[15], (D_B,), 0.05),
        "r_k": nrm(ks[16], (H_B, HEAD_B), 0.1),
        "gn_g": 1.0 + nrm(ks[17], (H_B, HEAD_B), 0.05),
        "gn_b": nrm(ks[18], (H_B, HEAD_B), 0.02),
        "w_out": nrm(ks[19], (D_MIX, D_MODEL), BETA * D_MIX ** -0.5),
        "ln_g": 1.0 + nrm(ks[20], (D_MODEL,), 0.05),
        "ln_b": nrm(ks[21], (D_MODEL,), 0.02),
    }

def first_block(x, c, w_ada, b_ada, w_in, mu_b, ln_v_g, ln_v_b, w_spatial, b_spatial,
              w0, w_up, a0, a_up, k_k, k_a, r_k, gn_g, gn_b, w_out, ln_g, ln_b):
    mod = jax.nn.silu(c) @ w_ada + b_ada
    shift, scale, gate = [m[:, None, :] for m in jnp.split(mod, 3, axis=-1)]
    for _ in range(DEPTH):
        h = x * (1 + scale) + shift
        p = h @ w_in
        out_a = _gmlp_branch(p[..., :N_COLS_A], ln_v_g, ln_v_b, w_spatial, b_spatial)
        out_b = _rwkv7_branch(p[..., N_COLS_A:], mu_b, w0, w_up, a0, a_up, k_k, k_a, r_k, gn_g, gn_b)
        o = jnp.concatenate([out_a, out_b], axis=-1) @ w_out
        x = _layer_norm(ALPHA * x + gate * o, ln_g, ln_b, LN_EPS)
    return x


DEPTH_2 = 2

N_MIXERS = 2
N_MLA = (DEPTH_2 + 1) // 2
N_HGRN = DEPTH_2 // 2

MLA_HEADS = 8
MLA_Q_LORA = 512
MLA_KV_LORA = 256
MLA_NOPE = 128
MLA_ROPE = 64
MLA_V = 128
ROPE_BASE = 10000.0
ATTN_BLOCK = 128

HGRN_HEADS = 8
HGRN_DK = D_MODEL // HGRN_HEADS
HGRN_DV = D_MODEL // HGRN_HEADS
HGRN_CHUNK = 32

D_FF = 4 * D_MODEL

EPS = 1e-6


def rms_norm(x, g):
    xf = x.astype(jnp.float32)
    y = xf * lax.rsqrt(jnp.mean(xf * xf, axis=-1, keepdims=True) + EPS)
    return (y * g.astype(jnp.float32)).astype(x.dtype)

def rope_cos_sin(positions):
    inv_freq = jnp.power(ROPE_BASE, -jnp.arange(0, MLA_ROPE, 2, dtype=jnp.float32) / MLA_ROPE)
    ang = positions.astype(jnp.float32)[..., None] * inv_freq
    return jnp.cos(ang), jnp.sin(ang)

def apply_rope(t, cos, sin):
    tf = t.astype(jnp.float32)
    t1, t2 = jnp.split(tf, 2, axis=-1)
    return jnp.concatenate([t1 * cos - t2 * sin, t1 * sin + t2 * cos], axis=-1).astype(t.dtype)

def mla_mixer(h, cos, sin, w_in, q_norm, kv_norm, w_uq, w_ukv, w_o):
    B, S, _ = h.shape
    H = MLA_HEADS
    proj = h @ w_in
    c_q, c_kv, k_r = jnp.split(proj, [MLA_Q_LORA, MLA_Q_LORA + MLA_KV_LORA], axis=-1)
    q = (rms_norm(c_q, q_norm) @ w_uq).reshape(B, S, H, MLA_NOPE + MLA_ROPE)
    q_nope = q[..., :MLA_NOPE]
    q_rope = apply_rope(q[..., MLA_NOPE:], cos[:, :, None, :], sin[:, :, None, :])
    kv = (rms_norm(c_kv, kv_norm) @ w_ukv).reshape(B, S, H, MLA_NOPE + MLA_V)
    k_nope, v = kv[..., :MLA_NOPE], kv[..., MLA_NOPE:]
    k_rope = apply_rope(k_r, cos, sin)
    scale = (MLA_NOPE + MLA_ROPE) ** -0.5
    nb = S // ATTN_BLOCK
    qn_b = q_nope.reshape(B, nb, ATTN_BLOCK, H, MLA_NOPE).transpose(1, 0, 2, 3, 4)
    qr_b = q_rope.reshape(B, nb, ATTN_BLOCK, H, MLA_ROPE).transpose(1, 0, 2, 3, 4)
    k_pos = jnp.arange(S)

    def block(args):
        qn, qr, blk = args
        s = (jnp.einsum('bqhd,bkhd->bhqk', qn, k_nope)
             + jnp.einsum('bqhr,bkr->bhqk', qr, k_rope)).astype(jnp.float32) * scale
        q_pos = blk * ATTN_BLOCK + jnp.arange(ATTN_BLOCK)
        s = jnp.where(q_pos[:, None] >= k_pos[None, :], s, -jnp.inf)
        p = jax.nn.softmax(s, axis=-1).astype(v.dtype)
        return jnp.einsum('bhqk,bkhd->bqhd', p, v)

    o = lax.map(block, (qn_b, qr_b, jnp.arange(nb)))
    o = o.transpose(1, 0, 2, 3, 4).reshape(B, S, H * MLA_V)
    return o @ w_o

def hgrn2_mixer(h, lb, w_in, o_norm, w_o):
    B, S, _ = h.shape
    H, DK, DV, C = HGRN_HEADS, HGRN_DK, HGRN_DV, HGRN_CHUNK
    nc = S // C
    HK, HV = H * DK, H * DV
    proj = h @ w_in
    q_x, f_x, i_x, g_x = jnp.split(proj, [HK, 2 * HK, 2 * HK + HV], axis=-1)

    def heads(t, d):
        return t.astype(jnp.float32).reshape(B, nc, C, H, d).transpose(0, 3, 1, 2, 4)

    f = lb + (1.0 - lb) * jax.nn.sigmoid(f_x.astype(jnp.float32))
    q = heads(jax.nn.silu(q_x.astype(jnp.float32)), DK)
    k = heads(1.0 - f, DK)
    log_f = heads(jnp.log(f), DK)
    v = heads(i_x, DV)

    b = jnp.cumsum(log_f, axis=3)
    b_ref = b[:, :, :, C // 2:C // 2 + 1, :]
    b_last = b[:, :, :, -1:, :]
    q_rel = q * jnp.exp(b - b_ref)
    k_rel = k * jnp.exp(b_ref - b)
    causal = jnp.tril(jnp.ones((C, C), dtype=bool))
    a = jnp.where(causal, jnp.einsum('bhncd,bhnsd->bhncs', q_rel, k_rel), 0.0)
    o_intra = jnp.einsum('bhncs,bhnse->bhnce', a, v)

    q_dec = q * jnp.exp(b)
    k_dec = k * jnp.exp(b_last - b)
    chunk_decay = jnp.exp(b_last[:, :, :, 0, :])

    def step(state, xs):
        qd, kd, vc, dec = xs
        o_inter = jnp.einsum('bhcd,bhde->bhce', qd, state)
        state = dec[..., None] * state + jnp.einsum('bhcd,bhce->bhde', kd, vc)
        return state, o_inter

    mv = lambda t: jnp.moveaxis(t, 2, 0)
    s0 = jnp.zeros((B, H, DK, DV), jnp.float32)
    _, o_inter = lax.scan(step, s0, (mv(q_dec), mv(k_dec), mv(v), mv(chunk_decay)))
    o = o_intra + jnp.moveaxis(o_inter, 0, 2)
    o = o.transpose(0, 2, 3, 1, 4).reshape(B, S, H, DV)
    gate = jax.nn.silu(g_x.astype(jnp.float32)).reshape(B, S, H, DV)
    o = rms_norm(o, o_norm) * gate
    return o.reshape(B, S, HV).astype(h.dtype) @ w_o

def sq_relu_mlp(h, w1, w2):
    a = jax.nn.relu(h @ w1)
    return (a * a) @ w2

def second_inputs(seed: int = 0) -> dict:
    key = jax.random.key(seed)
    ks = jax.random.split(key, 16)
    f32 = jnp.float32
    nrm = lambda k, shape, fan_in: jax.random.normal(k, shape, f32) * (fan_in ** -0.5)
    mla_in_w = MLA_Q_LORA + MLA_KV_LORA + MLA_ROPE
    hgrn_in_w = 3 * HGRN_HEADS * HGRN_DK + HGRN_HEADS * HGRN_DV
    return {
        "x": jax.random.normal(ks[0], (BATCH, SEQ, D_MODEL), f32),
        "positions": jnp.broadcast_to(jnp.arange(SEQ, dtype=jnp.int32), (BATCH, SEQ)),
        "norm_gains": 1.0 + 0.1 * jax.random.normal(ks[1], (DEPTH_2, 4, D_MODEL), f32),
        "mla_w_in": nrm(ks[2], (N_MLA, D_MODEL, mla_in_w), D_MODEL),
        "mla_q_norm": 1.0 + 0.1 * jax.random.normal(ks[3], (N_MLA, MLA_Q_LORA), f32),
        "mla_kv_norm": 1.0 + 0.1 * jax.random.normal(ks[4], (N_MLA, MLA_KV_LORA), f32),
        "mla_w_uq": nrm(ks[5], (N_MLA, MLA_Q_LORA, MLA_HEADS * (MLA_NOPE + MLA_ROPE)), MLA_Q_LORA),
        "mla_w_ukv": nrm(ks[6], (N_MLA, MLA_KV_LORA, MLA_HEADS * (MLA_NOPE + MLA_V)), MLA_KV_LORA),
        "mla_w_o": nrm(ks[7], (N_MLA, MLA_HEADS * MLA_V, D_MODEL), MLA_HEADS * MLA_V),
        "hgrn_w_in": nrm(ks[8], (N_HGRN, D_MODEL, hgrn_in_w), D_MODEL),
        "hgrn_lb_logits": 0.1 * jax.random.normal(ks[9], (DEPTH_2, HGRN_HEADS * HGRN_DK), f32),
        "hgrn_o_norm": 1.0 + 0.1 * jax.random.normal(ks[10], (N_HGRN, HGRN_DV), f32),
        "hgrn_w_o": nrm(ks[11], (N_HGRN, HGRN_HEADS * HGRN_DV, D_MODEL), HGRN_HEADS * HGRN_DV),
        "mlp_w1": nrm(ks[12], (DEPTH_2, D_MODEL, D_FF), D_MODEL),
        "mlp_w2": nrm(ks[13], (DEPTH_2, D_FF, D_MODEL), D_FF),
    }

def second_block(x, positions, norm_gains, mla_w_in, mla_q_norm, mla_kv_norm, mla_w_uq, mla_w_ukv,
              mla_w_o, hgrn_w_in, hgrn_lb_logits, hgrn_o_norm, hgrn_w_o, mlp_w1, mlp_w2):
    cos, sin = rope_cos_sin(positions)
    p = jax.nn.softmax(hgrn_lb_logits.astype(jnp.float32), axis=0)
    lower_bounds = jnp.cumsum(p, axis=0) - p[0]
    h = x
    for layer in range(DEPTH_2):
        slot = layer // N_MIXERS
        a = rms_norm(h, norm_gains[layer, 0])
        if layer % N_MIXERS == 0:
            m = mla_mixer(a, cos, sin, mla_w_in[slot], mla_q_norm[slot], mla_kv_norm[slot],
                          mla_w_uq[slot], mla_w_ukv[slot], mla_w_o[slot])
        else:
            m = hgrn2_mixer(a, lower_bounds[layer], hgrn_w_in[slot], hgrn_o_norm[slot], hgrn_w_o[slot])
        h = h + rms_norm(m, norm_gains[layer, 1])
        a = rms_norm(h, norm_gains[layer, 2])
        h = h + rms_norm(sq_relu_mlp(a, mlp_w1[layer], mlp_w2[layer]), norm_gains[layer, 3])
    return h


def setup_inputs(seed=0):
    out = dict(first_inputs(seed))
    for name, value in second_inputs(seed + 1).items():
        if name != "x":
            out[name + "_2"] = value
    return out


def reference(
    x, c, w_ada, b_ada, w_in, mu_b, ln_v_g, ln_v_b, w_spatial, b_spatial, w0, w_up, a0, a_up,
    k_k, k_a, r_k, gn_g, gn_b, w_out, ln_g, ln_b, positions_2, norm_gains_2, mla_w_in_2,
    mla_q_norm_2, mla_kv_norm_2, mla_w_uq_2, mla_w_ukv_2, mla_w_o_2, hgrn_w_in_2,
    hgrn_lb_logits_2, hgrn_o_norm_2, hgrn_w_o_2, mlp_w1_2, mlp_w2_2,
):
    x = first_block(
        x, c, w_ada, b_ada, w_in, mu_b, ln_v_g, ln_v_b, w_spatial, b_spatial, w0, w_up, a0,
        a_up, k_k, k_a, r_k, gn_g, gn_b, w_out, ln_g, ln_b,
    )
    return second_block(
        x, positions_2, norm_gains_2, mla_w_in_2, mla_q_norm_2, mla_kv_norm_2, mla_w_uq_2,
        mla_w_ukv_2, mla_w_o_2, hgrn_w_in_2, hgrn_lb_logits_2, hgrn_o_norm_2, hgrn_w_o_2,
        mlp_w1_2, mlp_w2_2,
    )


_drawn_inputs = setup_inputs


def setup_inputs(seed=0):
    import zlib

    import numpy as np

    out = dict(_drawn_inputs(seed))
    spreads = {}
    factors = {'ln_v_g': 7.281,
     'ln_v_b': 28.845,
     'gn_g': 4.516,
     'gn_b': 3.895,
     'hgrn_lb_logits_2': 8.0,
     'b_spatial': 3.641}
    for name, (base, spread) in spreads.items():
        noise = np.random.default_rng([zlib.crc32(name.encode()), seed]).standard_normal(out[name].shape)
        drawn = base * np.exp(spread * noise) if base else spread * noise
        out[name] = __import__('jax').numpy.asarray(drawn.astype(out[name].dtype))
    for name, factor in factors.items():
        out[name] = (out[name] * factor).astype(out[name].dtype)
    return out
```

```python
from contextlib import ExitStack

import numpy as np
import concourse.bass as bass
from concourse import mybir

F32 = mybir.dt.float32
F32R = mybir.dt.float32r
I32 = mybir.dt.int32
ALU = mybir.AluOpType
ACT = mybir.ActivationFunctionType
AX = mybir.AxisListType.X
P = 128


def block_kernel(nc, x, c, w_ada, b_ada, w_in, mu_b, ln_v_g, ln_v_b, w_spatial, b_spatial, w0, w_up, a0, a_up,
                 k_k, k_a, r_k, gn_g, gn_b, w_out, ln_g, ln_b, positions, norm_gains, mla_w_in, mla_q_norm,
                 mla_kv_norm, mla_w_uq, mla_w_ukv, mla_w_o, hgrn_w_in, hgrn_lb, hgrn_o_norm, hgrn_w_o,
                 mlp_w1, mlp_w2, inv_freq, out):
    T, D = x.shape[1], x.shape[2]
    KT = D // P
    TT = T // P
    DA = D // 2
    JA = DA // P
    HB = 64
    NH = DA // HB
    CH = 64
    NCH = T // CH
    FF = mlp_w1.shape[2]
    NQ = FF // D
    HEADS = 8
    NOPE, ROPE = 128, 64
    QL = mla_q_norm.shape[1] // P
    KVL = mla_kv_norm.shape[1] // P
    HC = 32
    ALPHA = 2.0 ** 0.25
    KAPPA = float(np.exp(-0.5))
    SCALE = float(NOPE + ROPE) ** -0.5
    NEG = -3.0e38

    ctx = ExitStack()
    with ctx:
        base = -(-nc.sbuf_base // 32) * 32
        ctx.enter_context(nc.sbuf_tensor("arena", [P, 206 * 256], F32))
        placed = {}

        def at(name, kb, shape, dt=F32):
            placed[name] = nc.alloc_sbuf_tensor_at(name, shape, dt, offset=base + int(kb * 1024))
            return placed[name]

        def sem(name):
            return ctx.enter_context(nc.semaphore(name))

        WR = at("w_raw", 0, [P, 2, 8, P])
        WH = at("w_high", 8, [P, 2, 8, P], F32R)
        WL = at("w_low", 16, [P, 2, 8, P], F32R)
        XH = at("resid", 24, [P, KT, T])
        AH = at("act_high", 40, [P, KT, T], F32R)
        AL = at("act_low", 56, [P, KT, T], F32R)
        M = at("mix_out", 72, [P, KT, T])
        HH = at("hid_high", 88, [P, KT, T], F32R)
        HL = at("hid_low", 104, [P, KT, T], F32R)
        TMP = [at(f"tmp{n}", 120 + 2 * n, [P, T]) for n in range(6)]
        R1 = at("rstd_a", 132, [P, T])
        R2 = at("rstd_b", 134, [P, T])
        SQA = at("sum_sq", 136, [P, T])
        ONES = at("ones", 138, [P, P])
        IDENT = at("ident", 138.5, [P, P])
        BONES = at("head_ones", 139, [P, P])
        COL = at("cols", 139.5, [P, 192])
        MOD = at("mod", 140.25, [P, 24])
        SMALL = at("small", 140.375, [P, 96])
        CST = at("consts", 140.75, [P, 8])
        XTOK = at("x_tok", 72, [P, TT, D])
        ROWS = at("param_rows", 199, [P, 2, P])
        CSIL = at("c_act", 200, [P, 2 * KT])
        ADA = at("w_ada_piece", 88, [P, 2, KT, T])
        VTOK = at("v_tok", 173, [P, TT * NH, HB])
        VC = at("v_centred", 181, [P, TT * NH, HB])
        VSQ = at("v_sq", 191, [P, TT * NH, HB])
        U = at("u_act", 141, [P, JA, T])
        SG = at("gate_a", 149, [P, JA, T])
        WSP = at("w_spatial_sb", 157, [P, NH, P])
        WSPT = at("w_spatial_t", 161, [P, NH, P])
        LVG = at("ln_v_gain", 165, [P, DA])
        LVB = at("ln_v_bias", 167, [P, DA])
        BSP = at("b_spatial_sb", 169, [P, JA, P])
        WUA = at("w_up_a_up", 171, [P, DA])
        RKVG = at("rkvg", 72, [P, 4 * JA, T])
        WAD = at("wd_ad", 104, [P, T])
        PR = at("p_shift", 106, [P, 2, T + 2])
        CS = at("decay_sum", 149, [P, JA, T])
        SIG = at("decay_sig", 157, [P, JA, T])
        ICL = at("iclr_a", 173, [P, JA, T])
        KKN = at("kk_norm", 181, [P, JA, T])
        SQB = at("sq_bulk", 40, [P, JA, T])
        RSET = at("scan_reset", 189, [P, T])
        YT = at("y_rwkv", 48, [P, JA, T])
        EL = at("e_incl", 56, [P, JA, CH])
        ENL = at("e_neg", 57, [P, JA, CH])
        EX = at("e_excl", 58, [P, JA, CH])
        AR = at("ar_ops", 59, [P, JA, 2 * CH])
        BK = at("bk_ops", 61, [P, JA, 2 * CH])
        VS = at("v_ops", 63, [P, JA, 2 * CH])
        GM = at("g_masked", 65, [P, NH, 2 * CH])
        BKT = at("bk_tok", 69, [P, JA, P])
        UV = at("uv", 191, [P, NH, CH])
        ZS = at("z_sb", 193, [CH, NH, CH])
        NM = at("n_mat", 195, [CH, NH, CH])
        ND = at("n_diag", 197, [CH, NH, CH])
        NDT = at("n_diag_t", 199, [CH, NH, CH])
        X1 = at("pow_1", 201, [CH, NH, CH])
        X1T = at("pow_1t", 203, [CH, NH, CH])
        TD = at("inv_diag", 165, [CH, NH, CH])
        XC = at("inv_full", 167, [CH, NH, CH])
        TDT = at("inv_diag_t", 169, [CH, NH, CH])
        TTM = at("inv_full_t", 110.25, [CH, NH, CH])
        MSKG = at("mask_g", 112.25, [P, 2 * CH])
        MSKS = at("mask_s", 112.75, [CH, CH])
        MSKD = at("mask_d", 113, [CH, CH])
        S = at("state", 113.25, [P, JA, CH])
        FS = at("state_decay", 114.25, [P, JA])
        CQ = at("latents", 141, [P, QL + KVL, T])
        CQH = at("latents_high", 153, [P, QL + KVL, T], F32R)
        CQL = at("latents_low", 165, [P, QL + KVL, T], F32R)
        KR = at("k_rope", 177, [ROPE, T])
        QR = at("q_rope", 179, [ROPE, T])
        QN = at("q_nope", 181, [P, T])
        KN = at("k_nope", 183, [P, T])
        VM = at("v_mla", 185, [P, TT, P])
        PRB = at("probs", 187, [P, 2, T])
        PT = at("probs_t", 191, [P, 2, TT, P])
        COS = at("cos", 195, [ROPE, T])
        SIN = at("sin", 197, [ROPE, T])
        ANG = at("angle", 199, [ROPE, T])
        ANGK = at("angle_k", 201, [ROPE, T], I32)
        PIX = at("positions_sb", 141, [ROPE, T], I32)
        CMASK = at("causal_mask", 203, [P, P])
        QG = at("hg_q", 141, [P, T])
        FG = at("hg_f", 143, [P, T])
        KG = at("hg_k", 145, [P, T])
        BG = at("hg_b", 147, [P, T])
        GG = at("hg_gate", 149, [P, T])
        VG = at("hg_v", 151, [P, TT, P])
        QREL = at("hg_q_rel", 153, [P, T])
        KREL = at("hg_k_rel", 155, [P, T])
        QDEC = at("hg_q_dec", 157, [P, T])
        KDEC = at("hg_k_dec", 159, [P, T])
        EBL = at("hg_decay", 161, [P, T // HC])
        KDT = at("hg_k_dec_t", 162, [P, TT, P])
        AT = at("hg_scores", 164, [P, TT, P])
        ST = at("hg_state", 182, [P, T // HC, P])
        OG = at("hg_out", 168, [P, T])
        HMSK = at("hg_mask", 170, [P, TT, P], I32)
        HRST = at("hg_reset", 172, [P, T])
        TG = [at(f"hg_t{n}", 174 + 2 * n, [P, T]) for n in range(4)]
        LBS = at("hg_bounds", 204.5, [P, 3 * HEADS])
        LBH = at("hg_bound", 204.75, [P, 2])
        BON = at("bonus", 120, [P, JA, T])
        FC = at("inv_freq_sb", 205, [ROPE, 1])
        OTOK = at("out_tok", 88, [P, TT, D])

        PB = [ctx.enter_context(nc.psum_tensor(f"bank{n}", [P, 512], F32)) for n in range(8)]

        rows, col_of = [], {}
        for name, src, n in (("gains", norm_gains.rearrange("l a (k p) -> (l a k) p", p=P), 8 * KT),
                             ("b_ada", b_ada.rearrange("(k p) -> k p", p=P), 3 * KT),
                             ("mu", mu_b.rearrange("(k p) -> k p", p=P), 17),
                             ("lb", hgrn_lb.rearrange("l (k p) -> (l k) p", p=P), 2 * HEADS),
                             ("ln_g", ln_g.rearrange("(k p) -> k p", p=P), KT),
                             ("ln_b", ln_b.rearrange("(k p) -> k p", p=P), KT),
                             ("w0", w0.rearrange("(k p) -> k p", p=P), JA),
                             ("a0", a0.rearrange("(k p) -> k p", p=P), JA),
                             ("k_k", k_k.rearrange("(k p) -> k p", p=P), JA),
                             ("k_a", k_a.rearrange("(k p) -> k p", p=P), JA),
                             ("r_k", r_k.rearrange("(k a) d -> k (a d)", a=2), JA),
                             ("gn_g", gn_g.rearrange("(k a) d -> k (a d)", a=2), JA),
                             ("gn_b", gn_b.rearrange("(k a) d -> k (a d)", a=2), JA),
                             ("q_norm", mla_q_norm.rearrange("l (k p) -> (l k) p", p=P), QL),
                             ("kv_norm", mla_kv_norm.rearrange("l (k p) -> (l k) p", p=P), KVL),
                             ("o_norm", hgrn_o_norm, 1)):
            start = sum(r[2] for r in rows)
            if start < P < start + n:
                rows.append((None, None, P - start))
                start = P
            col_of[name] = start
            rows.append((name, src, n))
        n_rows = sum(r[2] for r in rows)

        def col(name, j=0, n=1, p0=0, p1=P):
            return COL[p0:p1, col_of[name] + j:col_of[name] + j + n]

        def gain(layer, which, k):
            return col("gains", (layer * 4 + which) * KT + k)

        A0 = 0
        B0 = A0 + 3 * JA
        O0 = B0 + 4 * JA + 1
        I0 = O0 + KT
        H0 = I0 + QL + KVL + 1
        V0 = H0 + 4 * HEADS
        F0 = V0 + KT
        G0 = F0 + 2 * KT * NQ
        W0 = G0 + 4 * HEADS
        E0 = W0 + KT
        NJ = E0 + 2 * KT * NQ
        USE = {n: k for k, n in enumerate(("in", "out", "mla", "mla_o", "mlp0", "hgrn", "hgrn_o", "mlp1"))}

        x_loaded, c_loaded, par_loaded = sem("x_loaded"), sem("c_loaded"), sem("par_loaded")
        bc_loaded = sem("bc_loaded")
        pos_loaded = sem("pos_loaded")
        ada_loaded = [sem("ada_loaded0"), sem("ada_loaded1")]
        w_loaded = [sem("w_loaded0"), sem("w_loaded1")]
        w_hi, w_lo = sem("w_hi"), sem("w_lo")
        job_done = sem("job_done")
        act_hi, act_lo = sem("act_hi"), sem("act_lo")
        const_ready, const_pool, colz = sem("const_ready"), sem("const_pool"), sem("cols_ready")
        x_turned, x_read, par_turned = sem("x_turned"), sem("x_read"), sem("par_turned")
        c_ready, ada_done, mod_ready = sem("c_ready"), sem("ada_done"), sem("mod_ready")
        gate_ready = sem("gate_ready")
        free = {n: sem("free_" + n) for n in ("a", "b", "o", "mi", "h", "mo", "f0", "g", "go", "f1")}
        v_gelu, v_ms, v_sd, v_ready = sem("v_gelu"), sem("v_ms"), sem("v_sd"), sem("v_ready")
        wsp_t, wsp_r, sp_done, u_ready, oa_ready = (sem("wsp_t"), sem("wsp_r"), sem("sp_done"), sem("u_ready"),
                                                    sem("oa_ready"))
        wsp_masked = sem("wsp_masked")
        p_copied, p_free, p_mixed = sem("p_copied"), sem("p_free"), sem("p_mixed")
        lr_tanh, lr_done, lr_sig = sem("lr_tanh"), sem("lr_done"), sem("lr_sig")
        kk_sq, kk_ss, kk_sd, rk_ready, rk_done, bulk_ready = (sem("kk_sq"), sem("kk_ss"), sem("kk_sd"),
                                                              sem("rk_ready"), sem("rk_done"), sem("bulk_ready"))
        g_silu = sem("g_silu")
        ch_exp, ch_ops, ch_g, ch_gm, ch_tok = sem("ch_exp"), sem("ch_ops"), sem("ch_g"), sem("ch_gm"), sem("ch_tok")
        iv_pe, iv_dve, iv_act = sem("iv_pe"), sem("iv_dve"), sem("iv_act")
        mv_done, z_done, z_read, u_done, u_read, s_done, s_new, y_done, y_read = (
            sem("mv_done"), sem("z_done"), sem("z_read"), sem("u_done"), sem("u_read"), sem("s_done"), sem("s_new"), sem("y_done"),
            sem("y_read"))
        gn_pe, gn_dve, gn_act, ob_ready = sem("gn_pe"), sem("gn_dve"), sem("gn_act"), sem("ob_ready")
        ln_pe, ln_dve, ln_act, x1_ready = sem("ln_pe"), sem("ln_dve"), sem("ln_act"), sem("x1_ready")
        nm_dve, nm_pe, nm_act, nm_sq = sem("nm_dve"), sem("nm_pe"), sem("nm_act"), sem("nm_sq")
        rp_ang, rp_sin = sem("rp_ang"), sem("rp_sin")
        cq_ready, kr_ready = sem("cq_ready"), sem("kr_ready")
        cq_hi, cqh_ready, cq_lo = sem("cq_normed"), sem("cq_high"), sem("cq_low")
        lb_diff, lb_exp = sem("lb_diff"), sem("lb_exp")
        h_q, h_r, h_s, h_mx, h_exp, h_pn, h_pt, h_ptr, h_o, h_or = (
            sem("h_q"), sem("h_r"), sem("h_s"), sem("h_mx"), sem("h_exp"), sem("h_pn"), sem("h_pt"), sem("h_ptr"),
            sem("h_o"), sem("h_or"))
        mx_out, resid_ready = sem("mx_out"), sem("resid_ready")
        m_relu, m_hid, m_hidlo = sem("m_relu"), sem("m_hid"), sem("m_hidlo")
        nm_dev = sem("nm_dev")
        f_up, f_dn = [sem("free_up0"), sem("free_up1")], [sem("free_dn0"), sem("free_dn1")]
        g_r1, g_r1t = sem("g_r1"), sem("g_r1t")
        g_silu3, g_f, g_ln, g_diff, g_exp, g_ops, g_sc, g_at, g_kt, g_inc, g_st, g_out, g_sq, g_ss, g_sd, g_fin = (
            sem("g_" + n) for n in ("silu3", "f", "ln", "diff", "exp", "ops", "sc", "at", "kt", "inc", "st", "out",
                                    "sq", "ss", "sd", "fin"))
        out_t, out_r, stored = sem("out_t"), sem("out_r"), sem("stored")
        block = ctx.enter_context(nc.Block())

        w_in_v = w_in.rearrange("(k p) n -> p k n", p=P)
        w_out_v = w_out.rearrange("(k p) n -> p k n", p=P)
        mla_in_v = mla_w_in[0].rearrange("(k p) n -> p k n", p=P)
        uq_v = mla_w_uq[0].rearrange("(k p) n -> p k n", p=P)
        ukv_v = mla_w_ukv[0].rearrange("(k p) n -> p k n", p=P)
        mla_o_v = mla_w_o[0].rearrange("(k p) n -> p k n", p=P)
        hg_in_v = hgrn_w_in[0].rearrange("(k p) n -> p k n", p=P)
        hg_o_v = hgrn_w_o[0].rearrange("(k p) n -> p k n", p=P)
        w1_v = [mlp_w1[l].rearrange("(k p) n -> p k n", p=P) for l in range(2)]
        w2_v = [mlp_w2[l].rearrange("(q k p) n -> p (q k) n", p=P, k=KT) for l in range(2)]
        ada_v = w_ada.rearrange("(p j) n -> p j n", j=KT)

        @block.sync
        def _(sp):
            sp.dma_start(CSIL[:, 0:KT], c.rearrange("a (p j) -> (a p) j", j=KT)).then_inc(c_loaded, 16)
            for n in range(6):
                if n >= 2:
                    sp.wait_ge(ada_done, n - 1)
                sp.dma_start(ADA[:, n % 2], ada_v[:, :, n * T:(n + 1) * T]).then_inc(ada_loaded[n % 2], 16)

            def load(c0, src, r=0, kt=8, m=P):
                if c0 >= 2:
                    sp.wait_ge(w_lo, c0 - 1 + r)
                sp.dma_start(WR[:, c0 % 2, 0:kt, 0:m], src).then_inc(w_loaded[c0 % 2], 16)

            for j in range(2):
                load(j, w_in_v[:, :, j * P:(j + 1) * P])
            with sp.Fori(1, (O0 - 1) // 2) as i:
                for s in range(2):
                    load(A0 + 2 + s, w_in_v[:, :, bass.ds(i * 2 * P + s * P, P)], (i - 1) * 2)
            load(O0 - 1, w_in_v[:, :, (O0 - 1) * P:O0 * P])
            with sp.Fori(0, KT // 2) as i:
                for s in range(2):
                    load(O0 + s, w_out_v[:, :, bass.ds(i * 2 * P + s * P, P)], i * 2)
            for j in range(QL + KVL):
                load(I0 + j, mla_in_v[:, :, j * P:(j + 1) * P])
            load(H0 - 1, mla_in_v[:, :, (QL + KVL) * P:(QL + KVL) * P + ROPE], m=ROPE)
            with sp.Fori(0, HEADS) as h:
                load(H0, uq_v[:, :, bass.ds(h * (NOPE + ROPE), NOPE)], h * 4, kt=QL)
                load(H0 + 1, uq_v[:, :, bass.ds(h * (NOPE + ROPE) + NOPE, ROPE)], h * 4, kt=QL, m=ROPE)
                load(H0 + 2, ukv_v[:, :, bass.ds(h * 2 * P, P)], h * 4, kt=KVL)
                load(H0 + 3, ukv_v[:, :, bass.ds(h * 2 * P + P, P)], h * 4, kt=KVL)
            with sp.Fori(0, KT // 2) as i:
                for s in range(2):
                    load(V0 + s, mla_o_v[:, :, bass.ds(i * 2 * P + s * P, P)], i * 2)

            def load_mlp(l, j0):
                with sp.Fori(0, NQ) as q:
                    with sp.Fori(0, KT // 2) as i:
                        for s in range(2):
                            load(j0 + s, w1_v[l][:, :, bass.ds(q * D + i * 2 * P + s * P, P)], q * 2 * KT + i * 2)
                    with sp.Fori(0, KT // 2) as i:
                        for s in range(2):
                            load(j0 + KT + s, w2_v[l][:, bass.ds(q * KT, KT), bass.ds(i * 2 * P + s * P, P)],
                                 q * 2 * KT + i * 2)

            load_mlp(0, F0)
            with sp.Fori(0, HEADS) as h:
                for j in range(4):
                    load(G0 + j, hg_in_v[:, :, bass.ds(h * P + j * D, P)], h * 4)
            with sp.Fori(0, KT // 2) as i:
                for s in range(2):
                    load(W0 + s, hg_o_v[:, :, bass.ds(i * 2 * P + s * P, P)], i * 2)
            load_mlp(1, E0)
            sp.wait_ge(out_r, TT * 2)
            sp.dma_start(out[0].rearrange("(t p) d -> p t d", p=P), OTOK[:, :, :]).then_inc(stored, 16)
            sp.wait_ge(stored, 16)

        @block.gpsimd
        def _(gp):
            gp.memset(ONES[:, :], 1.0)
            gp.memset(IDENT[:, :], 0.0)
            gp.memset(BONES[:, :], 0.0)
            gp.memset(CST[:, 0:1], 1e-5)
            gp.memset(CST[:, 1:2], 1e-12)
            gp.memset(CST[:, 2:3], 64e-5)
            gp.memset(CST[:, 3:4], 1e-6)
            gp.memset(CST[:, 4:5], float(np.pi / 2))
            gp.memset(RSET[:, :], 1.0)
            gp.drain()
            gp.affine_select(out=IDENT[:, :], in_=IDENT[:, :], compare_op=ALU.not_equal, fill=1.0, base=0,
                             pattern=[[-1, P]], channel_multiplier=1)
            gp.drain()
            gp.memset(BONES[0:HB, 0:HB], 1.0)
            gp.drain()
            gp.memset(BONES[HB:P, HB:P], 1.0)
            gp.drain()
            gp.memset(RSET[:, :].rearrange("p (c t) -> p c t", t=CH)[:, :, 0:1], 0.0)
            gp.drain()
            gp.nop().then_inc(const_ready, 1)
            at_row = 0
            gp.memset(ROWS[:, :, :], 0.0)
            gp.drain()
            n_dma = 0
            for name, src, n in rows:
                if name:
                    t, r = divmod(at_row, P)
                    gp.dma_start(ROWS[r:r + n, t, :], src).then_inc(par_loaded, 16)
                    n_dma += 1
                at_row += n
            gp.dma_start(WSP[:, :, :], w_spatial.rearrange("g t s -> t g s")).then_inc(bc_loaded, 16)
            gp.dma_start(LVG[:, :], ln_v_g.rearrange("g d -> (g d)").partition_broadcast(P)).then_inc(bc_loaded, 16)
            gp.dma_start(LVB[:, :], ln_v_b.rearrange("g d -> (g d)").partition_broadcast(P)).then_inc(bc_loaded, 16)
            for a in range(2):
                gp.dma_start(BSP[a * HB:(a + 1) * HB, :, :],
                             b_spatial.rearrange("(j a) t -> a j t", a=2)[a].partition_broadcast(HB))\
                    .then_inc(bc_loaded, 16)
            gp.dma_start(WUA[0:64, :], w_up).then_inc(bc_loaded, 16)
            gp.dma_start(WUA[64:128, :], a_up).then_inc(bc_loaded, 16)
            gp.wait_ge(bc_loaded, 16 * 7)
            gp.affine_select(out=WSP[:, :, :], in_=WSP[:, :, :], compare_op=ALU.is_ge, fill=0.0, base=0,
                             pattern=[[0, NH], [-1, P]], channel_multiplier=1).then_inc(wsp_masked, 1)

            def low(c0, r=0, kt=8, m=P):
                gp.wait_ge(w_hi, c0 + 1 + r)
                gp.tensor_tensor(WL[:, c0 % 2, 0:kt, 0:m], WR[:, c0 % 2, 0:kt, 0:m],
                                 WH[:, c0 % 2, 0:kt, 0:m].bitcast(F32), ALU.subtract).then_inc(w_lo, 1)

            with gp.Fori(0, O0 // 2) as i:
                for s in range(2):
                    low(s, i * 2)
            low(O0 - 1)
            gp.wait_ge(p_mixed, 4 * JA + 1)
            gp.memset(MSKG[:, :], 1.0)
            gp.memset(MSKS[:, :], 1.0)
            gp.memset(MSKD[:, :], 0.0)
            gp.drain()
            for half in range(2):
                rows_ = MSKG[half * CH:(half + 1) * CH, :]
                gp.affine_select(out=rows_[:, 0:CH], in_=rows_[:, 0:CH], compare_op=ALU.is_gt, fill=0.0,
                                 base=0, pattern=[[1, CH]], channel_multiplier=-1)
                gp.affine_select(out=rows_[:, CH:2 * CH], in_=rows_[:, CH:2 * CH], compare_op=ALU.is_ge,
                                 fill=0.0, base=0, pattern=[[1, CH]], channel_multiplier=-1)
                gp.drain()
            gp.affine_select(out=MSKS[:, :], in_=MSKS[:, :], compare_op=ALU.is_gt, fill=0.0, base=0,
                             pattern=[[-1, CH]], channel_multiplier=1)
            md = MSKD[:, :].rearrange("p (b t) -> p b t", t=16)
            gp.affine_select(out=md, in_=md, compare_op=ALU.is_gt, fill=1.0, base=0,
                             pattern=[[16, CH // 16], [0, 16]], channel_multiplier=-1)
            gp.drain()
            gp.affine_select(out=md, in_=md, compare_op=ALU.is_ge, fill=0.0, base=15,
                             pattern=[[16, CH // 16], [0, 16]], channel_multiplier=-1).then_inc(const_pool, 1)
            with gp.Fori(0, KT // 2) as i:
                for s in range(2):
                    low(O0 + s, i * 2)
            gp.memset(CMASK[:, :], 0.0)
            gp.drain()
            gp.affine_select(out=CMASK[:, :], in_=CMASK[:, :], compare_op=ALU.is_ge, fill=NEG, base=0,
                             pattern=[[-1, P]], channel_multiplier=1).then_inc(const_pool, 1)
            for j in range(QL + KVL):
                low(I0 + j)
            low(H0 - 1, m=ROPE)
            with gp.Fori(0, HEADS) as h:
                low(H0, h * 4, kt=QL)
                low(H0 + 1, h * 4, kt=QL, m=ROPE)
                low(H0 + 2, h * 4, kt=KVL)
                low(H0 + 3, h * 4, kt=KVL)
            with gp.Fori(0, KT // 2) as i:
                for s in range(2):
                    low(V0 + s, i * 2)
            with gp.Fori(0, NQ * KT) as i:
                for s in range(2):
                    low(F0 + s, i * 2)
            gp.memset(TG[0][:, :], 1.0)
            gp.memset(HRST[:, :], 1.0)
            gp.drain()
            gp.memset(HRST[:, :].rearrange("p (c t) -> p c t", t=HC)[:, :, 0:1], 0.0)
            hm = TG[0][:, :].rearrange("p (a b t) -> p a b t", a=TT, t=HC)
            gp.affine_select(out=hm, in_=hm, compare_op=ALU.is_ge, fill=0.0, base=0,
                             pattern=[[0, TT], [HC, P // HC], [1, HC]], channel_multiplier=-1)
            gp.drain()
            gp.affine_select(out=hm, in_=hm, compare_op=ALU.is_ge, fill=0.0, base=0,
                             pattern=[[0, TT], [-HC, P // HC], [0, HC]], channel_multiplier=1)
            gp.drain()
            gp.tensor_copy(HMSK[:, :, :].rearrange("p a t -> p (a t)"), TG[0][:, :])
            gp.memset(AT[:, :, :], 0.0)
            gp.drain()
            gp.nop().then_inc(const_pool, 1)
            with gp.Fori(0, HEADS * 2) as i:
                for s in range(2):
                    low(G0 + s, i * 2)
            with gp.Fori(0, KT // 2) as i:
                for s in range(2):
                    low(W0 + s, i * 2)
            with gp.Fori(0, NQ * KT) as i:
                for s in range(2):
                    low(E0 + s, i * 2)

        @block.tensor
        def _(pe):
            def job(c0, r, fr, n, kt=8, m=P, hi=AH, lo=AL, k0=0, token_major=False, ready=None):
                s = c0 % 2
                pe.wait_ge(w_lo, c0 + 1 + r)
                pe.wait_ge(fr, n)
                if not token_major:
                    for k in range(kt):
                        if ready is not None:
                            pe.wait_ge(ready[0], ready[1] + k + 1)
                        for w, a in ((WH, hi), (WH, lo), (WL, hi)):
                            mm = pe.matmul(PB[s][0:m, :], w[:, s, k, 0:m], a[:, k0 + k, :],
                                           start=(k == 0 and w is WH and a is hi), stop=(k == kt - 1 and w is WL))
                else:
                    for t in range(TT):
                        for k in range(kt):
                            for w, a in ((WH, hi), (WH, lo), (WL, hi)):
                                mm = pe.matmul(PB[s][:, t * P:(t + 1) * P], a[:, k0 + k, t * P:(t + 1) * P],
                                               w[:, s, k, :], start=(k == 0 and w is WH and a is hi),
                                               stop=(k == kt - 1 and w is WL))
                mm.then_inc(job_done, 1)

            def hold(*waits):
                waits = [(signal, pe.to_reg(n)) for signal, n in waits]
                pe.wait_ge(const_ready, 1)
                for signal, n in waits:
                    pe.wait_ge(signal, n)

            pe.wait_ge(const_ready, 1)
            pe.wait_ge(par_loaded, 16 * sum(1 for r in rows if r[0]))
            for t in range(2):
                mm = pe.transpose(PB[7][:, t * P:(t + 1) * P], ROWS[:, t, :], IDENT[:, :])
            mm.then_inc(par_turned, 1)
            pe.wait_ge(x_loaded, 16)
            for k in range(KT):
                if k == 7:
                    pe.wait_ge(colz, 1)
                for t in range(TT):
                    mm = pe.transpose(PB[k][:, t * P:(t + 1) * P], XTOK[:, t, k * P:(k + 1) * P], IDENT[:, :])
                mm.then_inc(x_turned, 1)
            pe.wait_ge(c_ready, 1)
            pe.wait_ge(x_read, KT)
            for n in range(3 * KT // 4):
                pe.wait_ge(ada_loaded[n % 2], 16 * (n // 2 + 1))
                for b in range(4):
                    col_ps = PB[7 if n < 4 else 6][:, 4 * n + b:4 * n + b + 1]
                    for j in range(KT):
                        mm = pe.matmul(col_ps, ADA[:, n % 2, j, b * P:(b + 1) * P], CSIL[:, KT + j:KT + j + 1],
                                       start=(j == 0), stop=(j == KT - 1))
                mm.then_inc(ada_done, 1)

            job(A0, 0, free["a"], 1, ready=(act_lo, 0))
            job(A0 + 1, 0, free["a"], 2)
            for i in range(2, JA):
                job(A0 + i, 0, free["a"], i + 1)
            for i in range(JA, 2 * JA):
                job(A0 + i, 0, free["a"], i + 1, token_major=True)
            with pe.Fori(0, JA // 2) as i:
                for s in range(2):
                    job(A0 + 2 * JA + s, i * 2, free["a"], i * 2 + s + 1 + 2 * JA)
            pe.wait_ge(wsp_masked, 1)
            for g in range(NH):
                mm = pe.transpose(PB[2 + g // 4][:, (g % 4) * P:(g % 4 + 1) * P], WSP[:, g, :], IDENT[:, :])
            mm.then_inc(wsp_t, 1)
            with pe.Fori(0, 2 * JA) as i:
                for s in range(2):
                    job(B0 + s, i * 2, free["b"], i * 2 + s + 1)
            job(O0 - 1, 0, free["b"], 4 * JA + 1)
            pe.wait_ge(wsp_r, 1)
            pe.wait_ge(v_ready, 1)
            for j in range(JA):
                for t in range(TT):
                    for a in range(2):
                        g = 2 * j + a
                        mm = pe.matmul(PB[2 + j][a * HB:(a + 1) * HB, t * P:(t + 1) * P],
                                       VC[:, t * NH + g, :], WSPT[:, g, :], start=True, stop=True)
                mm.then_inc(sp_done, 1)
            pe.wait_ge(lr_tanh, 1)
            for j in range(JA):
                mm = pe.matmul(PB[(6 + j) % 8][:, :], WUA[0:64, j * P:(j + 1) * P], WAD[0:64, :],
                               start=True, stop=True)
                mm.then_inc(lr_done, 1)
            pe.wait_ge(oa_ready, 1)
            for j in range(JA):
                mm = pe.matmul(PB[2 + j][:, :], WUA[64:128, j * P:(j + 1) * P], WAD[64:128, :],
                               start=True, stop=True)
                mm.then_inc(lr_done, 1)
            pe.wait_ge(kk_sq, 1)
            pe.wait_ge(lr_sig, 2)
            for j in range(JA):
                mm = pe.matmul(PB[(6 + j) % 8][:, :], BONES[:, :], SQB[:, j, :], start=True, stop=True)
            mm.then_inc(kk_ss, 1)
            pe.wait_ge(rk_ready, 1)
            for j in range(JA):
                mm = pe.matmul(PB[2 + j][:, :], BONES[:, :], SQB[:, j, :], start=True, stop=True)
            mm.then_inc(rk_done, 1)
            pe.wait_ge(bulk_ready, 1)

            def heads():
                return [(h, h // 2, (h % 2) * HB) for h in range(NH)]

            def hs(h, bank, p0=0, n=HB):
                return PB[bank][p0:p0 + n, h * HB:(h + 1) * HB]

            with pe.Fori(0, NCH) as ci:
                hold((ch_ops, ci + 1))
                for h, j, p in heads():
                    pe.matmul(PB[2 + h % 2][:, j * P:(j + 1) * P], BK[p:p + HB, j, :],
                              AR[p:p + HB, j, :], start=True, stop=True)
                for h, j, p in heads():
                    pe.matmul(hs(j, 4 * (1 - h % 2)), AR[p:p + HB, j, 0:CH], BK[p:p + HB, j, 0:CH], start=True,
                              stop=True)
                for j in range(JA):
                    pe.transpose(PB[5][:, j * P:(j + 1) * P], BK[:, j, :], IDENT[:, :])
                for j in range(JA):
                    mm = pe.transpose(PB[6][:, j * P:(j + 1) * P], VS[:, j, :], IDENT[:, :])
                mm.then_inc(ch_g, 1)
                hold((ch_tok, ci + 1), (iv_dve, ci * 9 + 1))
                for h in range(NH):
                    mm = pe.matmul(hs(h, 7), GM[CH:P, h, 0:CH], UV[CH:P, h, :], start=True, stop=True)
                mm.then_inc(mv_done, 1)
                hold((iv_dve, ci * 9 + 1))
                for h in range(NH):
                    pe.matmul(hs(h, 2), NDT[:, h, :], ND[:, h, :], start=True, stop=True)
                for h in range(NH):
                    mm = pe.matmul(hs(h, 3), ND[:, h, :], NDT[:, h, :], start=True, stop=True)
                mm.then_inc(iv_pe, 1)
                hold((iv_dve, ci * 9 + 2), (iv_act, ci * 5 + 1))
                for h in range(NH):
                    pe.matmul(hs(h, 4), X1T[:, h, :], TD[:, h, :], start=True, stop=True)
                for h in range(NH):
                    pe.matmul(hs(h, 2), X1T[:, h, :], X1[:, h, :], start=True, stop=True)
                for h in range(NH):
                    mm = pe.matmul(hs(h, 3), X1[:, h, :], X1T[:, h, :], start=True, stop=True)
                mm.then_inc(iv_pe, 1)
                hold((iv_dve, ci * 9 + 3), (iv_act, ci * 5 + 2))
                for h in range(NH):
                    pe.matmul(hs(h, 4), X1T[:, h, :], TD[:, h, :], start=True, stop=True)
                for h in range(NH):
                    mm = pe.matmul(hs(h, 3), X1[:, h, :], X1T[:, h, :], start=True, stop=True)
                mm.then_inc(iv_pe, 1)
                hold((iv_dve, ci * 9 + 4), (iv_act, ci * 5 + 3))
                for h in range(NH):
                    mm = pe.matmul(hs(h, 4), X1T[:, h, :], TD[:, h, :], start=True, stop=True)
                mm.then_inc(iv_pe, 1)
                hold((iv_dve, ci * 9 + 5))
                for h in range(NH):
                    mm = pe.transpose(hs(h, 2), TD[:, h, :], IDENT[0:CH, 0:CH])
                mm.then_inc(iv_pe, 1)
                hold((iv_act, ci * 5 + 4))
                for h in range(NH):
                    mm = pe.matmul(hs(h, 3), NM[:, h, :], TDT[:, h, :], start=True, stop=True)
                mm.then_inc(iv_pe, 1)
                for n in range(3):
                    if n == 0:
                        hold((iv_act, ci * 5 + 5))
                    else:
                        hold((iv_dve, ci * 9 + 5 + n))
                    for h in range(NH):
                        mm = pe.matmul(hs(h, 4), X1T[:, h, :], (TD if n == 0 else XC)[:, h, :], start=True,
                                       stop=True)
                    mm.then_inc(iv_pe, 1)
                hold((iv_dve, ci * 9 + 8))
                for h in range(NH):
                    mm = pe.transpose(hs(h, 2), XC[:, h, :], IDENT[0:CH, 0:CH])
                mm.then_inc(iv_pe, 1)
                hold((ch_tok, ci + 1), (s_new, ci + 1))
                for h, j, p in heads():
                    mm = pe.matmul(hs(j, 1 if h % 2 == 0 else 4), AR[p:p + HB, j, 0:CH], S[p:p + HB, j, :],
                                   start=True, stop=True)
                mm.then_inc(z_done, 1)
                hold((z_read, ci + 1), (iv_dve, ci * 9 + 9))
                for h in range(NH):
                    mm = pe.matmul(hs(h, 5), TTM[:, h, :], ZS[:, h, :], start=True, stop=True)
                mm.then_inc(u_done, 1)
                hold((u_read, ci + 1))
                for h, j, p in heads():
                    mm = pe.matmul(PB[6][p:p + HB, j * HB:(j + 1) * HB], BKT[:, j, p:p + HB], UV[:, h, :],
                                   start=True, stop=True)
                for h, j, p in heads():
                    pe.matmul(PB[7][p:p + HB, j * HB:(j + 1) * HB], S[p:p + HB, j, :], AR[p:p + HB, j, CH:P],
                              start=True, stop=False)
                    mm = pe.matmul(PB[7][p:p + HB, j * HB:(j + 1) * HB], UV[:, h, :], GM[:, h, CH:P],
                                   start=False, stop=True)
                mm.then_inc(y_done, 1)
            pe.wait_ge(y_read, NCH)
            for j in range(JA):
                mm = pe.matmul(PB[2 + j][:, :], BONES[:, :], YT[:, j, :], start=True, stop=True)
            mm.then_inc(gn_pe, 1)
            pe.wait_ge(gn_dve, 1)
            for j in range(JA):
                mm = pe.matmul(PB[2 + j][:, :], BONES[:, :], SQB[:, j, :], start=True, stop=True)
            mm.then_inc(gn_pe, 1)

            def eight_jobs(c0, fr, use, hi=AH, lo=AL):
                pe.wait_ge(act_lo, 8 * (USE[use] + 1))
                with pe.Fori(0, KT // 2) as i:
                    for s in range(2):
                        job(c0 + s, i * 2, fr, i * 2 + s + 1, hi=hi, lo=lo)

            eight_jobs(O0, free["o"], "out")
            pe.wait_ge(ln_dve, 1)
            mm = pe.matmul(PB[2][:, :], ONES[:, :], SQA[:, :], start=True, stop=True)
            mm.then_inc(ln_pe, 1)
            pe.wait_ge(ln_dve, 2)
            mm = pe.matmul(PB[3][:, :], ONES[:, :], SQA[:, :], start=True, stop=True)
            mm.then_inc(ln_pe, 1)

            norms = [0]

            def norm_sum():
                norms[0] += 1
                pe.wait_ge(nm_dve, norms[0])
                pe.matmul(PB[2][:, :], ONES[:, :], SQA[:, :], start=True, stop=True).then_inc(nm_pe, 1)

            norm_sum()
            pe.wait_ge(act_lo, 8 * (USE["mla"] + 1))
            for j in range(QL + KVL):
                job(I0 + j, 0, free["mi"], j + 1)
            job(H0 - 1, 0, free["mi"], QL + KVL + 1, m=ROPE)
            norm_sum()
            norm_sum()
            pe.wait_ge(cq_lo, 1)
            pe.wait_ge(kr_ready, 1)
            pe.wait_ge(const_pool, 2)
            pe.sem_inc(h_o, 1)
            with pe.Fori(0, HEADS) as h:
                job(H0, h * 4, h_q, h * 3 + 1, kt=QL, hi=CQH, lo=CQL)
                job(H0 + 1, h * 4, h_q, h * 3 + 1, kt=QL, m=ROPE, hi=CQH, lo=CQL)
                job(H0 + 2, h * 4, h_q, h * 3 + 2, kt=KVL, hi=CQH, lo=CQL, k0=QL)
                job(H0 + 3, h * 4, h_r, h + 1, kt=KVL, hi=CQH, lo=CQL, k0=QL, token_major=True)
                pe.wait_ge(h_q, h * 3 + 3)
                pe.wait_ge(h_r, h + 1)

                def scores(q):
                    n = (q + 1) * P
                    if q >= 2:
                        pe.wait_ge(h_exp, h * TT + q - 1)
                    pe.matmul(PB[2 + q % 2][:, 0:n], QN[:, q * P:n], KN[:, 0:n], start=True, stop=False)
                    pe.matmul(PB[2 + q % 2][:, 0:n], QR[:, q * P:n], KR[:, 0:n], start=False, stop=True)\
                        .then_inc(h_s, 1)

                def weigh(q):
                    pe.wait_ge(h_pn, h * TT + q + 1)
                    for b in range(q + 1):
                        mm = pe.transpose(PB[4 + q % 2][:, b * P:(b + 1) * P], PRB[:, q % 2, b * P:(b + 1) * P],
                                          IDENT[:, :])
                    mm.then_inc(h_pt, 1)

                def values(q):
                    pe.wait_ge(h_ptr, h * TT + q + 1)
                    for b in range(q + 1):
                        mm = pe.matmul(PB[6][:, q * P:(q + 1) * P], VM[:, b, :], PT[:, q % 2, b, :],
                                       start=(b == 0), stop=(b == q))
                    if q == TT - 1:
                        mm.then_inc(h_o, 1)

                scores(0)
                scores(1)
                weigh(0)
                scores(2)
                weigh(1)
                pe.wait_ge(h_q, h * 3 + 4)
                pe.wait_ge(h_or, h + 1)
                values(0)
                scores(3)
                weigh(2)
                values(1)
                weigh(3)
                values(2)
                values(3)
            eight_jobs(V0, free["mo"], "mla_o")
            norm_sum()

            def mlp(l, j0, use):
                norm_sum()
                pe.wait_ge(act_lo, 8 * (USE[use] + 1))
                with pe.Fori(0, NQ) as q:
                    hold((f_dn[l], q * KT + 2))
                    with pe.Fori(0, KT // 2) as i:
                        for s in range(2):
                            job(j0 + s, q * 2 * KT + i * 2, f_up[l], q * KT + i * 2 + s + 1)
                    hold((m_hidlo, q * KT + KT + l * NQ * KT))
                    with pe.Fori(0, KT // 2) as i:
                        for s in range(2):
                            job(j0 + KT + s, q * 2 * KT + i * 2, f_dn[l], q * KT + i * 2 + s + 1, hi=HH, lo=HL)
                norm_sum()

            mlp(0, F0, "mlp0")
            norm_sum()
            pe.wait_ge(act_lo, 8 * (USE["hgrn"] + 1))
            pe.wait_ge(const_pool, 3)
            pe.wait_ge(g_r1, 1)
            for t in range(TT):
                mm = pe.transpose(PB[3][:, t * P:(t + 1) * P], R1[:, t * P:(t + 1) * P], IDENT[:, :])
            mm.then_inc(g_r1t, 1)
            NC = T // HC
            with pe.Fori(0, HEADS) as h:
                for j in range(4):
                    job(G0 + j, h * 4, free["g"], h * 4 + j + 1, token_major=(j == 2))
                pe.wait_ge(g_ops, h + 1)
                for t in range(TT):
                    pe.matmul(PB[2][:, t * P:(t + 1) * P], KREL[:, t * P:(t + 1) * P], QREL[:, t * P:(t + 1) * P],
                              start=True, stop=True)
                for t in range(TT):
                    mm = pe.transpose(PB[3][:, t * P:(t + 1) * P], KDEC[:, t * P:(t + 1) * P], IDENT[:, :])
                mm.then_inc(g_sc, 1)
                pe.wait_ge(g_at, h + 1)
                pe.wait_ge(g_kt, h + 1)
                for n in range(NC - 1):
                    t, b = divmod(n, P // HC)
                    mm = pe.matmul(PB[2 + b][:, t * P:(t + 1) * P], KDT[b * HC:(b + 1) * HC, t, :],
                                   VG[b * HC:(b + 1) * HC, t, :], start=True, stop=True)
                mm.then_inc(g_inc, 1)
                for t in range(TT):
                    pe.matmul(PB[6][:, t * P:(t + 1) * P], VG[:, t, :], AT[:, t, :], start=True, stop=False)
                    for b in range(P // HC):
                        n = t * (P // HC) + b
                        if n:
                            pe.wait_ge(g_st, h * (NC - 1) + n)
                            mm = pe.matmul(PB[6][:, n * HC:(n + 1) * HC], ST[:, n, :],
                                           QDEC[:, n * HC:(n + 1) * HC], start=False, stop=(b == P // HC - 1))
                mm.then_inc(g_out, 1)
                pe.wait_ge(g_sq, h + 1)
                pe.matmul(PB[7][:, :], ONES[:, :], TG[0][:, :], start=True, stop=True).then_inc(g_ss, 1)
            eight_jobs(W0, free["go"], "hgrn_o", hi=HH, lo=HL)
            norm_sum()
            mlp(1, E0, "mlp1")
            pe.wait_ge(resid_ready, 4)
            for t in range(TT):
                if t:
                    pe.wait_ge(out_r, 2 * t)
                for k in range(KT):
                    mm = pe.transpose(PB[2 + k // 4][:, (k % 4) * P:(k % 4 + 1) * P], XH[:, k, t * P:(t + 1) * P],
                                      IDENT[:, :])
                mm.then_inc(out_t, 1)

        @block.scalar
        def _(act):
            act.dma_start(XTOK[:, :, :], x[0].rearrange("(t p) d -> p t d", p=P)).then_inc(x_loaded, 16)
            act.wait_ge(c_loaded, 16)
            act.activation(CSIL[:, KT:2 * KT], CSIL[:, 0:KT], ACT.Silu).then_inc(c_ready, 1)

            def high(c0, r=0, kt=8, m=P):
                act.wait_ge(w_loaded[c0 % 2], (c0 // 2 + 1) * 16 + r * 8)
                if c0 >= 2:
                    act.wait_ge(job_done, c0 - 1 + r)
                act.activation(WH[:, c0 % 2, 0:kt, 0:m], WR[:, c0 % 2, 0:kt, 0:m], ACT.Copy).then_inc(w_hi, 1)

            high(0)
            act.wait_ge(mod_ready, 1)
            for k in range(KT):
                act.activation(AH[:, k, :], XH[:, k, :], ACT.Identity, scale=MOD[:, KT + k:KT + k + 1],
                               bias=MOD[:, k:k + 1]).then_inc(act_hi, 1)
            act.sem_inc(free["a"], 2)
            for i in range(3 * JA):
                high(A0 + i + 1)
                act.wait_ge(job_done, A0 + i + 1)
                if i < JA:
                    act.activation(U[:, i, :], PB[(A0 + i) % 2][:, :], ACT.Gelu_apprx_tanh).then_inc(free["a"], 1)
                elif i < 2 * JA:
                    j = i - JA
                    act.activation(VTOK[:, :, :].rearrange("p (t g) d -> p t (g d)", t=TT)[:, :, j * P:(j + 1) * P],
                                   PB[(A0 + i) % 2][:, :].rearrange("p (t f) -> p t f", t=TT),
                                   ACT.Gelu_apprx_tanh).then_inc(free["a"], 1)
                    if j == JA - 1:
                        act.drain()
                        act.sem_inc(v_gelu, 1)
                else:
                    act.activation(SG[:, i - 2 * JA, :], PB[(A0 + i) % 2][:, :], ACT.Silu).then_inc(free["a"], 1)
            act.drain()
            act.sem_inc(u_ready, 1)
            act.wait_ge(v_ms, 1)
            act.activation(SMALL[:, 64:96], SMALL[:, 32:64], ACT.Sqrt, scale=1.0 / HB, bias=CST[:, 0:1])\
                .then_inc(v_sd, 1)
            act.sem_inc(free["b"], 2)
            with act.Fori(0, 2 * JA) as i:
                for s in range(2):
                    high(B0 + 1 + s, i * 2)
                    act.wait_ge(job_done, B0 + 1 + s + i * 2)
                    act.wait_ge(p_free, i * 2 + s + 1)
                    act.activation(PR[:, s, 1:T + 1], PB[(B0 + s) % 2][:, :], ACT.Copy).then_inc(p_copied, 1)
                    act.drain()
                    act.sem_inc(free["b"], 1)
            high(O0)
            act.wait_ge(job_done, O0)
            act.wait_ge(p_free, 4 * JA + 1)
            act.activation(PR[:, 0, 1:T + 1], PB[(O0 - 1) % 2][:, :], ACT.Copy).then_inc(p_copied, 1)
            act.wait_ge(p_mixed, 4 * JA + 1)
            act.activation(WAD[0:64, :], WAD[0:64, :], ACT.Tanh).then_inc(lr_tanh, 1)
            for j in range(JA):
                act.wait_ge(lr_done, j + 1)
                act.activation(SIG[:, j, :], PB[(6 + j) % 8][:, :], ACT.Sigmoid, bias=col("w0", j))
            act.drain()
            act.sem_inc(lr_sig, 1)
            for j in range(JA):
                act.wait_ge(lr_done, JA + j + 1)
                act.activation(ICL[:, j, :], PB[2 + j][:, :], ACT.Sigmoid, bias=col("a0", j))
            act.drain()
            act.sem_inc(lr_sig, 1)
            act.activation(RKVG[:, 3 * JA:4 * JA, :], RKVG[:, 3 * JA:4 * JA, :], ACT.Silu).then_inc(g_silu, 1)
            act.wait_ge(kk_ss, 1)
            for j in range(JA):
                act.activation(YT[:, j, :], PB[(6 + j) % 8][:, :], ACT.Sqrt, bias=CST[:, 1:2])
            act.drain()
            act.sem_inc(kk_sd, 1)
            act.wait_ge(bulk_ready, 1)
            with act.Fori(0, NCH) as ci:
                t0 = ci * CH
                act.wait_ge(s_new, ci + 1)
                act.activation(EL[:, :, :], CS[:, :, bass.ds(t0, CH)], ACT.Exp, scale=-KAPPA)
                act.activation(ENL[:, :, :], CS[:, :, bass.ds(t0, CH)], ACT.Exp, scale=KAPPA)
                act.activation(EX[:, :, :], SIG[:, :, bass.ds(t0, CH)], ACT.Exp, scale=-KAPPA)
                act.activation(VS[:, :, CH:2 * CH], RKVG[:, 2 * JA:3 * JA, bass.ds(t0, CH)], ACT.Copy)
                act.drain()
                act.sem_inc(ch_exp, 1)
                act.wait_ge(ch_g, ci + 1)
                act.activation(BKT[:, :, :].rearrange("p j s -> p (j s)"), PB[5][:, :], ACT.Copy)
                act.activation(UV[CH:P, :, :].rearrange("p h d -> p (h d)"), PB[6][CH:P, :], ACT.Copy)
                act.drain()
                act.sem_inc(ch_tok, 1)
                for n, (dst, bank, step) in enumerate(((X1T, 3, 1), (X1T, 3, 2), (X1T, 3, 3), (TDT, 2, 5),
                                                       (X1T, 3, 6))):
                    act.wait_ge(iv_pe, ci * 10 + step)
                    if n in (1, 2):
                        pass
                    act.activation(dst[:, :, :].rearrange("p h s -> p (h s)"), PB[bank][0:CH, :], ACT.Copy)\
                        .then_inc(iv_act, 1)
                act.wait_ge(y_done, ci + 1)
                act.activation(YT[:, :, bass.ds(t0, CH)], PB[7][:, 0:JA * CH].rearrange("p (j t) -> p j t", j=JA),
                               ACT.Copy).then_inc(y_read, 1)
            act.wait_ge(gn_pe, 2)
            for j in range(JA):
                act.activation(KKN[:, j, :], PB[2 + j][:, :], ACT.Sqrt, scale=1.0 / HB, bias=CST[:, 2:3])
            act.drain()
            act.sem_inc(gn_act, 1)
            act.wait_ge(ob_ready, 1)
            for k in range(KT):
                src = U[:, k, :] if k < JA else CS[:, k - JA, :]
                act.activation(AH[:, k, :], src, ACT.Copy).then_inc(act_hi, 1)

            act.wait_ge(act_lo, 8 * (USE["out"] + 1))
            act.dma_start(PIX[:, :], positions[0].partition_broadcast(ROPE)).then_inc(pos_loaded, 16)
            act.dma_start(FC[:, :], inv_freq).then_inc(pos_loaded, 16)
            with act.Fori(0, KT // 2) as i:
                for s in range(2):
                    high(O0 + 1 + s, i * 2)
            act.wait_ge(ln_pe, 1)
            act.activation(R2[:, :], PB[2][:, :], ACT.Copy, scale=1.0 / D).then_inc(ln_act, 1)
            act.wait_ge(ln_pe, 2)
            act.activation(R2[:, :], PB[3][:, :], ACT.Sqrt, scale=1.0 / D, bias=CST[:, 0:1]).then_inc(ln_act, 1)

            norms, squares = [0], [0]

            def squares_of(src, n, ready, first):
                for k in range(n):
                    squares[0] += 1
                    if ready is not None:
                        act.wait_ge(ready, first + k)
                    act.wait_ge(nm_sq, squares[0])
                    act.activation(TMP[(squares[0] - 1) % 2][:, :], src[:, k, :], ACT.Square).then_inc(nm_act, 1)

            def deviation(n, eps=3):
                norms[0] += 1
                act.wait_ge(nm_pe, norms[0])
                act.activation(R2[:, :], PB[2][:, :], ACT.Sqrt, scale=1.0 / n, bias=CST[:, eps:eps + 1])\
                    .then_inc(nm_dev, 1)

            def pre_norm(layer, which, resid):
                act.wait_ge(resid_ready, resid)
                for k in range(KT):
                    act.activation(AH[:, k, :], XH[:, k, :], ACT.Copy, scale=gain(layer, which, k))\
                        .then_inc(act_hi, 1)
                squares_of(XH, KT, None, 0)
                deviation(D)

            act.wait_ge(rp_ang, 1)
            act.wait_ge(rp_ang, 1)
            act.activation(SIN[:, :], ANG[:, :], ACT.Sin).then_inc(rp_sin, 1)
            act.wait_ge(rp_ang, 2)
            act.activation(COS[:, :], ANG[:, :], ACT.Sin).then_inc(rp_sin, 1)
            for k in range(KT):
                act.activation(AH[:, k, :], XH[:, k, :], ACT.Copy, scale=gain(0, 0, k)).then_inc(act_hi, 1)
            squares_of(XH, KT, None, 0)
            deviation(D)
            for j in range(QL + KVL):
                high(I0 + j + 1)
            high(H0, kt=QL)
            act.wait_ge(cq_ready, QL + KVL)
            squares_of(CQ, QL, None, 0)
            deviation(QL * P)
            squares_of(CQ[:, QL:QL + KVL, :], KVL, None, 0)
            deviation(KVL * P)
            for k in range(QL + KVL):
                act.wait_ge(cq_hi, QL + KVL)
                g = col("q_norm", k) if k < QL else col("kv_norm", k - QL)
                act.activation(CQH[:, k, :], CQ[:, k, :], ACT.Copy, scale=g)
            act.drain()
            act.sem_inc(cqh_ready, 1)
            act.sem_inc(h_q, 1)
            with act.Fori(0, HEADS) as h:
                high(H0 + 1, h * 4, kt=QL, m=ROPE)
                act.wait_ge(job_done, H0 + 1 + h * 4)
                act.wait_ge(h_o, h + 1)
                act.activation(QN[:, :], PB[H0 % 2][:, :], ACT.Copy).then_inc(h_q, 1)
                high(H0 + 2, h * 4, kt=KVL)
                high(H0 + 3, h * 4, kt=KVL)
                act.wait_ge(job_done, H0 + 3 + h * 4)
                act.activation(KN[:, :], PB[H0 % 2][:, :], ACT.Copy).then_inc(h_q, 1)
                high(H0 + 4, h * 4)
                act.wait_ge(job_done, H0 + 4 + h * 4)
                act.activation(VM[:, :, :].rearrange("p t d -> p (t d)"), PB[(H0 + 1) % 2][:, :], ACT.Copy)\
                    .then_inc(h_q, 1)

                def turned(q):
                    act.wait_ge(h_pt, h * TT + q + 1)
                    act.activation(PT[:, q % 2, 0:q + 1, :].rearrange("p b s -> p (b s)"),
                                   PB[4 + q % 2][:, 0:(q + 1) * P], ACT.Copy).then_inc(h_ptr, 1)

                for q in range(TT):
                    n = (q + 1) * P
                    act.wait_ge(h_mx, h * TT + q + 1)
                    if q >= 2:
                        act.wait_ge(h_pt, h * TT + q - 1)
                    act.activation(PRB[:, q % 2, 0:n], PB[2 + q % 2][:, 0:n], ACT.Exp, scale=SCALE,
                                   bias=SMALL[:, 8 + q:9 + q], accum_out=SMALL[:, 16 + q:17 + q])
                    act.drain()
                    act.sem_inc(h_exp, 1)
                    if q >= 1:
                        turned(q - 1)
                turned(TT - 1)
                act.wait_ge(h_o, h + 2)
                act.activation(AH[:, bass.ds(h, 1), :], PB[6][:, :].rearrange("p (a t) -> p a t", a=1), ACT.Copy)\
                    .then_inc(act_hi, 1)

            def mixer_out(c0, fr_count):
                for k in range(KT):
                    high(c0 + 1 + k)
                    squares[0] += 1
                    act.wait_ge(mx_out, fr_count + k + 1)
                    act.wait_ge(nm_sq, squares[0])
                    act.activation(TMP[(squares[0] - 1) % 2][:, :], M[:, k, :], ACT.Square).then_inc(nm_act, 1)
                deviation(D)

            mixer_out(V0, 0)

            def mlp(l, j0, resid):
                pre_norm(l, 2, resid)

                act.sem_inc(f_up[l], 2)

                def up(q):
                    with act.Fori(0, KT // 2) as i:
                        for s in range(2):
                            high(j0 + 1 + s, q * 2 * KT + i * 2)
                            act.wait_ge(job_done, j0 + 1 + s + q * 2 * KT + i * 2)
                            act.wait_ge(m_hid, l * NQ * KT + q * KT + i * 2 + s + 1)
                            act.activation(TMP[2 + s][:, :], PB[(j0 + s) % 2][:, :], ACT.Relu)
                            act.drain()
                            act.sem_inc(f_up[l], 1)
                            act.sem_inc(m_relu, 1)
                            act.activation(HH[:, bass.ds(i * 2 + s, 1), :],
                                           TMP[2 + s][:, :].rearrange("p (a t) -> p a t", a=1), ACT.Square)\
                                .then_inc(m_relu, 1)

                with act.Fori(0, NQ - 1) as q:
                    up(q)
                    with act.Fori(0, KT // 2) as i:
                        for s in range(2):
                            high(j0 + KT + 1 + s, q * 2 * KT + i * 2)
                up(NQ - 1)
                for k in range(KT):
                    c_next = j0 + 2 * KT * NQ - KT + k + 1
                    if c_next < NJ:
                        high(c_next)
                    squares[0] += 1
                    act.wait_ge(mx_out, KT * (1 + 2 * l) + k + 1)
                    act.wait_ge(nm_sq, squares[0])
                    act.activation(TMP[(squares[0] - 1) % 2][:, :], M[:, k, :], ACT.Square).then_inc(nm_act, 1)
                deviation(D)

            mlp(0, F0, 1)
            act.wait_ge(lb_diff, 1)
            act.activation(LBS[:, HEADS:3 * HEADS], LBS[:, HEADS:3 * HEADS], ACT.Exp).then_inc(lb_exp, 1)
            pre_norm(1, 0, 2)
            with act.Fori(0, HEADS) as h:
                high(G0 + 1, h * 4)
                act.wait_ge(free["g"], h * 4 + 3)
                act.activation(QG[:, :], TG[1][:, :], ACT.Silu).then_inc(g_silu3, 1)
                high(G0 + 2, h * 4)
                act.wait_ge(free["g"], h * 4 + 4)
                act.activation(FG[:, :], TG[2][:, :], ACT.Sigmoid).then_inc(g_silu3, 1)
                high(G0 + 3, h * 4)
                act.wait_ge(g_f, h + 1)
                act.activation(TG[2][:, :], FG[:, :], ACT.Ln).then_inc(g_ln, 1)
                high(G0 + 4, h * 4)
                act.wait_ge(free["g"], h * 4 + 6)
                act.activation(GG[:, :], TG[3][:, :], ACT.Silu).then_inc(g_silu3, 1)
                act.wait_ge(g_diff, h + 1)
                act.activation(QREL[:, :], TG[1][:, :], ACT.Exp)
                act.activation(KREL[:, :], TG[1][:, :], ACT.Exp, scale=-1.0)
                act.activation(QDEC[:, :], BG[:, :], ACT.Exp)
                act.activation(KDEC[:, :], TG[0][:, :], ACT.Exp)
                act.activation(EBL[:, :], BG[:, :].rearrange("p (c t) -> p c t", t=HC)[:, :, HC - 1], ACT.Exp)
                act.drain()
                act.sem_inc(g_exp, 1)
                act.wait_ge(g_sc, h + 1)
                act.activation(KDT[:, :, :].rearrange("p t d -> p (t d)"), PB[3][:, :], ACT.Copy).then_inc(g_kt, 1)
                act.wait_ge(g_out, h + 1)
                act.activation(OG[:, :], PB[6][:, :], ACT.Copy)
                act.activation(TG[0][:, :], PB[6][:, :], ACT.Square)
                act.drain()
                act.sem_inc(g_sq, 1)
                act.wait_ge(g_ss, h + 1)
                act.activation(TG[1][:, :], PB[7][:, :], ACT.Sqrt, scale=1.0 / P, bias=CST[:, 3:4]).then_inc(g_sd, 1)
                act.wait_ge(g_fin, h + 1)
                act.activation(HH[:, bass.ds(h, 1), :], OG[:, :].rearrange("p (a t) -> p a t", a=1), ACT.Copy)\
                    .then_inc(act_hi, 1)
            mixer_out(W0, 2 * KT)
            mlp(1, E0, 3)

        @block.vector
        def _(dve):
            def bc(ap, n):
                return ap.unsqueeze(2).broadcast_to([ap.shape[0], ap.shape[1], n])

            def bc1(ap, n):
                return ap.unsqueeze(1).broadcast_to([ap.shape[0], n, ap.shape[1]])

            def tt(out_, a, b, op):
                return dve.tensor_tensor(out_, a, b, op)

            def stt(out_, a, sc, b, op0, op1):
                return dve.scalar_tensor_tensor(out=out_, in0=a, scalar=sc, in1=b, op0=op0, op1=op1)

            def after(signal, n=1):
                dve.drain()
                dve.sem_inc(signal, n)

            MUL, ADD, SUB = ALU.mult, ALU.add, ALU.subtract
            dve.wait_ge(par_turned, 1)
            dve.tensor_copy(COL[:, 0:n_rows], PB[7][:, 0:n_rows]).then_inc(colz, 1)
            for k in range(KT):
                dve.wait_ge(x_turned, k + 1)
                dve.tensor_copy(XH[:, k, :], PB[k][:, :]).then_inc(x_read, 1)
            dve.wait_ge(ada_done, 4)
            tt(MOD[:, 0:2 * KT], PB[7][:, 0:2 * KT], col("b_ada", 0, 2 * KT), ADD)
            dve.drain()
            dve.tensor_scalar(MOD[:, KT:2 * KT], MOD[:, KT:2 * KT], 1.0, None, ADD).then_inc(mod_ready, 1)
            dve.drain()
            for k in range(KT):
                t = TMP[4 + k % 2]
                dve.tensor_scalar(t[:, :], XH[:, k, :], MOD[:, KT + k:KT + k + 1], MOD[:, k:k + 1], MUL, ADD)
                dve.drain()
                dve.wait_ge(act_hi, k + 1)
                tt(AL[:, k, :], t[:, :], AH[:, k, :].bitcast(F32), SUB).then_inc(act_lo, 1)
            dve.drain()
            dve.wait_ge(ada_done, 6)
            tt(MOD[:, 2 * KT:3 * KT], PB[6][:, 2 * KT:3 * KT], col("b_ada", 2 * KT, KT), ADD)
            dve.tensor_scalar(XH[:, :, :], XH[:, :, :], ALPHA, None, MUL)
            dve.wait_ge(v_gelu, 1)
            dve.tensor_reduce(SMALL[:, 0:32], VTOK[:, :, :], AX, ADD)
            dve.drain()
            dve.tensor_scalar(SMALL[:, 0:32], SMALL[:, 0:32], 1.0 / HB, None, MUL)
            dve.drain()
            tt(VC[:, :, :], VTOK[:, :, :], bc(SMALL[:, 0:32], HB), SUB)
            dve.drain()
            tt(VSQ[:, :, :], VC[:, :, :], VC[:, :, :], MUL)
            dve.drain()
            dve.tensor_reduce(SMALL[:, 32:64], VSQ[:, :, :], AX, ADD).then_inc(v_ms, 1)
            dve.wait_ge(v_sd, 1)
            dve.reciprocal(SMALL[:, 64:96], SMALL[:, 64:96])
            dve.drain()
            tt(VC[:, :, :], VC[:, :, :], bc(SMALL[:, 64:96], HB), MUL)
            dve.drain()
            dve.wait_ge(bc_loaded, 16 * 7)
            vt = VC[:, :, :].rearrange("p (t g) d -> p t (g d)", t=TT)
            tt(vt, vt, bc1(LVG[:, :], TT), MUL)
            dve.drain()
            tt(vt, vt, bc1(LVB[:, :], TT), ADD).then_inc(v_ready, 1)
            dve.wait_ge(wsp_t, 1)
            for a in range(2):
                dve.tensor_copy(WSPT[:, 4 * a:4 * a + 4, :].rearrange("p g t -> p (g t)"), PB[2 + a][:, :])
            after(wsp_r)
            dve.wait_ge(x_read, KT)
            dve.memset(PR[:, :, 0:1], 0.0)
            after(p_free, 2)

            def mix(s, dst, mu):
                tt(TMP[4 + s][:, :], PR[:, s, 0:T], PR[:, s, 1:T + 1], SUB)
                dve.drain()
                stt(dst, TMP[4 + s][:, :], mu, PR[:, s, 1:T + 1], MUL, ADD)
                dve.drain()
                dve.sem_inc(p_free, 1)
                dve.sem_inc(p_mixed, 1)

            for i in range(4 * JA):
                dve.wait_ge(p_copied, i + 1)
                mix(i % 2, RKVG[:, i, :], col("mu", i))
            dve.wait_ge(p_copied, 4 * JA + 1)
            mix(0, WAD[:, :], col("mu", 4 * JA))
            dve.wait_ge(u_ready, 1)
            for j in range(JA):
                dve.wait_ge(sp_done, j + 1)
                t = TMP[4 + j % 2]
                tt(t[:, :].rearrange("p (c t) -> p c t", c=TT), PB[2 + j][:, :].rearrange("p (c t) -> p c t", c=TT),
                   bc1(BSP[:, j, :], TT), ADD)
                tt(U[:, j, :], U[:, j, :], SG[:, j, :], MUL)
                dve.drain()
                tt(U[:, j, :], U[:, j, :], t[:, :], MUL)
                dve.drain()
            dve.sem_inc(oa_ready, 1)
            R_, K_, V_, G_ = (RKVG[:, n * JA:(n + 1) * JA, :] for n in range(4))
            for j in range(JA):
                dve.tensor_scalar(KKN[:, j, :], K_[:, j, :], col("k_k", j), None, MUL)
            dve.drain()
            tt(SQB[:, :, :], KKN[:, :, :], KKN[:, :, :], MUL).then_inc(kk_sq, 1)
            dve.wait_ge(lr_sig, 1)
            for j in range(JA):
                dve.tensor_tensor_scan(CS[:, j, :], RSET[:, :], SIG[:, j, :], 0.0, MUL, ADD)
            dve.drain()
            tt(SIG[:, :, :], CS[:, :, :], SIG[:, :, :], SUB)
            dve.wait_ge(lr_sig, 2)
            for j in range(JA):
                t = TMP[4 + j % 2]
                dve.tensor_scalar(t[:, :], ICL[:, j, :], 1.0, col("k_a", j), SUB, MUL)
                dve.drain()
                stt(K_[:, j, :], t[:, :], 1.0, K_[:, j, :], ADD, MUL)
            dve.drain()
            dve.wait_ge(kk_sd, 1)
            dve.reciprocal(YT[:, :, :], YT[:, :, :])
            for j in range(JA):
                stt(SQB[:, j, :], R_[:, j, :], col("r_k", j), K_[:, j, :], MUL, MUL)
            after(rk_ready)
            tt(KKN[:, :, :], KKN[:, :, :], YT[:, :, :], MUL)
            dve.drain()
            tt(ICL[:, :, :], KKN[:, :, :], ICL[:, :, :], MUL)
            dve.wait_ge(rk_done, 1)
            for j in range(JA):
                tt(BON[:, j, :], PB[2 + j][:, :], V_[:, j, :], MUL)
            dve.memset(S[:, :, :], 0.0)
            dve.memset(VS[:, :, 0:CH], 0.0)
            dve.wait_ge(g_silu, 1)
            dve.wait_ge(const_pool, 1)
            dve.drain()
            dve.sem_inc(bulk_ready, 1)
            dve.sem_inc(s_new, 1)
            fl = "p h s -> p (h s)"
            with dve.Fori(0, NCH) as ci:
                t0 = bass.ds(ci * CH, CH)
                dve.wait_ge(ch_exp, ci + 1)
                stt(AR[:, :, 0:CH], KKN[:, :, t0], -1.0, EX[:, :, :], MUL, MUL)
                tt(AR[:, :, CH:P], R_[:, :, t0], EL[:, :, :], MUL)
                tt(BK[:, :, 0:CH], ICL[:, :, t0], ENL[:, :, :], MUL)
                tt(BK[:, :, CH:P], K_[:, :, t0], ENL[:, :, :], MUL)
                dve.tensor_copy(FS[:, :], EL[:, :, CH - 1])
                after(ch_ops)
                dve.wait_ge(ch_g, ci + 1)
                for a in range(2):
                    tt(GM[:, a::2, :], PB[2 + a][:, :].rearrange("p (h s) -> p h s", s=P),
                       bc1(MSKG[:, :], JA), MUL)
                for a in range(2):
                    tt(NM[:, a::2, :], PB[4 * (1 - a)][0:CH, 0:JA * CH].rearrange("p (h s) -> p h s", s=CH),
                       bc1(MSKS[:, :], JA), MUL)
                dve.drain()
                tt(ND[:, :, :], NM[:, :, :], bc1(MSKD[:, :], NH), MUL)
                tt(NDT[:, :, :], GM[0:CH, :, 0:CH], bc1(MSKD[:, :], NH), MUL)
                dve.drain()
                tt(NM[:, :, :], NM[:, :, :], ND[:, :, :], SUB)
                tt(TD[:, :, :], ND[:, :, :], bc1(IDENT[0:CH, 0:CH], NH), ADD)
                after(iv_dve)
                dve.wait_ge(mv_done, ci + 1)
                dve.tensor_copy(ZS[:, :, :].rearrange(fl), PB[7][0:CH, :])
                dve.wait_ge(iv_pe, ci * 10 + 1)
                dve.tensor_copy(X1[:, :, :].rearrange(fl), PB[2][0:CH, :])
                after(iv_dve)
                dve.wait_ge(iv_pe, ci * 10 + 2)
                tt(TD[:, :, :].rearrange(fl), PB[4][0:CH, :], TD[:, :, :].rearrange(fl), ADD)
                dve.tensor_copy(X1[:, :, :].rearrange(fl), PB[2][0:CH, :])
                after(iv_dve)
                for n in (3, 4):
                    dve.wait_ge(iv_pe, ci * 10 + n)
                    tt(TD[:, :, :].rearrange(fl), PB[4][0:CH, :], TD[:, :, :].rearrange(fl), ADD)
                    after(iv_dve)
                for n in (7, 8, 9):
                    dve.wait_ge(iv_pe, ci * 10 + n)
                    tt(XC[:, :, :].rearrange(fl), PB[4][0:CH, :], TD[:, :, :].rearrange(fl), ADD)
                    after(iv_dve)
                dve.wait_ge(iv_pe, ci * 10 + 10)
                dve.tensor_copy(TTM[:, :, :].rearrange(fl), PB[2][0:CH, :])
                after(iv_dve)
                dve.wait_ge(z_done, ci + 1)
                for a in range(2):
                    tt(ZS[:, a::2, :], PB[(1, 4)[a]][0:CH, 0:JA * CH].rearrange("p (h s) -> p h s", s=CH),
                       ZS[:, a::2, :], ADD)
                after(z_read)
                dve.wait_ge(u_done, ci + 1)
                dve.tensor_copy(UV[0:CH, :, :].rearrange(fl), PB[5][0:CH, :]).then_inc(u_read, 1)
                dve.wait_ge(y_done, ci + 1)
                sv = S[:, :, :].rearrange("p j i -> p (j i)")
                tt(sv, PB[6][:, 0:JA * CH], sv, ADD)
                dve.drain()
                tt(S[:, :, :], S[:, :, :], bc(FS[:, :], CH), MUL)
                after(s_new)
            dve.wait_ge(gn_pe, 1)
            for j in range(JA):
                stt(YT[:, j, :], PB[2 + j][:, :], -1.0 / HB, YT[:, j, :], MUL, ADD)
            dve.drain()
            tt(SQB[:, :, :], YT[:, :, :], YT[:, :, :], MUL)
            after(gn_dve)
            dve.wait_ge(gn_act, 1)
            dve.reciprocal(KKN[:, :, :], KKN[:, :, :])
            dve.drain()
            tt(YT[:, :, :], YT[:, :, :], KKN[:, :, :], MUL)
            dve.drain()
            for j in range(JA):
                dve.tensor_scalar(YT[:, j, :], YT[:, j, :], col("gn_g", j), col("gn_b", j), MUL, ADD)
            dve.drain()
            tt(YT[:, :, :], YT[:, :, :], BON[:, :, :], ADD)
            dve.drain()
            tt(CS[:, :, :], YT[:, :, :], G_, MUL)
            after(ob_ready)
            for k in range(KT):
                src = U[:, k, :] if k < JA else CS[:, k - JA, :]
                dve.wait_ge(act_hi, 8 * USE["out"] + k + 1)
                tt(AL[:, k, :], src, AH[:, k, :].bitcast(F32), SUB).then_inc(act_lo, 1)
            dve.sem_inc(free["o"], 2)
            for k in range(KT):
                dve.wait_ge(job_done, O0 + k + 1)
                stt(M[:, k, :], PB[(O0 + k) % 2][:, :], MOD[:, 2 * KT + k:2 * KT + k + 1], XH[:, k, :], MUL, ADD)\
                    .then_inc(free["o"], 1)
                dve.drain()
                if k == 0:
                    dve.tensor_copy(SQA[:, :], M[:, k, :])
                else:
                    tt(SQA[:, :], SQA[:, :], M[:, k, :], ADD)
            after(ln_dve)
            dve.wait_ge(ln_act, 1)
            for k in range(KT):
                tt(M[:, k, :], M[:, k, :], R2[:, :], SUB)
                dve.drain()
                if k == 0:
                    tt(SQA[:, :], M[:, k, :], M[:, k, :], MUL)
                else:
                    tt(TMP[4][:, :], M[:, k, :], M[:, k, :], MUL)
                    dve.drain()
                    tt(SQA[:, :], SQA[:, :], TMP[4][:, :], ADD)
            after(ln_dve)
            dve.wait_ge(ln_act, 2)
            dve.reciprocal(R1[:, :], R2[:, :])
            dve.drain()
            for k in range(KT):
                tt(M[:, k, :], M[:, k, :], R1[:, :], MUL)
            dve.drain()
            for k in range(KT):
                dve.tensor_scalar(XH[:, k, :], M[:, k, :], col("ln_g", k), col("ln_b", k), MUL, ADD)
            after(x1_ready)

            squares, devs, his = [0], [0], [8 * USE["mla"]]

            def add_squares(n):
                for k in range(n):
                    squares[0] += 1
                    dve.wait_ge(nm_act, squares[0])
                    t = TMP[(squares[0] - 1) % 2]
                    if k == 0:
                        dve.tensor_copy(SQA[:, :], t[:, :]).then_inc(nm_sq, 1)
                    else:
                        tt(SQA[:, :], SQA[:, :], t[:, :], ADD).then_inc(nm_sq, 1)
                    dve.drain()
                dve.sem_inc(nm_dve, 1)

            def inverse(dst):
                devs[0] += 1
                dve.wait_ge(nm_dev, devs[0])
                dve.reciprocal(dst[:, :], R2[:, :])
                dve.drain()

            def low_of_gained(layer, which):
                for k in range(KT):
                    his[0] += 1
                    dve.wait_ge(act_hi, his[0])
                    stt(AL[:, k, :], XH[:, k, :], gain(layer, which, k), AH[:, k, :].bitcast(F32), MUL, SUB)\
                        .then_inc(act_lo, 1)

            def add_to_residual(layer, which):
                inverse(R2)
                for k in range(KT):
                    tt(M[:, k, :], M[:, k, :], R2[:, :], MUL)
                dve.drain()
                for k in range(KT):
                    stt(XH[:, k, :], M[:, k, :], gain(layer, which, k), XH[:, k, :], MUL, ADD)
                after(resid_ready)

            dve.wait_ge(pos_loaded, 32)
            dve.tensor_copy(ANG[:, :], PIX[:, :])
            dve.drain()
            dve.tensor_scalar(ANG[:, :], ANG[:, :], FC[:, 0:1], None, MUL)
            dve.drain()
            dve.tensor_scalar(ANGK[:, :], ANG[:, :], float(1 / (2 * np.pi)), None, MUL)
            dve.drain()
            dve.tensor_copy(SIN[:, :], ANGK[:, :])
            dve.drain()
            hi1 = 6.28125
            hi2 = float(np.float32(2 * np.pi - hi1))
            hi2 = float(np.frombuffer((np.frombuffer(np.float32(hi2).tobytes(), np.uint32) & np.uint32(0xFFFFF000))
                                      .tobytes(), np.float32)[0])
            for part in (hi1, hi2, float(2 * np.pi - hi1 - hi2)):
                stt(ANG[:, :], SIN[:, :], -part, ANG[:, :], MUL, ADD)
                dve.drain()
            dve.tensor_scalar(ANG[:, :], ANG[:, :], -3.1415925, 3.1415925, ALU.max, ALU.min)
            after(rp_ang)
            dve.wait_ge(rp_sin, 1)
            dve.tensor_scalar(ANG[:, :], ANG[:, :], float(np.pi / 2), None, ADD)
            dve.drain()
            dve.tensor_scalar(COS[:, :], ANG[:, :], float(np.pi), float(-2 * np.pi), ALU.is_gt, MUL)
            dve.drain()
            tt(ANG[:, :], ANG[:, :], COS[:, :], ADD)
            dve.drain()
            dve.tensor_scalar(ANG[:, :], ANG[:, :], -3.1415925, 3.1415925, ALU.max, ALU.min)
            after(rp_ang)
            dve.tensor_scalar(SIN[ROPE // 2:ROPE, :], SIN[ROPE // 2:ROPE, :], -1.0, None, MUL)
            dve.wait_ge(rp_sin, 2)

            def rope(dst, src, a, b):
                hf = ROPE // 2
                tt(a[0:ROPE, :], src, COS[:, :], MUL)
                tt(b[0:hf, :], src[hf:ROPE, :], SIN[hf:ROPE, :], MUL)
                tt(b[hf:ROPE, :], src[0:hf, :], SIN[0:hf, :], MUL)
                dve.drain()
                return tt(dst, a[0:ROPE, :], b[0:ROPE, :], ADD)

            dve.sem_inc(nm_sq, 2)
            low_of_gained(0, 0)
            add_squares(KT)
            inverse(R1)
            dve.sem_inc(free["mi"], 2)
            for k in range(QL + KVL):
                dve.wait_ge(job_done, I0 + k + 1)
                tt(CQ[:, k, :], PB[(I0 + k) % 2][:, :], R1[:, :], MUL)
                dve.drain()
                dve.sem_inc(free["mi"], 1)
                dve.sem_inc(cq_ready, 1)
            dve.wait_ge(job_done, H0)
            tt(TMP[2][0:ROPE, :], PB[(H0 - 1) % 2][0:ROPE, :], R1[0:ROPE, :], MUL)
            dve.drain()
            rope(KR[:, :], TMP[2][0:ROPE, :], TMP[4], TMP[5])
            after(kr_ready)
            add_squares(QL)
            inverse(R1)
            add_squares(KVL)
            for k in range(QL):
                tt(CQ[:, k, :], CQ[:, k, :], R1[:, :], MUL)
            dve.drain()
            inverse(R1)
            for k in range(KVL):
                tt(CQ[:, QL + k, :], CQ[:, QL + k, :], R1[:, :], MUL)
            after(cq_hi, QL + KVL)
            dve.wait_ge(cqh_ready, 1)
            for k in range(QL + KVL):
                g = col("q_norm", k) if k < QL else col("kv_norm", k - QL)
                stt(CQL[:, k, :], CQ[:, k, :], g, CQH[:, k, :].bitcast(F32), MUL, SUB)
            after(cq_lo)
            dve.sem_inc(h_or, 1)
            dve.wait_ge(const_pool, 2)
            with dve.Fori(0, HEADS) as h:
                dve.wait_ge(job_done, h * 4 + H0 + 2)
                rope(QR[:, :], PB[(H0 + 1) % 2][0:ROPE, :], TMP[4], TMP[5])
                after(h_r)

                def row_max(q):
                    n = (q + 1) * P
                    ps = PB[2 + q % 2]
                    dve.wait_ge(h_s, h * TT + q + 1)
                    tt(ps[:, q * P:n], ps[:, q * P:n], CMASK[:, :], ADD)
                    dve.drain()
                    dve.tensor_reduce(SMALL[:, q:q + 1], ps[:, 0:n], AX, ALU.max)
                    dve.drain()
                    dve.tensor_scalar(SMALL[:, 8 + q:9 + q], SMALL[:, q:q + 1], -SCALE, None, MUL).then_inc(h_mx, 1)

                def normalise(q):
                    n = (q + 1) * P
                    dve.wait_ge(h_exp, h * TT + q + 1)
                    dve.reciprocal(SMALL[:, 24 + q:25 + q], SMALL[:, 16 + q:17 + q])
                    dve.drain()
                    dve.tensor_scalar(PRB[:, q % 2, 0:n], PRB[:, q % 2, 0:n], SMALL[:, 24 + q:25 + q], None, MUL)\
                        .then_inc(h_pn, 1)

                for q in range(TT):
                    row_max(q)
                    if q:
                        normalise(q - 1)
                normalise(TT - 1)
                dve.wait_ge(act_hi, h + 8 * USE["mla_o"] + 1)
                tt(AL[:, bass.ds(h, 1), :], PB[6][:, :].rearrange("p (a t) -> p a t", a=1),
                   AH[:, bass.ds(h, 1), :].bitcast(F32), SUB)
                dve.drain()
                dve.sem_inc(act_lo, 1)
                dve.sem_inc(h_or, 1)
            his[0] += 8

            def read_mixer(c0, fr):
                dve.sem_inc(fr, 2)
                for k in range(KT):
                    dve.wait_ge(job_done, c0 + k + 1)
                    dve.tensor_copy(M[:, k, :], PB[(c0 + k) % 2][:, :])
                    dve.drain()
                    dve.sem_inc(fr, 1)
                    dve.sem_inc(mx_out, 1)
                    if k:
                        one_square(k - 1)
                one_square(KT - 1)
                dve.sem_inc(nm_dve, 1)

            def one_square(k):
                squares[0] += 1
                dve.wait_ge(nm_act, squares[0])
                t = TMP[(squares[0] - 1) % 2]
                if k == 0:
                    dve.tensor_copy(SQA[:, :], t[:, :]).then_inc(nm_sq, 1)
                else:
                    tt(SQA[:, :], SQA[:, :], t[:, :], ADD).then_inc(nm_sq, 1)
                dve.drain()

            read_mixer(V0, free["mo"])
            add_to_residual(0, 1)

            def mlp(l, j0):
                if l == 0:
                    dve.sem_inc(m_hid, 2)
                dve.sem_inc(f_dn[l], 2)
                low_of_gained(l, 2)
                add_squares(KT)
                inverse(R1)
                tt(R1[:, :], R1[:, :], R1[:, :], MUL)
                dve.drain()

                def up(q):
                    with dve.Fori(0, KT // 2) as i:
                        for s in range(2):
                            n = l * NQ * KT + q * KT + i * 2 + s
                            dve.wait_ge(m_relu, n * 2 + 1)
                            tt(TMP[4 + s][:, :], TMP[2 + s][:, :], TMP[2 + s][:, :], MUL)
                            after(m_hid)
                            dve.wait_ge(m_relu, n * 2 + 2)
                            tt(HL[:, bass.ds(i * 2 + s, 1), :], TMP[4 + s][:, :].rearrange("p (a t) -> p a t", a=1),
                               HH[:, bass.ds(i * 2 + s, 1), :].bitcast(F32), SUB).then_inc(m_hidlo, 1)

                def down(q, first):
                    with dve.Fori(0, KT // 2) as i:
                        for s in range(2):
                            dve.wait_ge(job_done, q * 2 * KT + i * 2 + j0 + KT + s + 1)
                            m = M[:, bass.ds(i * 2 + s, 1), :]
                            ps = PB[(j0 + s) % 2][:, :].rearrange("p (a t) -> p a t", a=1)
                            if first:
                                dve.tensor_copy(m, ps).then_inc(f_dn[l], 1)
                            else:
                                tt(m, ps, m, ADD).then_inc(f_dn[l], 1)
                            dve.drain()

                up(0)
                down(0, True)
                with dve.Fori(1, NQ - 1) as q:
                    up(q)
                    down(q, False)
                up(NQ - 1)
                for k in range(KT):
                    dve.wait_ge(job_done, j0 + 2 * KT * NQ - KT + k + 1)
                    tt(M[:, k, :], PB[(j0 + k) % 2][:, :], M[:, k, :], ADD).then_inc(f_dn[l], 1)
                    dve.drain()
                    tt(M[:, k, :], M[:, k, :], R1[:, :], MUL)
                    after(mx_out)
                    if k:
                        one_square(k - 1)
                one_square(KT - 1)
                dve.sem_inc(nm_dve, 1)
                add_to_residual(l, 3)

            mlp(0, F0)
            n = HEADS
            l0, l1 = col("lb", 0, n), col("lb", n, n)
            tt(LBS[:, 0:n], l0, l1, ALU.max)
            dve.drain()
            tt(LBS[:, n:2 * n], l0, LBS[:, 0:n], SUB)
            tt(LBS[:, 2 * n:3 * n], l1, LBS[:, 0:n], SUB)
            after(lb_diff)
            low_of_gained(1, 0)
            add_squares(KT)
            inverse(R1)
            dve.sem_inc(g_r1, 1)
            dve.wait_ge(lb_exp, 1)
            tt(LBS[:, 0:n], LBS[:, n:2 * n], LBS[:, 2 * n:3 * n], ADD)
            dve.drain()
            dve.reciprocal(LBS[:, 0:n], LBS[:, 0:n])
            dve.drain()
            tt(LBS[:, n:2 * n], LBS[:, n:2 * n], LBS[:, 0:n], MUL)
            tt(LBS[:, 2 * n:3 * n], LBS[:, 2 * n:3 * n], LBS[:, 0:n], MUL)
            dve.drain()
            tt(LBS[:, 2 * n:3 * n], LBS[:, n:2 * n], LBS[:, 2 * n:3 * n], ADD)
            dve.drain()
            tt(LBS[:, 0:n], LBS[:, 2 * n:3 * n], LBS[:, n:2 * n], SUB)
            dve.drain()
            dve.tensor_scalar(LBS[:, n:2 * n], LBS[:, 0:n], -1.0, 1.0, MUL, ADD)
            dve.wait_ge(g_r1t, 1)
            dve.tensor_copy(SMALL[:, 32:32 + TT], PB[3][:, :].rearrange("p (t f) -> p t f", t=TT)[:, :, 0])
            dve.drain()
            dve.wait_ge(const_pool, 3)
            dve.sem_inc(free["g"], 2)
            with dve.Fori(0, HEADS) as h:
                for j in range(4):
                    dve.wait_ge(job_done, h * 4 + G0 + j + 1)
                    ps = PB[(G0 + j) % 2]
                    if j == 2:
                        tt(VG[:, :, :], ps[:, :].rearrange("p (t f) -> p t f", t=TT), bc(SMALL[:, 32:32 + TT], P),
                           MUL).then_inc(free["g"], 1)
                    else:
                        tt(TG[(1, 2, 0, 3)[j]][:, :], ps[:, :], R1[:, :], MUL).then_inc(free["g"], 1)
                    if j == 1:
                        dve.tensor_copy(LBH[:, 0:1], LBS[:, bass.ds(h, 1)])
                        dve.tensor_copy(LBH[:, 1:2], LBS[:, bass.ds(h + n, 1)])
                        dve.drain()
                        dve.wait_ge(g_silu3, h * 3 + 2)
                        dve.tensor_scalar(FG[:, :], FG[:, :], LBH[:, 1:2], LBH[:, 0:1], MUL, ADD)
                        after(g_f)
                        dve.tensor_scalar(KG[:, :], FG[:, :], -1.0, 1.0, MUL, ADD)
                dve.wait_ge(g_ln, h + 1)
                dve.tensor_tensor_scan(BG[:, :], HRST[:, :], TG[2][:, :], 0.0, MUL, ADD)
                dve.drain()
                b3 = BG[:, :].rearrange("p (c t) -> p c t", t=HC)
                tt(TG[1][:, :].rearrange("p (c t) -> p c t", t=HC), b3, bc(b3[:, :, HC // 2], HC), SUB)
                tt(TG[0][:, :].rearrange("p (c t) -> p c t", t=HC), bc(b3[:, :, HC - 1], HC), b3, SUB)
                after(g_diff)
                dve.wait_ge(g_exp, h + 1)
                for a, b in ((QREL, QG), (KREL, KG), (QDEC, QG), (KDEC, KG)):
                    tt(a[:, :], a[:, :], b[:, :], MUL)
                after(g_ops)
                dve.wait_ge(const_pool, 3)
                dve.wait_ge(g_sc, h + 1)
                dve.copy_predicated(AT[:, :, :].rearrange("p t s -> p (t s)"),
                                    HMSK[:, :, :].rearrange("p t s -> p (t s)"), PB[2][:, :]).then_inc(g_at, 1)
                dve.wait_ge(g_inc, h + 1)
                for k in range(T // HC - 1):
                    ps = PB[2 + k % (P // HC)][:, k // (P // HC) * P:(k // (P // HC) + 1) * P]
                    if k == 0:
                        dve.tensor_copy(ST[:, 1, :], ps).then_inc(g_st, 1)
                    else:
                        stt(ST[:, k + 1, :], ST[:, k, :], EBL[:, k:k + 1], ps, MUL, ADD).then_inc(g_st, 1)
                    dve.drain()
                dve.wait_ge(g_sd, h + 1)
                dve.reciprocal(TG[1][:, :], TG[1][:, :])
                dve.drain()
                stt(OG[:, :], OG[:, :], col("o_norm"), TG[1][:, :], MUL, MUL)
                dve.drain()
                dve.wait_ge(g_silu3, h * 3 + 3)
                tt(OG[:, :], OG[:, :], GG[:, :], MUL)
                after(g_fin)
                dve.wait_ge(act_hi, h + 8 * USE["hgrn_o"] + 1)
                tt(HL[:, bass.ds(h, 1), :], OG[:, :].rearrange("p (a t) -> p a t", a=1),
                   HH[:, bass.ds(h, 1), :].bitcast(F32), SUB).then_inc(act_lo, 1)
            his[0] += 8
            dve.drain()
            read_mixer(W0, free["go"])
            add_to_residual(1, 1)
            mlp(1, E0)
            for t in range(TT):
                dve.wait_ge(out_t, t + 1)
                for a in range(2):
                    dve.tensor_copy(OTOK[:, t, a * T:(a + 1) * T], PB[2 + a][:, :]).then_inc(out_r, 1)
    return nc


INS = ['x', 'c', 'w_ada', 'b_ada', 'w_in', 'mu_b', 'ln_v_g', 'ln_v_b', 'w_spatial', 'b_spatial', 'w0', 'w_up', 'a0',
       'a_up', 'k_k', 'k_a', 'r_k', 'gn_g', 'gn_b', 'w_out', 'ln_g', 'ln_b', 'positions_2', 'norm_gains_2',
       'mla_w_in_2', 'mla_q_norm_2', 'mla_kv_norm_2', 'mla_w_uq_2', 'mla_w_ukv_2', 'mla_w_o_2', 'hgrn_w_in_2',
       'hgrn_lb_logits_2', 'hgrn_o_norm_2', 'hgrn_w_o_2', 'mlp_w1_2', 'mlp_w2_2']


def kernel(**inputs):
    import concourse.bacc as bacc
    from concourse.bass_utils import run_bass_kernel_spmd

    nc = bacc.Bacc("TRN2", target_bir_lowering=False, num_devices=1)
    arrays = {f"in_{name}": np.ascontiguousarray(inputs[name]) for name in INS}
    half = 32
    freq = (10000.0 ** (-np.arange(half, dtype=np.float64) / half)).astype(np.float32)
    arrays["inv_freq"] = np.concatenate([freq, freq]).reshape(2 * half, 1)
    aps = [nc.dram_tensor(name, a.shape, mybir.dt.from_np(a.dtype), kind="ExternalInput").ap()
           for name, a in arrays.items()]
    out = nc.dram_tensor("out", inputs["x"].shape, F32, kind="ExternalOutput").ap()
    block_kernel(nc, *aps, out)
    r = run_bass_kernel_spmd(nc, [arrays], core_ids=[0])
    return r.results[0]["out"]
```

```python
from contextlib import ExitStack

import numpy as np
import concourse.bass as bass
from concourse import mybir

F32 = mybir.dt.float32
F32R = mybir.dt.float32r
I32 = mybir.dt.int32
ALU = mybir.AluOpType
ACT = mybir.ActivationFunctionType
AX = mybir.AxisListType.X
P = 128


def block_kernel(nc, x, c, w_ada, b_ada, w_in, mu_b, ln_v_g, ln_v_b, w_spatial, b_spatial, w0, w_up, a0, a_up,
                 k_k, k_a, r_k, gn_g, gn_b, w_out, ln_g, ln_b, positions, norm_gains, mla_w_in, mla_q_norm,
                 mla_kv_norm, mla_w_uq, mla_w_ukv, mla_w_o, hgrn_w_in, hgrn_lb, hgrn_o_norm, hgrn_w_o,
                 mlp_w1, mlp_w2, inv_freq, out):
    T, D = x.shape[1], x.shape[2]
    KT = D // P
    TT = T // P
    DA = D // 2
    JA = DA // P
    HB = 64
    NH = DA // HB
    CH = 64
    NCH = T // CH
    FF = mlp_w1.shape[2]
    NQ = FF // D
    HEADS = 8
    NOPE, ROPE = 128, 64
    QL = mla_q_norm.shape[1] // P
    KVL = mla_kv_norm.shape[1] // P
    HC = 32
    ALPHA = 2.0 ** 0.25
    KAPPA = float(np.exp(-0.5))
    SCALE = float(NOPE + ROPE) ** -0.5
    NEG = -3.0e38

    ctx = ExitStack()
    with ctx:
        base = -(-nc.sbuf_base // 32) * 32
        ctx.enter_context(nc.sbuf_tensor("arena", [P, 206 * 256], F32))
        placed = {}

        def at(name, kb, shape, dt=F32):
            placed[name] = nc.alloc_sbuf_tensor_at(name, shape, dt, offset=base + int(kb * 1024))
            return placed[name]

        def sem(name):
            return ctx.enter_context(nc.semaphore(name))

        WR = at("w_raw", 0, [P, 2, 8, P])
        WH = at("w_high", 8, [P, 2, 8, P], F32R)
        WL = at("w_low", 16, [P, 2, 8, P], F32R)
        XH = at("resid", 24, [P, KT, T])
        AH = at("act_high", 40, [P, KT, T], F32R)
        AL = at("act_low", 56, [P, KT, T], F32R)
        M = at("mix_out", 72, [P, KT, T])
        HH = at("hid_high", 88, [P, KT, T], F32R)
        HL = at("hid_low", 104, [P, KT, T], F32R)
        TMP = [at(f"tmp{n}", 120 + 2 * n, [P, T]) for n in range(6)]
        R1 = at("rstd_a", 132, [P, T])
        R2 = at("rstd_b", 134, [P, T])
        SQA = at("sum_sq", 136, [P, T])
        ONES = at("ones", 138, [P, P])
        IDENT = at("ident", 138.5, [P, P])
        BONES = at("head_ones", 139, [P, P])
        COL = at("cols", 139.5, [P, 192])
        MOD = at("mod", 140.25, [P, 24])
        SMALL = at("small", 140.375, [P, 96])
        CST = at("consts", 140.75, [P, 8])
        XTOK = at("x_tok", 72, [P, TT, D])
        ROWS = at("param_rows", 199, [P, 2, P])
        CSIL = at("c_act", 200, [P, 2 * KT])
        ADA = at("w_ada_piece", 88, [P, 2, KT, T])
        VTOK = at("v_tok", 173, [P, TT * NH, HB])
        VC = at("v_centred", 181, [P, TT * NH, HB])
        VSQ = at("v_sq", 191, [P, TT * NH, HB])
        U = at("u_act", 141, [P, JA, T])
        SG = at("gate_a", 149, [P, JA, T])
        WSP = at("w_spatial_sb", 157, [P, NH, P])
        WSPT = at("w_spatial_t", 161, [P, NH, P])
        LVG = at("ln_v_gain", 165, [P, DA])
        LVB = at("ln_v_bias", 167, [P, DA])
        BSP = at("b_spatial_sb", 169, [P, JA, P])
        WUA = at("w_up_a_up", 171, [P, DA])
        RKVG = at("rkvg", 72, [P, 4 * JA, T])
        WAD = at("wd_ad", 104, [P, T])
        PR = at("p_shift", 106, [P, 2, T + 2])
        CS = at("decay_sum", 149, [P, JA, T])
        SIG = at("decay_sig", 157, [P, JA, T])
        ICL = at("iclr_a", 173, [P, JA, T])
        KKN = at("kk_norm", 181, [P, JA, T])
        SQB = at("sq_bulk", 40, [P, JA, T])
        RSET = at("scan_reset", 189, [P, T])
        YT = at("y_rwkv", 48, [P, JA, T])
        AR = [at(f"ar_ops{n}", 40 + 2 * n, [P, JA, 2 * CH]) for n in range(3)]
        BK = at("bk_ops", 46, [P, JA, 2 * CH])
        BKT = [at(f"bk_tok{n}", 56 + 2 * n, [P, JA, P]) for n in range(3)]
        UV = [at(f"uv{n}", 62 + 2 * n, [P, NH, CH]) for n in range(3)]
        VS = at("v_ops", 68, [P, JA, 2 * CH])
        GA = at("g_masked_a", 70, [P, NH, CH])
        ZS = [at(f"z_sb{n}", 104 + 2 * n, [P, JA, CH]) for n in range(3)]
        GR = [at(f"g_masked_r{n}", 189 + 2 * n, [P, NH, CH]) for n in range(3)]
        MSKG = at("mask_g", 112.25, [P, 2 * CH])
        MSKS = at("mask_s", 112.75, [P, CH])
        MSKD = at("mask_d", 113, [P, CH])
        S = at("state", 113.25, [P, JA, CH])
        FS = at("state_decay", 114.25, [P, 3, JA])
        MSKSD = at("mask_sd", 114.5, [P, CH])
        ID2 = at("ident_halves", 114.75, [P, CH])
        EL = at("e_incl", 115, [P, JA, CH])
        ENL = at("e_neg", 116, [P, JA, CH])
        EX = at("e_excl", 117, [P, JA, CH])
        ND = at("n_diag", 118, [P, JA, CH])
        NDT = at("n_diag_t", 128, [P, JA, CH])
        NOT = at("n_off_t", 130, [P, JA, CH])
        X1 = at("pow_1", 132, [P, JA, CH])
        X1T = at("pow_1t", 134, [P, JA, CH])
        TD = at("inv_diag", 136, [P, JA, CH])
        TDF = at("inv_diag_full", 165, [P, JA, CH])
        FM = at("f_mat", 167, [P, JA, CH])
        FMT = at("f_mat_t", 169, [P, JA, CH])
        TDT = at("inv_diag_t", 171, [P, JA, CH])
        Y1 = at("inv_part_t", 195, [P, JA, CH])
        F2 = at("f_sq", 197, [P, JA, CH])
        TTM = at("inv_full_t", 199, [P, JA, CH])
        CQ = at("latents", 141, [P, QL + KVL, T])
        CQH = at("latents_high", 153, [P, QL + KVL, T], F32R)
        CQL = at("latents_low", 165, [P, QL + KVL, T], F32R)
        KR = at("k_rope", 177, [ROPE, T])
        QR = at("q_rope", 179, [ROPE, T])
        QN = at("q_nope", 181, [P, T])
        KN = at("k_nope", 183, [P, T])
        VM = at("v_mla", 185, [P, TT, P])
        PRB = at("probs", 187, [P, 2, T])
        PT = at("probs_t", 191, [P, 2, TT, P])
        COS = at("cos", 195, [ROPE, T])
        SIN = at("sin", 197, [ROPE, T])
        ANG = at("angle", 199, [ROPE, T])
        ANGK = at("angle_k", 201, [ROPE, T], I32)
        PIX = at("positions_sb", 141, [ROPE, T], I32)
        CMASK = at("causal_mask", 203, [P, P])
        QG = at("hg_q", 141, [P, T])
        FG = at("hg_f", 143, [P, T])
        KG = at("hg_k", 145, [P, T])
        BG = at("hg_b", 147, [P, T])
        GG = at("hg_gate", 149, [P, T])
        VG = at("hg_v", 151, [P, TT, P])
        QREL = at("hg_q_rel", 153, [P, T])
        KREL = at("hg_k_rel", 155, [P, T])
        QDEC = at("hg_q_dec", 157, [P, T])
        KDEC = at("hg_k_dec", 159, [P, T])
        EBL = at("hg_decay", 161, [P, T // HC])
        KDT = at("hg_k_dec_t", 162, [P, TT, P])
        AT = at("hg_scores", 164, [P, TT, P])
        ST = at("hg_state", 182, [P, T // HC, P])
        OG = at("hg_out", 168, [P, T])
        HMSK = at("hg_mask", 170, [P, TT, P], I32)
        HRST = at("hg_reset", 172, [P, T])
        TG = [at(f"hg_t{n}", 174 + 2 * n, [P, T]) for n in range(4)]
        OSQ = at("hg_out_sq", 190, [P, T])
        OSD = at("hg_out_dev", 192, [P, T])
        VF = at("hg_v_feature", 194, [P, T])
        LREL = at("hg_b_less_ref", 196, [P, T])
        LBS = at("hg_bounds", 204.5, [P, 3 * HEADS])
        LBH = at("hg_bound", 204.75, [P, 2])
        BON = at("bonus", 120, [P, JA, T])
        FC = at("inv_freq_sb", 205, [ROPE, 1])
        OTOK = at("out_tok", 88, [P, TT, D])

        PB = [ctx.enter_context(nc.psum_tensor(f"bank{n}", [P, 512], F32)) for n in range(8)]

        rows, col_of = [], {}
        for name, src, n in (("gains", norm_gains.rearrange("l a (k p) -> (l a k) p", p=P), 8 * KT),
                             ("b_ada", b_ada.rearrange("(k p) -> k p", p=P), 3 * KT),
                             ("mu", mu_b.rearrange("(k p) -> k p", p=P), 17),
                             ("lb", hgrn_lb.rearrange("l (k p) -> (l k) p", p=P), 2 * HEADS),
                             ("ln_g", ln_g.rearrange("(k p) -> k p", p=P), KT),
                             ("ln_b", ln_b.rearrange("(k p) -> k p", p=P), KT),
                             ("w0", w0.rearrange("(k p) -> k p", p=P), JA),
                             ("a0", a0.rearrange("(k p) -> k p", p=P), JA),
                             ("k_k", k_k.rearrange("(k p) -> k p", p=P), JA),
                             ("k_a", k_a.rearrange("(k p) -> k p", p=P), JA),
                             ("r_k", r_k.rearrange("(k a) d -> k (a d)", a=2), JA),
                             ("gn_g", gn_g.rearrange("(k a) d -> k (a d)", a=2), JA),
                             ("gn_b", gn_b.rearrange("(k a) d -> k (a d)", a=2), JA),
                             ("q_norm", mla_q_norm.rearrange("l (k p) -> (l k) p", p=P), QL),
                             ("kv_norm", mla_kv_norm.rearrange("l (k p) -> (l k) p", p=P), KVL),
                             ("o_norm", hgrn_o_norm, 1)):
            start = sum(r[2] for r in rows)
            if start < P < start + n:
                rows.append((None, None, P - start))
                start = P
            col_of[name] = start
            rows.append((name, src, n))
        n_rows = sum(r[2] for r in rows)

        def col(name, j=0, n=1, p0=0, p1=P):
            return COL[p0:p1, col_of[name] + j:col_of[name] + j + n]

        def gain(layer, which, k):
            return col("gains", (layer * 4 + which) * KT + k)

        A0 = 0
        B0 = A0 + 3 * JA
        O0 = B0 + 4 * JA + 1
        I0 = O0 + KT
        H0 = I0 + QL + KVL + 1
        V0 = H0 + 4 * HEADS
        F0 = V0 + KT
        G0 = F0 + 2 * KT * NQ
        W0 = G0 + 4 * HEADS
        E0 = W0 + KT
        NJ = E0 + 2 * KT * NQ
        USE = {n: k for k, n in enumerate(("in", "out", "mla", "mla_o", "mlp0", "hgrn", "hgrn_o", "mlp1"))}

        x_loaded, c_loaded, par_loaded = sem("x_loaded"), sem("c_loaded"), sem("par_loaded")
        bc_loaded = sem("bc_loaded")
        pos_loaded = sem("pos_loaded")
        ada_loaded = [sem("ada_loaded0"), sem("ada_loaded1")]
        w_loaded = [sem("w_loaded0"), sem("w_loaded1")]
        w_hi, w_lo = sem("w_hi"), sem("w_lo")
        job_done = sem("job_done")
        act_hi, act_lo = sem("act_hi"), sem("act_lo")
        const_ready, const_pool, colz = sem("const_ready"), sem("const_pool"), sem("cols_ready")
        x_turned, x_read, par_turned = sem("x_turned"), sem("x_read"), sem("par_turned")
        c_ready, ada_done, mod_ready = sem("c_ready"), sem("ada_done"), sem("mod_ready")
        gate_ready = sem("gate_ready")
        free = {n: sem("free_" + n) for n in ("a", "b", "o", "mi", "h", "mo", "f0", "g", "go", "f1")}
        v_gelu, v_ms, v_sd, v_ready = sem("v_gelu"), sem("v_ms"), sem("v_sd"), sem("v_ready")
        wsp_t, wsp_r, sp_done, u_ready, oa_ready = (sem("wsp_t"), sem("wsp_r"), sem("sp_done"), sem("u_ready"),
                                                    sem("oa_ready"))
        wsp_masked = sem("wsp_masked")
        p_copied, p_free, p_mixed = sem("p_copied"), sem("p_free"), sem("p_mixed")
        lr_tanh, lr_done, lr_sig = sem("lr_tanh"), sem("lr_done"), sem("lr_sig")
        kk_sq, kk_ss, kk_sd, rk_ready, rk_done, bulk_ready = (sem("kk_sq"), sem("kk_ss"), sem("kk_sd"),
                                                              sem("rk_ready"), sem("rk_done"), sem("bulk_ready"))
        g_silu = sem("g_silu")
        ch_exp, ch_vs, ch_ops, ch_g, ch_t, ch_nd, ch_tok = (sem("ch_" + n) for n in ("exp", "vs", "ops", "g", "t",
                                                                                     "nd", "tok"))
        pw_pe, pw_dve, pw_act, in_pe, in_dve, in_act = (sem(n) for n in ("pw_pe", "pw_dve", "pw_act", "in_pe",
                                                                         "in_dve", "in_act"))
        mv_done, mv_read = sem("mv_done"), sem("mv_read")
        z_done, z_read, u_done, u_read, s_new, y_done, y_read = (
            sem("z_done"), sem("z_read"), sem("u_done"), sem("u_read"), sem("s_new"), sem("y_done"), sem("y_read"))
        gn_pe, gn_dve, gn_act, ob_ready = sem("gn_pe"), sem("gn_dve"), sem("gn_act"), sem("ob_ready")
        ln_pe, ln_dve, ln_act, x1_ready = sem("ln_pe"), sem("ln_dve"), sem("ln_act"), sem("x1_ready")
        nm_dve, nm_pe, nm_act, nm_sq = sem("nm_dve"), sem("nm_pe"), sem("nm_act"), sem("nm_sq")
        rp_ang, rp_sin = sem("rp_ang"), sem("rp_sin")
        cq_ready, kr_ready = sem("cq_ready"), sem("kr_ready")
        cq_hi, cqh_ready, cq_lo = sem("cq_normed"), sem("cq_high"), sem("cq_low")
        lb_diff, lb_exp = sem("lb_diff"), sem("lb_exp")
        h_q, h_r, h_s, h_mx, h_exp, h_pn, h_pt, h_ptr, h_o, h_or = (
            sem("h_q"), sem("h_r"), sem("h_s"), sem("h_mx"), sem("h_exp"), sem("h_pn"), sem("h_pt"), sem("h_ptr"),
            sem("h_o"), sem("h_or"))
        mx_out, resid_ready = sem("mx_out"), sem("resid_ready")
        m_relu, m_hid, m_hidlo = sem("m_relu"), sem("m_hid"), sem("m_hidlo")
        nm_dev = sem("nm_dev")
        f_up, f_dn = [sem("free_up0"), sem("free_up1")], [sem("free_dn0"), sem("free_dn1")]
        g_vt, g_vc = sem("g_vt"), sem("g_vc")
        g_silu3, g_f, g_ln, g_diff, g_exp, g_ops, g_sc, g_at, g_kt, g_inc, g_st, g_out, g_sq, g_ss, g_sd, g_fin = (
            sem("g_" + n) for n in ("silu3", "f", "ln", "diff", "exp", "ops", "sc", "at", "kt", "inc", "st", "out",
                                    "sq", "ss", "sd", "fin"))
        out_t, out_r, stored = sem("out_t"), sem("out_r"), sem("stored")
        block = ctx.enter_context(nc.Block())

        def following(k, wrap=1):
            return (k + 1) & (NCH - 1) if wrap else k + 1

        def rwkv_pipeline(engine, step):
            step(0, 0, None, None, None, None)
            step(1, 1, 0, 0, None, None)
            with engine.Fori(0, (NCH - 2) // 3) as g:
                for n in range(3):
                    step(g * 3 + 2 + n, (2 + n) % 3, g * 3 + 1 + n, (1 + n) % 3, g * 3 + n, n)
            step(None, None, NCH - 1, (NCH - 1) % 3, NCH - 2, (NCH - 2) % 3)
            step(None, None, None, None, NCH - 1, (NCH - 1) % 3)

        w_in_v = w_in.rearrange("(k p) n -> p k n", p=P)
        w_out_v = w_out.rearrange("(k p) n -> p k n", p=P)
        mla_in_v = mla_w_in[0].rearrange("(k p) n -> p k n", p=P)
        uq_v = mla_w_uq[0].rearrange("(k p) n -> p k n", p=P)
        ukv_v = mla_w_ukv[0].rearrange("(k p) n -> p k n", p=P)
        mla_o_v = mla_w_o[0].rearrange("(k p) n -> p k n", p=P)
        hg_in_v = hgrn_w_in[0].rearrange("(k p) n -> p k n", p=P)
        hg_o_v = hgrn_w_o[0].rearrange("(k p) n -> p k n", p=P)
        w1_v = [mlp_w1[l].rearrange("(k p) n -> p k n", p=P) for l in range(2)]
        w2_v = [mlp_w2[l].rearrange("(q k p) n -> p (q k) n", p=P, k=KT) for l in range(2)]
        ada_v = w_ada.rearrange("(p j) n -> p j n", j=KT)

        @block.sync
        def _(sp):
            sp.dma_start(CSIL[:, 0:KT], c.rearrange("a (p j) -> (a p) j", j=KT)).then_inc(c_loaded, 16)
            for n in range(6):
                if n >= 2:
                    sp.wait_ge(ada_done, n - 1)
                sp.dma_start(ADA[:, n % 2], ada_v[:, :, n * T:(n + 1) * T]).then_inc(ada_loaded[n % 2], 16)

            def load(c0, src, r=0, kt=8, m=P):
                if c0 >= 2:
                    sp.wait_ge(w_lo, c0 - 1 + r)
                sp.dma_start(WR[:, c0 % 2, 0:kt, 0:m], src).then_inc(w_loaded[c0 % 2], 16)

            for j in range(2):
                load(j, w_in_v[:, :, j * P:(j + 1) * P])
            with sp.Fori(1, (O0 - 1) // 2) as i:
                for s in range(2):
                    load(A0 + 2 + s, w_in_v[:, :, bass.ds(i * 2 * P + s * P, P)], (i - 1) * 2)
            load(O0 - 1, w_in_v[:, :, (O0 - 1) * P:O0 * P])
            with sp.Fori(0, KT // 2) as i:
                for s in range(2):
                    load(O0 + s, w_out_v[:, :, bass.ds(i * 2 * P + s * P, P)], i * 2)
            for j in range(QL + KVL):
                load(I0 + j, mla_in_v[:, :, j * P:(j + 1) * P])
            load(H0 - 1, mla_in_v[:, :, (QL + KVL) * P:(QL + KVL) * P + ROPE], m=ROPE)
            with sp.Fori(0, HEADS) as h:
                load(H0, uq_v[:, :, bass.ds(h * (NOPE + ROPE), NOPE)], h * 4, kt=QL)
                load(H0 + 1, uq_v[:, :, bass.ds(h * (NOPE + ROPE) + NOPE, ROPE)], h * 4, kt=QL, m=ROPE)
                load(H0 + 2, ukv_v[:, :, bass.ds(h * 2 * P, P)], h * 4, kt=KVL)
                load(H0 + 3, ukv_v[:, :, bass.ds(h * 2 * P + P, P)], h * 4, kt=KVL)
            with sp.Fori(0, KT // 2) as i:
                for s in range(2):
                    load(V0 + s, mla_o_v[:, :, bass.ds(i * 2 * P + s * P, P)], i * 2)

            def load_mlp(l, j0):
                with sp.Fori(0, NQ) as q:
                    with sp.Fori(0, KT // 2) as i:
                        for s in range(2):
                            load(j0 + s, w1_v[l][:, :, bass.ds(q * D + i * 2 * P + s * P, P)], q * 2 * KT + i * 2)
                    with sp.Fori(0, KT // 2) as i:
                        for s in range(2):
                            load(j0 + KT + s, w2_v[l][:, bass.ds(q * KT, KT), bass.ds(i * 2 * P + s * P, P)],
                                 q * 2 * KT + i * 2)

            load_mlp(0, F0)
            with sp.Fori(1, HEADS + 1) as h1:
                for j, part in enumerate((1, 0, 2, 3)):
                    load(G0 + j, hg_in_v[:, :, bass.ds(h1 * P + (part * D - P), P)], h1 * 4 - 4)
            with sp.Fori(0, KT // 2) as i:
                for s in range(2):
                    load(W0 + s, hg_o_v[:, :, bass.ds(i * 2 * P + s * P, P)], i * 2)
            load_mlp(1, E0)
            sp.wait_ge(out_r, TT * 2)
            sp.dma_start(out[0].rearrange("(t p) d -> p t d", p=P), OTOK[:, :, :]).then_inc(stored, 16)
            sp.wait_ge(stored, 16)

        @block.gpsimd
        def _(gp):
            gp.memset(ONES[:, :], 1.0)
            gp.memset(IDENT[:, :], 0.0)
            gp.memset(BONES[:, :], 0.0)
            gp.memset(CST[:, 0:1], 1e-5)
            gp.memset(CST[:, 1:2], 1e-12)
            gp.memset(CST[:, 2:3], 64e-5)
            gp.memset(CST[:, 3:4], 1e-6)
            gp.memset(CST[:, 4:5], float(np.pi / 2))
            gp.memset(RSET[:, :], 1.0)
            gp.drain()
            gp.affine_select(out=IDENT[:, :], in_=IDENT[:, :], compare_op=ALU.not_equal, fill=1.0, base=0,
                             pattern=[[-1, P]], channel_multiplier=1)
            gp.drain()
            gp.memset(BONES[0:HB, 0:HB], 1.0)
            gp.drain()
            gp.memset(BONES[HB:P, HB:P], 1.0)
            gp.drain()
            gp.memset(RSET[:, :].rearrange("p (c t) -> p c t", t=CH)[:, :, 0:1], 0.0)
            gp.drain()
            gp.nop().then_inc(const_ready, 1)
            at_row = 0
            gp.memset(ROWS[:, :, :], 0.0)
            gp.drain()
            n_dma = 0
            for name, src, n in rows:
                if name:
                    t, r = divmod(at_row, P)
                    gp.dma_start(ROWS[r:r + n, t, :], src).then_inc(par_loaded, 16)
                    n_dma += 1
                at_row += n
            gp.dma_start(WSP[:, :, :], w_spatial.rearrange("g t s -> t g s")).then_inc(bc_loaded, 16)
            gp.dma_start(LVG[:, :], ln_v_g.rearrange("g d -> (g d)").partition_broadcast(P)).then_inc(bc_loaded, 16)
            gp.dma_start(LVB[:, :], ln_v_b.rearrange("g d -> (g d)").partition_broadcast(P)).then_inc(bc_loaded, 16)
            for a in range(2):
                gp.dma_start(BSP[a * HB:(a + 1) * HB, :, :],
                             b_spatial.rearrange("(j a) t -> a j t", a=2)[a].partition_broadcast(HB))\
                    .then_inc(bc_loaded, 16)
            gp.dma_start(WUA[0:64, :], w_up).then_inc(bc_loaded, 16)
            gp.dma_start(WUA[64:128, :], a_up).then_inc(bc_loaded, 16)
            gp.wait_ge(bc_loaded, 16 * 7)
            gp.affine_select(out=WSP[:, :, :], in_=WSP[:, :, :], compare_op=ALU.is_ge, fill=0.0, base=0,
                             pattern=[[0, NH], [-1, P]], channel_multiplier=1).then_inc(wsp_masked, 1)

            def low(c0, r=0, kt=8, m=P):
                gp.wait_ge(w_hi, c0 + 1 + r)
                gp.tensor_tensor(WL[:, c0 % 2, 0:kt, 0:m], WR[:, c0 % 2, 0:kt, 0:m],
                                 WH[:, c0 % 2, 0:kt, 0:m].bitcast(F32), ALU.subtract).then_inc(w_lo, 1)

            with gp.Fori(0, O0 // 2) as i:
                for s in range(2):
                    low(s, i * 2)
            low(O0 - 1)
            gp.wait_ge(p_mixed, 4 * JA + 1)
            gp.memset(MSKG[:, :], 1.0)
            gp.memset(MSKS[:, :], 1.0)
            gp.memset(MSKD[:, :], 0.0)
            gp.drain()
            for half in range(2):
                rows_ = MSKG[half * CH:(half + 1) * CH, :]
                gp.affine_select(out=rows_[:, 0:CH], in_=rows_[:, 0:CH], compare_op=ALU.is_gt, fill=0.0,
                                 base=0, pattern=[[1, CH]], channel_multiplier=-1)
                gp.affine_select(out=rows_[:, CH:2 * CH], in_=rows_[:, CH:2 * CH], compare_op=ALU.is_ge,
                                 fill=0.0, base=0, pattern=[[1, CH]], channel_multiplier=-1)
                gp.drain()
            for half in range(2):
                ms = MSKS[half * CH:(half + 1) * CH, :]
                gp.affine_select(out=ms, in_=ms, compare_op=ALU.is_gt, fill=0.0, base=0,
                                 pattern=[[-1, CH]], channel_multiplier=1)
                md = MSKD[half * CH:(half + 1) * CH, :].rearrange("p (b t) -> p b t", t=16)
                gp.affine_select(out=md, in_=md, compare_op=ALU.is_gt, fill=1.0, base=0,
                                 pattern=[[16, CH // 16], [0, 16]], channel_multiplier=-1)
                gp.drain()
                gp.affine_select(out=md, in_=md, compare_op=ALU.is_ge, fill=0.0, base=15,
                                 pattern=[[16, CH // 16], [0, 16]], channel_multiplier=-1)
                gp.drain()
            gp.tensor_tensor(MSKSD[:, :], MSKS[:, :], MSKD[:, :], ALU.mult).then_inc(const_pool, 1)
            with gp.Fori(0, KT // 2) as i:
                for s in range(2):
                    low(O0 + s, i * 2)
            gp.memset(CMASK[:, :], 0.0)
            gp.drain()
            gp.affine_select(out=CMASK[:, :], in_=CMASK[:, :], compare_op=ALU.is_ge, fill=NEG, base=0,
                             pattern=[[-1, P]], channel_multiplier=1).then_inc(const_pool, 1)
            for j in range(QL + KVL):
                low(I0 + j)
            low(H0 - 1, m=ROPE)
            with gp.Fori(0, HEADS) as h:
                low(H0, h * 4, kt=QL)
                low(H0 + 1, h * 4, kt=QL, m=ROPE)
                low(H0 + 2, h * 4, kt=KVL)
                low(H0 + 3, h * 4, kt=KVL)
            with gp.Fori(0, KT // 2) as i:
                for s in range(2):
                    low(V0 + s, i * 2)
            with gp.Fori(0, NQ * KT) as i:
                for s in range(2):
                    low(F0 + s, i * 2)
            gp.memset(TG[0][:, :], 1.0)
            gp.memset(HRST[:, :], 1.0)
            gp.drain()
            gp.memset(HRST[:, :].rearrange("p (c t) -> p c t", t=HC)[:, :, 0:1], 0.0)
            hm = TG[0][:, :].rearrange("p (a b t) -> p a b t", a=TT, t=HC)
            gp.affine_select(out=hm, in_=hm, compare_op=ALU.is_ge, fill=0.0, base=0,
                             pattern=[[0, TT], [HC, P // HC], [1, HC]], channel_multiplier=-1)
            gp.drain()
            gp.affine_select(out=hm, in_=hm, compare_op=ALU.is_ge, fill=0.0, base=0,
                             pattern=[[0, TT], [-HC, P // HC], [0, HC]], channel_multiplier=1)
            gp.drain()
            gp.tensor_copy(HMSK[:, :, :].rearrange("p a t -> p (a t)"), TG[0][:, :])
            gp.memset(AT[:, :, :], 0.0)
            gp.drain()
            gp.nop().then_inc(const_pool, 1)
            with gp.Fori(0, HEADS * 2) as i:
                for s in range(2):
                    low(G0 + s, i * 2)
            with gp.Fori(0, KT // 2) as i:
                for s in range(2):
                    low(W0 + s, i * 2)
            with gp.Fori(0, NQ * KT) as i:
                for s in range(2):
                    low(E0 + s, i * 2)

        @block.tensor
        def _(pe):
            def job(c0, r, fr, n, kt=8, m=P, hi=AH, lo=AL, k0=0, token_major=False, ready=None):
                s = c0 % 2
                pe.wait_ge(w_lo, c0 + 1 + r)
                pe.wait_ge(fr, n)
                if not token_major:
                    for k in range(kt):
                        if ready is not None:
                            pe.wait_ge(ready[0], ready[1] + k + 1)
                        for w, a in ((WH, hi), (WH, lo), (WL, hi)):
                            mm = pe.matmul(PB[s][0:m, :], w[:, s, k, 0:m], a[:, k0 + k, :],
                                           start=(k == 0 and w is WH and a is hi), stop=(k == kt - 1 and w is WL))
                else:
                    for t in range(TT):
                        for k in range(kt):
                            for w, a in ((WH, hi), (WH, lo), (WL, hi)):
                                mm = pe.matmul(PB[s][:, t * P:(t + 1) * P], a[:, k0 + k, t * P:(t + 1) * P],
                                               w[:, s, k, :], start=(k == 0 and w is WH and a is hi),
                                               stop=(k == kt - 1 and w is WL))
                mm.then_inc(job_done, 1)

            def hold(*waits):
                waits = [(signal, pe.to_reg(n)) for signal, n in waits]
                pe.wait_ge(const_ready, 1)
                for signal, n in waits:
                    pe.wait_ge(signal, n)

            pe.wait_ge(const_ready, 1)
            pe.wait_ge(par_loaded, 16 * sum(1 for r in rows if r[0]))
            for t in range(2):
                mm = pe.transpose(PB[7][:, t * P:(t + 1) * P], ROWS[:, t, :], IDENT[:, :])
            mm.then_inc(par_turned, 1)
            pe.wait_ge(x_loaded, 16)
            for k in range(KT):
                if k == 7:
                    pe.wait_ge(colz, 1)
                for t in range(TT):
                    mm = pe.transpose(PB[k][:, t * P:(t + 1) * P], XTOK[:, t, k * P:(k + 1) * P], IDENT[:, :])
                mm.then_inc(x_turned, 1)
            pe.wait_ge(c_ready, 1)
            pe.wait_ge(x_read, KT)
            for n in range(3 * KT // 4):
                pe.wait_ge(ada_loaded[n % 2], 16 * (n // 2 + 1))
                for b in range(4):
                    col_ps = PB[7 if n < 4 else 6][:, 4 * n + b:4 * n + b + 1]
                    for j in range(KT):
                        mm = pe.matmul(col_ps, ADA[:, n % 2, j, b * P:(b + 1) * P], CSIL[:, KT + j:KT + j + 1],
                                       start=(j == 0), stop=(j == KT - 1))
                mm.then_inc(ada_done, 1)

            job(A0, 0, free["a"], 1, ready=(act_lo, 0))
            job(A0 + 1, 0, free["a"], 2)
            for i in range(2, JA):
                job(A0 + i, 0, free["a"], i + 1)
            for i in range(JA, 2 * JA):
                job(A0 + i, 0, free["a"], i + 1, token_major=True)
            with pe.Fori(0, JA // 2) as i:
                for s in range(2):
                    job(A0 + 2 * JA + s, i * 2, free["a"], i * 2 + s + 1 + 2 * JA)
            pe.wait_ge(wsp_masked, 1)
            for g in range(NH):
                mm = pe.transpose(PB[2 + g // 4][:, (g % 4) * P:(g % 4 + 1) * P], WSP[:, g, :], IDENT[:, :])
            mm.then_inc(wsp_t, 1)
            with pe.Fori(0, 2 * JA) as i:
                for s in range(2):
                    job(B0 + s, i * 2, free["b"], i * 2 + s + 1)
            job(O0 - 1, 0, free["b"], 4 * JA + 1)
            pe.wait_ge(wsp_r, 1)
            pe.wait_ge(v_ready, 1)
            for j in range(JA):
                for t in range(TT):
                    for a in range(2):
                        g = 2 * j + a
                        mm = pe.matmul(PB[2 + j][a * HB:(a + 1) * HB, t * P:(t + 1) * P],
                                       VC[:, t * NH + g, :], WSPT[:, g, :], start=True, stop=True)
                mm.then_inc(sp_done, 1)
            pe.wait_ge(lr_tanh, 1)
            for j in range(JA):
                mm = pe.matmul(PB[(6 + j) % 8][:, :], WUA[0:64, j * P:(j + 1) * P], WAD[0:64, :],
                               start=True, stop=True)
                mm.then_inc(lr_done, 1)
            pe.wait_ge(oa_ready, 1)
            for j in range(JA):
                mm = pe.matmul(PB[2 + j][:, :], WUA[64:128, j * P:(j + 1) * P], WAD[64:128, :],
                               start=True, stop=True)
                mm.then_inc(lr_done, 1)
            pe.wait_ge(kk_sq, 1)
            pe.wait_ge(lr_sig, 2)
            for j in range(JA):
                mm = pe.matmul(PB[(6 + j) % 8][:, :], BONES[:, :], SQB[:, j, :], start=True, stop=True)
            mm.then_inc(kk_ss, 1)
            pe.wait_ge(rk_ready, 1)
            for j in range(JA):
                mm = pe.matmul(PB[2 + j][:, :], BONES[:, :], SQB[:, j, :], start=True, stop=True)
            mm.then_inc(rk_done, 1)
            pe.wait_ge(bulk_ready, 1)

            def heads():
                return [(h, h // 2, (h % 2) * HB) for h in range(NH)]

            def hs(h, bank):
                return PB[bank][h % 2 * HB:h % 2 * HB + HB, h // 2 * HB:(h // 2 + 1) * HB]

            def each(bank, left, right):
                for h, j, p in heads():
                    mm = pe.matmul(hs(h, bank), left[p:p + HB, j, :], right[p:p + HB, j, :], start=True, stop=True)
                return mm

            def step(k1, s1, k2, s2, k3, s3):
                if k1 is not None:
                    hold((ch_ops, k1 + 1), (ch_vs, k1 + 1))
                    for j in range(JA):
                        pe.transpose(PB[6][:, j * P:(j + 1) * P], VS[:, j, :], IDENT[:, :])
                    for h, j, p in heads()[0::2]:
                        pe.matmul(PB[1][:, j * P:(j + 1) * P], BK[p:p + HB, j, :], AR[s1][p:p + HB, j, :],
                                  start=True, stop=True)
                if k2 is not None:
                    hold((pw_dve, k2 * 4 + 3), (pw_act, k2 * 3 + 3))
                    each(0, X1T, TD).then_inc(pw_pe, 1)
                if k1 is not None:
                    for h, j, p in heads()[1::2]:
                        pe.matmul(PB[2][:, j * P:(j + 1) * P], BK[p:p + HB, j, :], AR[s1][p:p + HB, j, :],
                                  start=True, stop=True)
                    for h, j, p in heads():
                        mm = pe.matmul(hs(h, 3), AR[s1][p:p + HB, j, 0:CH], BK[p:p + HB, j, p:p + CH],
                                       start=True, stop=True)
                    mm.then_inc(ch_g, 1)
                    if k3 is not None:
                        hold((in_dve, k3 * 3 + 3))
                    for j in range(JA):
                        mm = pe.transpose(PB[5][:, j * P:(j + 1) * P], BK[:, j, :], IDENT[:, :])
                    mm.then_inc(ch_t, 1)
                if k2 is not None:
                    hold((pw_dve, k2 * 4 + 4))
                    each(0, NOT, TDF).then_inc(in_pe, 1)
                if k3 is not None:
                    hold((s_new, k3 + 1), (y_read, k3 + 1))
                    for h, j, p in heads():
                        mm = pe.matmul(hs(h, 4), AR[s3][p:p + HB, j, 0:CH], S[p:p + HB, j, :],
                                       start=True, stop=True)
                    mm.then_inc(z_done, 1)
                    for h, j, p in heads():
                        pe.matmul(PB[7][p:p + HB, j * HB:(j + 1) * HB], S[p:p + HB, j, :],
                                  AR[s3][p:p + HB, j, CH:P], start=(j == 0), stop=False)
                if k1 is not None:
                    hold((ch_nd, k1 + 1))
                    each(1, NDT, ND)
                    each(2, ND, NDT).then_inc(pw_pe, 1)
                    hold((ch_tok, k1 + 1))
                if k2 is not None:
                    each(5, TDF, NOT)
                    for h, j, p in heads():
                        mm = pe.matmul(hs(h, 6), TDF[p:p + HB, j, :], ID2[p:p + HB, :], start=True, stop=True)
                    mm.then_inc(in_pe, 1)
                if k3 is not None:
                    hold((z_read, k3 + 1), (in_dve, k3 * 3 + 3))
                    each(4, TTM, ZS[s3]).then_inc(u_done, 1)
                if k1 is not None:
                    if k2 is not None:
                        hold((in_dve, k2 * 3 + 1))
                    for h, j, p in heads():
                        mm = pe.matmul(hs(h, 0), GA[CH - p:P - p, h, :], UV[s1][CH - p:P - p, h, :], start=True,
                                       stop=True)
                    mm.then_inc(mv_done, 1)
                if k1 is not None:
                    hold((pw_dve, k1 * 4 + 1), (pw_act, k1 * 3 + 1))
                    each(3, X1T, TD)
                    each(1, X1T, X1)
                    each(2, X1, X1T).then_inc(pw_pe, 1)
                if k2 is not None:
                    hold((in_dve, k2 * 3 + 1), (in_act, k2 * 2 + 1))
                    if k1 is not None:
                        hold((mv_read, k1 + 1))
                    each(0, FM, TDT)
                    each(5, FMT, FM).then_inc(in_pe, 1)
                if k3 is not None:
                    hold((u_read, k3 + 1))
                    for h, j, p in heads():
                        pe.matmul(PB[7][p:p + HB, (JA + j) * HB:(JA + j + 1) * HB], BKT[s3][:, j, p:p + HB],
                                  UV[s3][:, h, :], start=False, stop=False)
                        mm = pe.matmul(PB[7][p:p + HB, j * HB:(j + 1) * HB], UV[s3][:, h, :], GR[s3][:, h, :],
                                       start=False, stop=(j == JA - 1))
                    mm.then_inc(y_done, 1)
                if k1 is not None:
                    hold((pw_dve, k1 * 4 + 2), (pw_act, k1 * 3 + 2))
                    each(3, X1T, TD)
                    each(2, X1, X1T).then_inc(pw_pe, 1)
                if k2 is not None:
                    hold((in_dve, k2 * 3 + 2), (in_act, k2 * 2 + 2))
                    each(5, F2, Y1).then_inc(in_pe, 1)

            rwkv_pipeline(pe, step)
            pe.wait_ge(y_read, NCH + 1)
            for j in range(JA):
                mm = pe.matmul(PB[2 + j][:, :], BONES[:, :], YT[:, j, :], start=True, stop=True)
            mm.then_inc(gn_pe, 1)
            pe.wait_ge(gn_dve, 1)
            for j in range(JA):
                mm = pe.matmul(PB[2 + j][:, :], BONES[:, :], SQB[:, j, :], start=True, stop=True)
            mm.then_inc(gn_pe, 1)

            def eight_jobs(c0, fr, use, hi=AH, lo=AL):
                pe.wait_ge(act_lo, 8 * (USE[use] + 1))
                with pe.Fori(0, KT // 2) as i:
                    for s in range(2):
                        job(c0 + s, i * 2, fr, i * 2 + s + 1, hi=hi, lo=lo)

            eight_jobs(O0, free["o"], "out")
            pe.wait_ge(ln_dve, 1)
            mm = pe.matmul(PB[2][:, :], ONES[:, :], SQA[:, :], start=True, stop=True)
            mm.then_inc(ln_pe, 1)
            pe.wait_ge(ln_dve, 2)
            mm = pe.matmul(PB[3][:, :], ONES[:, :], SQA[:, :], start=True, stop=True)
            mm.then_inc(ln_pe, 1)

            norms = [0]

            def norm_sum():
                norms[0] += 1
                pe.wait_ge(nm_dve, norms[0])
                pe.matmul(PB[2][:, :], ONES[:, :], SQA[:, :], start=True, stop=True).then_inc(nm_pe, 1)

            norm_sum()
            pe.wait_ge(act_lo, 8 * (USE["mla"] + 1))
            for j in range(QL + KVL):
                job(I0 + j, 0, free["mi"], j + 1)
            job(H0 - 1, 0, free["mi"], QL + KVL + 1, m=ROPE)
            norm_sum()
            norm_sum()
            pe.wait_ge(cq_lo, 1)
            pe.wait_ge(kr_ready, 1)
            pe.wait_ge(const_pool, 2)
            pe.sem_inc(h_o, 1)
            with pe.Fori(0, HEADS) as h:
                job(H0, h * 4, h_q, h * 3 + 1, kt=QL, hi=CQH, lo=CQL)
                job(H0 + 1, h * 4, h_q, h * 3 + 1, kt=QL, m=ROPE, hi=CQH, lo=CQL)
                job(H0 + 2, h * 4, h_q, h * 3 + 2, kt=KVL, hi=CQH, lo=CQL, k0=QL)
                job(H0 + 3, h * 4, h_r, h + 1, kt=KVL, hi=CQH, lo=CQL, k0=QL, token_major=True)
                pe.wait_ge(h_q, h * 3 + 3)
                pe.wait_ge(h_r, h + 1)

                def scores(q):
                    n = (q + 1) * P
                    if q >= 2:
                        pe.wait_ge(h_exp, h * TT + q - 1)
                    pe.matmul(PB[2 + q % 2][:, 0:n], QN[:, q * P:n], KN[:, 0:n], start=True, stop=False)
                    pe.matmul(PB[2 + q % 2][:, 0:n], QR[:, q * P:n], KR[:, 0:n], start=False, stop=True)\
                        .then_inc(h_s, 1)

                def weigh(q):
                    pe.wait_ge(h_pn, h * TT + q + 1)
                    for b in range(q + 1):
                        mm = pe.transpose(PB[4 + q % 2][:, b * P:(b + 1) * P], PRB[:, q % 2, b * P:(b + 1) * P],
                                          IDENT[:, :])
                    mm.then_inc(h_pt, 1)

                def values(q):
                    pe.wait_ge(h_ptr, h * TT + q + 1)
                    for b in range(q + 1):
                        mm = pe.matmul(PB[6][:, q * P:(q + 1) * P], VM[:, b, :], PT[:, q % 2, b, :],
                                       start=(b == 0), stop=(b == q))
                    if q == TT - 1:
                        mm.then_inc(h_o, 1)

                scores(0)
                scores(1)
                weigh(0)
                scores(2)
                weigh(1)
                pe.wait_ge(h_q, h * 3 + 4)
                pe.wait_ge(h_or, h + 1)
                values(0)
                scores(3)
                weigh(2)
                values(1)
                weigh(3)
                values(2)
                values(3)
            eight_jobs(V0, free["mo"], "mla_o")
            norm_sum()

            def mlp(l, j0, use):
                norm_sum()
                pe.wait_ge(act_lo, 8 * (USE[use] + 1))
                with pe.Fori(0, NQ) as q:
                    hold((f_dn[l], q * KT + 2))
                    with pe.Fori(0, KT // 2) as i:
                        for s in range(2):
                            job(j0 + s, q * 2 * KT + i * 2, f_up[l], q * KT + i * 2 + s + 1)
                    hold((m_hidlo, q * KT + KT + l * NQ * KT))
                    with pe.Fori(0, KT // 2) as i:
                        for s in range(2):
                            job(j0 + KT + s, q * 2 * KT + i * 2, f_dn[l], q * KT + i * 2 + s + 1, hi=HH, lo=HL)
                norm_sum()

            mlp(0, F0, "mlp0")
            norm_sum()
            pe.wait_ge(act_lo, 8 * (USE["hgrn"] + 1))
            pe.wait_ge(const_pool, 3)
            NC = T // HC

            def hgrn(n, o):
                if o is not None:
                    pe.wait_ge(g_ops, o + 1)
                    for t in range(TT):
                        pe.matmul(PB[2][:, t * P:(t + 1) * P], KREL[:, t * P:(t + 1) * P],
                                  QREL[:, t * P:(t + 1) * P], start=True, stop=True)
                    for t in range(TT):
                        mm = pe.transpose(PB[3][:, t * P:(t + 1) * P], KDEC[:, t * P:(t + 1) * P], IDENT[:, :])
                    mm.then_inc(g_sc, 1)
                if n is not None:
                    job(G0, n * 4, free["g"], n * 4 + 1)
                if o is not None:
                    pe.wait_ge(g_at, o + 1)
                    pe.wait_ge(g_kt, o + 1)
                    pe.wait_ge(g_vc, o + 1)
                    for c_ in range(NC - 1):
                        t, b = divmod(c_, P // HC)
                        mm = pe.matmul(PB[2 + b][:, t * P:(t + 1) * P], KDT[b * HC:(b + 1) * HC, t, :],
                                       VG[b * HC:(b + 1) * HC, t, :], start=True, stop=True)
                    mm.then_inc(g_inc, 1)
                if n is not None:
                    job(G0 + 1, n * 4, free["g"], n * 4 + 2)
                if o is not None:
                    for t in range(TT):
                        pe.matmul(PB[6][:, t * P:(t + 1) * P], VG[:, t, :], AT[:, t, :], start=True, stop=False)
                        for b in range(P // HC):
                            c_ = t * (P // HC) + b
                            if c_:
                                pe.wait_ge(g_st, o * (NC - 1) + c_)
                                mm = pe.matmul(PB[6][:, c_ * HC:(c_ + 1) * HC], ST[:, c_, :],
                                               QDEC[:, c_ * HC:(c_ + 1) * HC], start=False,
                                               stop=(b == P // HC - 1))
                    mm.then_inc(g_out, 1)
                if n is not None:
                    job(G0 + 2, n * 4, free["g"], n * 4 + 3)
                if o is not None:
                    pe.wait_ge(g_sq, o + 1)
                    pe.matmul(PB[7][:, :], ONES[:, :], OSQ[:, :], start=True, stop=True).then_inc(g_ss, 1)
                if n is not None:
                    job(G0 + 3, n * 4, free["g"], n * 4 + 4)
                    if o is not None:
                        pe.wait_ge(g_sd, o + 1)
                    pe.wait_ge(free["g"], n * 4 + 5)
                    for t in range(TT):
                        mm = pe.transpose(PB[7][:, t * P:(t + 1) * P], VF[:, t * P:(t + 1) * P], IDENT[:, :])
                    mm.then_inc(g_vt, 1)

            hgrn(0, None)
            with pe.Fori(1, HEADS) as h:
                hgrn(h, h - 1)
            hgrn(None, HEADS - 1)
            eight_jobs(W0, free["go"], "hgrn_o", hi=HH, lo=HL)
            norm_sum()
            mlp(1, E0, "mlp1")
            pe.wait_ge(resid_ready, 4)
            for t in range(TT):
                if t:
                    pe.wait_ge(out_r, 2 * t)
                for k in range(KT):
                    mm = pe.transpose(PB[2 + k // 4][:, (k % 4) * P:(k % 4 + 1) * P], XH[:, k, t * P:(t + 1) * P],
                                      IDENT[:, :])
                mm.then_inc(out_t, 1)

        @block.scalar
        def _(act):
            act.dma_start(XTOK[:, :, :], x[0].rearrange("(t p) d -> p t d", p=P)).then_inc(x_loaded, 16)
            act.wait_ge(c_loaded, 16)
            act.activation(CSIL[:, KT:2 * KT], CSIL[:, 0:KT], ACT.Silu).then_inc(c_ready, 1)

            def high(c0, r=0, kt=8, m=P):
                act.wait_ge(w_loaded[c0 % 2], (c0 // 2 + 1) * 16 + r * 8)
                if c0 >= 2:
                    act.wait_ge(job_done, c0 - 1 + r)
                act.activation(WH[:, c0 % 2, 0:kt, 0:m], WR[:, c0 % 2, 0:kt, 0:m], ACT.Copy).then_inc(w_hi, 1)

            high(0)
            act.wait_ge(mod_ready, 1)
            for k in range(KT):
                act.activation(AH[:, k, :], XH[:, k, :], ACT.Identity, scale=MOD[:, KT + k:KT + k + 1],
                               bias=MOD[:, k:k + 1]).then_inc(act_hi, 1)
            act.sem_inc(free["a"], 2)
            for i in range(3 * JA):
                high(A0 + i + 1)
                act.wait_ge(job_done, A0 + i + 1)
                if i < JA:
                    act.activation(U[:, i, :], PB[(A0 + i) % 2][:, :], ACT.Gelu_apprx_tanh).then_inc(free["a"], 1)
                elif i < 2 * JA:
                    j = i - JA
                    act.activation(VTOK[:, :, :].rearrange("p (t g) d -> p t (g d)", t=TT)[:, :, j * P:(j + 1) * P],
                                   PB[(A0 + i) % 2][:, :].rearrange("p (t f) -> p t f", t=TT),
                                   ACT.Gelu_apprx_tanh).then_inc(free["a"], 1)
                    if j == JA - 1:
                        act.drain()
                        act.sem_inc(v_gelu, 1)
                else:
                    act.activation(SG[:, i - 2 * JA, :], PB[(A0 + i) % 2][:, :], ACT.Silu).then_inc(free["a"], 1)
            act.drain()
            act.sem_inc(u_ready, 1)
            act.wait_ge(v_ms, 1)
            act.activation(SMALL[:, 64:96], SMALL[:, 32:64], ACT.Sqrt, scale=1.0 / HB, bias=CST[:, 0:1])\
                .then_inc(v_sd, 1)
            act.sem_inc(free["b"], 2)
            with act.Fori(0, 2 * JA) as i:
                for s in range(2):
                    high(B0 + 1 + s, i * 2)
                    act.wait_ge(job_done, B0 + 1 + s + i * 2)
                    act.wait_ge(p_free, i * 2 + s + 1)
                    act.activation(PR[:, s, 1:T + 1], PB[(B0 + s) % 2][:, :], ACT.Copy).then_inc(p_copied, 1)
                    act.drain()
                    act.sem_inc(free["b"], 1)
            high(O0)
            act.wait_ge(job_done, O0)
            act.wait_ge(p_free, 4 * JA + 1)
            act.activation(PR[:, 0, 1:T + 1], PB[(O0 - 1) % 2][:, :], ACT.Copy).then_inc(p_copied, 1)
            act.wait_ge(p_mixed, 4 * JA + 1)
            act.activation(WAD[0:64, :], WAD[0:64, :], ACT.Tanh).then_inc(lr_tanh, 1)
            for j in range(JA):
                act.wait_ge(lr_done, j + 1)
                act.activation(SIG[:, j, :], PB[(6 + j) % 8][:, :], ACT.Sigmoid, bias=col("w0", j))
            act.drain()
            act.sem_inc(lr_sig, 1)
            for j in range(JA):
                act.wait_ge(lr_done, JA + j + 1)
                act.activation(ICL[:, j, :], PB[2 + j][:, :], ACT.Sigmoid, bias=col("a0", j))
            act.drain()
            act.sem_inc(lr_sig, 1)
            act.activation(RKVG[:, 3 * JA:4 * JA, :], RKVG[:, 3 * JA:4 * JA, :], ACT.Silu).then_inc(g_silu, 1)
            act.wait_ge(kk_ss, 1)
            for j in range(JA):
                act.activation(YT[:, j, :], PB[(6 + j) % 8][:, :], ACT.Sqrt, bias=CST[:, 1:2])
            act.drain()
            act.sem_inc(kk_sd, 1)
            act.wait_ge(bulk_ready, 1)
            act.sem_inc(y_read, 1)
            flat = "p h s -> p (h s)"

            def prepare(k):
                t0 = bass.ds(k * CH, CH)
                act.activation(EL[:, :, :], CS[:, :, t0], ACT.Exp, scale=-KAPPA)
                act.activation(ENL[:, :, :], CS[:, :, t0], ACT.Exp, scale=KAPPA)
                act.activation(EX[:, :, :], SIG[:, :, t0], ACT.Exp, scale=-KAPPA)
                act.drain()
                act.sem_inc(ch_exp, 1)

            def values(k):
                for half in range(2):
                    act.activation(VS[:, :, half * CH:(half + 1) * CH],
                                   RKVG[:, 2 * JA:3 * JA, bass.ds(k * CH, CH)], ACT.Copy)
                act.drain()
                act.sem_inc(ch_vs, 1)

            def step(k1, s1, k2, s2, k3, s3):
                if k1 is not None:
                    act.wait_ge(ch_ops, k1 + 1)
                    prepare(following(k1))
                    act.wait_ge(ch_t, k1 + 1)
                    for a in range(2):
                        rows_ = slice((1 - a) * CH, (2 - a) * CH)
                        act.activation(UV[s1][rows_, a::2, :],
                                       PB[6][rows_, :].rearrange("p (h d) -> p h d", d=HB)[:, a::2, :], ACT.Copy)
                    act.activation(BKT[s1][:, :, :].rearrange(flat), PB[5][:, :], ACT.Copy)
                    act.drain()
                    act.sem_inc(ch_tok, 1)
                    act.wait_ge(pw_pe, k1 * 4 + 1)
                    act.activation(X1T[:, :, :].rearrange(flat), PB[2][:, 0:JA * CH], ACT.Copy).then_inc(pw_act, 1)
                    values(following(k1))
                if k2 is not None:
                    act.wait_ge(in_pe, k2 * 4 + 2)
                    act.activation(FMT[:, :, :].rearrange(flat), PB[5][:, 0:JA * CH], ACT.Copy)
                    act.activation(TDT[:, :, :].rearrange(flat), PB[6][:, 0:JA * CH], ACT.Copy)
                    act.drain()
                    act.sem_inc(in_act, 1)
                if k1 is not None:
                    act.wait_ge(mv_done, k1 + 1)
                    act.activation(ZS[s1][:, :, :].rearrange(flat), PB[0][:, 0:JA * CH], ACT.Copy).then_inc(mv_read, 1)
                if k1 is not None:
                    act.wait_ge(pw_pe, k1 * 4 + 2)
                    act.activation(X1T[:, :, :].rearrange(flat), PB[2][:, 0:JA * CH], ACT.Copy).then_inc(pw_act, 1)
                if k2 is not None:
                    act.wait_ge(in_pe, k2 * 4 + 3)
                    act.activation(F2[:, :, :].rearrange(flat), PB[5][:, 0:JA * CH], ACT.Copy).then_inc(in_act, 1)
                if k3 is not None:
                    act.wait_ge(s_new, k3 + 2)
                    act.activation(YT[:, :, bass.ds(k3 * CH, CH)],
                                   PB[7][:, 0:JA * CH].rearrange("p (j t) -> p j t", j=JA), ACT.Copy)\
                        .then_inc(y_read, 1)
                if k1 is not None:
                    act.wait_ge(pw_pe, k1 * 4 + 3)
                    act.activation(X1T[:, :, :].rearrange(flat), PB[2][:, 0:JA * CH], ACT.Copy).then_inc(pw_act, 1)

            prepare(0)
            values(0)
            rwkv_pipeline(act, step)
            act.wait_ge(gn_pe, 2)
            for j in range(JA):
                act.activation(KKN[:, j, :], PB[2 + j][:, :], ACT.Sqrt, scale=1.0 / HB, bias=CST[:, 2:3])
            act.drain()
            act.sem_inc(gn_act, 1)
            act.wait_ge(ob_ready, 1)
            for k in range(KT):
                src = U[:, k, :] if k < JA else CS[:, k - JA, :]
                act.activation(AH[:, k, :], src, ACT.Copy).then_inc(act_hi, 1)

            act.wait_ge(act_lo, 8 * (USE["out"] + 1))
            act.dma_start(PIX[:, :], positions[0].partition_broadcast(ROPE)).then_inc(pos_loaded, 16)
            act.dma_start(FC[:, :], inv_freq).then_inc(pos_loaded, 16)
            with act.Fori(0, KT // 2) as i:
                for s in range(2):
                    high(O0 + 1 + s, i * 2)
            act.wait_ge(ln_pe, 1)
            act.activation(R2[:, :], PB[2][:, :], ACT.Copy, scale=1.0 / D).then_inc(ln_act, 1)
            act.wait_ge(ln_pe, 2)
            act.activation(R2[:, :], PB[3][:, :], ACT.Sqrt, scale=1.0 / D, bias=CST[:, 0:1]).then_inc(ln_act, 1)

            norms, squares = [0], [0]

            def squares_of(src, n, ready, first):
                for k in range(n):
                    squares[0] += 1
                    if ready is not None:
                        act.wait_ge(ready, first + k)
                    act.wait_ge(nm_sq, squares[0])
                    act.activation(TMP[(squares[0] - 1) % 2][:, :], src[:, k, :], ACT.Square).then_inc(nm_act, 1)

            def deviation(n, eps=3):
                norms[0] += 1
                act.wait_ge(nm_pe, norms[0])
                act.activation(R2[:, :], PB[2][:, :], ACT.Sqrt, scale=1.0 / n, bias=CST[:, eps:eps + 1])\
                    .then_inc(nm_dev, 1)

            def pre_norm(layer, which, resid):
                act.wait_ge(resid_ready, resid)
                for k in range(KT):
                    act.activation(AH[:, k, :], XH[:, k, :], ACT.Copy, scale=gain(layer, which, k))\
                        .then_inc(act_hi, 1)
                squares_of(XH, KT, None, 0)
                deviation(D)

            act.wait_ge(rp_ang, 1)
            act.wait_ge(rp_ang, 1)
            act.activation(SIN[:, :], ANG[:, :], ACT.Sin).then_inc(rp_sin, 1)
            act.wait_ge(rp_ang, 2)
            act.activation(COS[:, :], ANG[:, :], ACT.Sin).then_inc(rp_sin, 1)
            for k in range(KT):
                act.activation(AH[:, k, :], XH[:, k, :], ACT.Copy, scale=gain(0, 0, k)).then_inc(act_hi, 1)
            squares_of(XH, KT, None, 0)
            deviation(D)
            for j in range(QL + KVL):
                high(I0 + j + 1)
            high(H0, kt=QL)
            act.wait_ge(cq_ready, QL + KVL)
            squares_of(CQ, QL, None, 0)
            deviation(QL * P)
            squares_of(CQ[:, QL:QL + KVL, :], KVL, None, 0)
            deviation(KVL * P)
            for k in range(QL + KVL):
                act.wait_ge(cq_hi, QL + KVL)
                g = col("q_norm", k) if k < QL else col("kv_norm", k - QL)
                act.activation(CQH[:, k, :], CQ[:, k, :], ACT.Copy, scale=g)
            act.drain()
            act.sem_inc(cqh_ready, 1)
            act.sem_inc(h_q, 1)
            with act.Fori(0, HEADS) as h:
                high(H0 + 1, h * 4, kt=QL, m=ROPE)
                act.wait_ge(job_done, H0 + 1 + h * 4)
                act.wait_ge(h_o, h + 1)
                act.activation(QN[:, :], PB[H0 % 2][:, :], ACT.Copy).then_inc(h_q, 1)
                high(H0 + 2, h * 4, kt=KVL)
                high(H0 + 3, h * 4, kt=KVL)
                act.wait_ge(job_done, H0 + 3 + h * 4)
                act.activation(KN[:, :], PB[H0 % 2][:, :], ACT.Copy).then_inc(h_q, 1)
                high(H0 + 4, h * 4)
                act.wait_ge(job_done, H0 + 4 + h * 4)
                act.activation(VM[:, :, :].rearrange("p t d -> p (t d)"), PB[(H0 + 1) % 2][:, :], ACT.Copy)\
                    .then_inc(h_q, 1)

                def turned(q):
                    act.wait_ge(h_pt, h * TT + q + 1)
                    act.activation(PT[:, q % 2, 0:q + 1, :].rearrange("p b s -> p (b s)"),
                                   PB[4 + q % 2][:, 0:(q + 1) * P], ACT.Copy).then_inc(h_ptr, 1)

                for q in range(TT):
                    n = (q + 1) * P
                    act.wait_ge(h_mx, h * TT + q + 1)
                    if q >= 2:
                        act.wait_ge(h_pt, h * TT + q - 1)
                    act.activation(PRB[:, q % 2, 0:n], PB[2 + q % 2][:, 0:n], ACT.Exp, scale=SCALE,
                                   bias=SMALL[:, 8 + q:9 + q], accum_out=SMALL[:, 16 + q:17 + q])
                    act.drain()
                    act.sem_inc(h_exp, 1)
                    if q >= 1:
                        turned(q - 1)
                turned(TT - 1)
                act.wait_ge(h_o, h + 2)
                act.activation(AH[:, bass.ds(h, 1), :], PB[6][:, :].rearrange("p (a t) -> p a t", a=1), ACT.Copy)\
                    .then_inc(act_hi, 1)

            def mixer_out(c0, fr_count):
                for k in range(KT):
                    high(c0 + 1 + k)
                    squares[0] += 1
                    act.wait_ge(mx_out, fr_count + k + 1)
                    act.wait_ge(nm_sq, squares[0])
                    act.activation(TMP[(squares[0] - 1) % 2][:, :], M[:, k, :], ACT.Square).then_inc(nm_act, 1)
                deviation(D)

            mixer_out(V0, 0)

            def mlp(l, j0, resid):
                pre_norm(l, 2, resid)

                act.sem_inc(f_up[l], 2)

                def up(q):
                    with act.Fori(0, KT // 2) as i:
                        for s in range(2):
                            high(j0 + 1 + s, q * 2 * KT + i * 2)
                            act.wait_ge(job_done, j0 + 1 + s + q * 2 * KT + i * 2)
                            act.wait_ge(m_hid, l * NQ * KT + q * KT + i * 2 + s + 1)
                            act.activation(TMP[2 + s][:, :], PB[(j0 + s) % 2][:, :], ACT.Relu)
                            act.drain()
                            act.sem_inc(f_up[l], 1)
                            act.sem_inc(m_relu, 1)
                            act.activation(HH[:, bass.ds(i * 2 + s, 1), :],
                                           TMP[2 + s][:, :].rearrange("p (a t) -> p a t", a=1), ACT.Square)\
                                .then_inc(m_relu, 1)

                with act.Fori(0, NQ - 1) as q:
                    up(q)
                    with act.Fori(0, KT // 2) as i:
                        for s in range(2):
                            high(j0 + KT + 1 + s, q * 2 * KT + i * 2)
                up(NQ - 1)
                for k in range(KT):
                    c_next = j0 + 2 * KT * NQ - KT + k + 1
                    if c_next < NJ:
                        high(c_next)
                    squares[0] += 1
                    act.wait_ge(mx_out, KT * (1 + 2 * l) + k + 1)
                    act.wait_ge(nm_sq, squares[0])
                    act.activation(TMP[(squares[0] - 1) % 2][:, :], M[:, k, :], ACT.Square).then_inc(nm_act, 1)
                deviation(D)

            mlp(0, F0, 1)
            act.wait_ge(lb_diff, 1)
            act.activation(LBS[:, HEADS:3 * HEADS], LBS[:, HEADS:3 * HEADS], ACT.Exp).then_inc(lb_exp, 1)
            pre_norm(1, 0, 2)

            def hgrn(n, o):
                if n is not None:
                    high(G0 + 1, n * 4)
                if o is not None:
                    act.wait_ge(g_sc, o + 1)
                    act.activation(KDT[:, :, :].rearrange("p t d -> p (t d)"), PB[3][:, :], ACT.Copy)\
                        .then_inc(g_kt, 1)
                if n is not None:
                    act.wait_ge(free["g"], n * 4 + 3)
                    act.activation(FG[:, :], TG[2][:, :], ACT.Sigmoid).then_inc(g_silu3, 1)
                    high(G0 + 2, n * 4)
                    act.wait_ge(g_f, n + 1)
                    act.activation(TG[2][:, :], FG[:, :], ACT.Ln).then_inc(g_ln, 1)
                    high(G0 + 3, n * 4)
                    act.wait_ge(free["g"], n * 4 + 4)
                    act.activation(QG[:, :], TG[1][:, :], ACT.Silu).then_inc(g_silu3, 1)
                    act.wait_ge(g_diff, n + 1)
                    act.activation(QREL[:, :], LREL[:, :], ACT.Exp)
                    act.activation(KREL[:, :], LREL[:, :], ACT.Exp, scale=-1.0)
                    act.activation(KDEC[:, :], TG[0][:, :], ACT.Exp)
                    if o is not None:
                        act.wait_ge(g_out, o + 1)
                    act.activation(QDEC[:, :], BG[:, :], ACT.Exp)
                    act.activation(EBL[:, :], BG[:, :].rearrange("p (c t) -> p c t", t=HC)[:, :, HC - 1], ACT.Exp)
                    act.drain()
                    act.sem_inc(g_exp, 1)
                if o is not None:
                    act.wait_ge(g_out, o + 1)
                    act.activation(OG[:, :], PB[6][:, :], ACT.Copy)
                    act.activation(OSQ[:, :], PB[6][:, :], ACT.Square)
                    act.drain()
                    act.sem_inc(g_sq, 1)
                if n is not None:
                    high(G0 + 4, n * 4)
                if o is not None:
                    act.wait_ge(g_ss, o + 1)
                    act.activation(OSD[:, :], PB[7][:, :], ACT.Sqrt, scale=1.0 / P, bias=CST[:, 3:4])\
                        .then_inc(g_sd, 1)
                if n is not None:
                    act.wait_ge(free["g"], n * 4 + 6)
                    if o is not None:
                        act.wait_ge(g_fin, o + 1)
                    act.activation(GG[:, :], TG[3][:, :], ACT.Silu).then_inc(g_silu3, 1)
                if o is not None:
                    act.wait_ge(g_fin, o + 1)
                    act.activation(HH[:, bass.ds(o, 1), :], OG[:, :].rearrange("p (a t) -> p a t", a=1), ACT.Copy)\
                        .then_inc(act_hi, 1)
                if n is not None:
                    act.wait_ge(g_vt, n + 1)
                    act.activation(VG[:, :, :].rearrange("p t d -> p (t d)"), PB[7][:, :], ACT.Copy)\
                        .then_inc(g_vc, 1)

            hgrn(0, None)
            with act.Fori(1, HEADS) as h:
                hgrn(h, h - 1)
            hgrn(None, HEADS - 1)
            mixer_out(W0, 2 * KT)
            mlp(1, E0, 3)

        @block.vector
        def _(dve):
            def bc(ap, n):
                return ap.unsqueeze(2).broadcast_to([ap.shape[0], ap.shape[1], n])

            def bc1(ap, n):
                return ap.unsqueeze(1).broadcast_to([ap.shape[0], n, ap.shape[1]])

            def tt(out_, a, b, op):
                return dve.tensor_tensor(out_, a, b, op)

            def stt(out_, a, sc, b, op0, op1):
                return dve.scalar_tensor_tensor(out=out_, in0=a, scalar=sc, in1=b, op0=op0, op1=op1)

            def after(signal, n=1):
                dve.drain()
                dve.sem_inc(signal, n)

            MUL, ADD, SUB = ALU.mult, ALU.add, ALU.subtract
            dve.wait_ge(par_turned, 1)
            dve.tensor_copy(COL[:, 0:n_rows], PB[7][:, 0:n_rows]).then_inc(colz, 1)
            for k in range(KT):
                dve.wait_ge(x_turned, k + 1)
                dve.tensor_copy(XH[:, k, :], PB[k][:, :]).then_inc(x_read, 1)
            dve.wait_ge(ada_done, 4)
            tt(MOD[:, 0:2 * KT], PB[7][:, 0:2 * KT], col("b_ada", 0, 2 * KT), ADD)
            dve.drain()
            dve.tensor_scalar(MOD[:, KT:2 * KT], MOD[:, KT:2 * KT], 1.0, None, ADD).then_inc(mod_ready, 1)
            dve.drain()
            for k in range(KT):
                t = TMP[4 + k % 2]
                dve.tensor_scalar(t[:, :], XH[:, k, :], MOD[:, KT + k:KT + k + 1], MOD[:, k:k + 1], MUL, ADD)
                dve.drain()
                dve.wait_ge(act_hi, k + 1)
                tt(AL[:, k, :], t[:, :], AH[:, k, :].bitcast(F32), SUB).then_inc(act_lo, 1)
            dve.drain()
            dve.wait_ge(ada_done, 6)
            tt(MOD[:, 2 * KT:3 * KT], PB[6][:, 2 * KT:3 * KT], col("b_ada", 2 * KT, KT), ADD)
            dve.tensor_scalar(XH[:, :, :], XH[:, :, :], ALPHA, None, MUL)
            dve.wait_ge(v_gelu, 1)
            dve.tensor_reduce(SMALL[:, 0:32], VTOK[:, :, :], AX, ADD)
            dve.drain()
            dve.tensor_scalar(SMALL[:, 0:32], SMALL[:, 0:32], 1.0 / HB, None, MUL)
            dve.drain()
            tt(VC[:, :, :], VTOK[:, :, :], bc(SMALL[:, 0:32], HB), SUB)
            dve.drain()
            tt(VSQ[:, :, :], VC[:, :, :], VC[:, :, :], MUL)
            dve.drain()
            dve.tensor_reduce(SMALL[:, 32:64], VSQ[:, :, :], AX, ADD).then_inc(v_ms, 1)
            dve.wait_ge(v_sd, 1)
            dve.reciprocal(SMALL[:, 64:96], SMALL[:, 64:96])
            dve.drain()
            tt(VC[:, :, :], VC[:, :, :], bc(SMALL[:, 64:96], HB), MUL)
            dve.drain()
            dve.wait_ge(bc_loaded, 16 * 7)
            vt = VC[:, :, :].rearrange("p (t g) d -> p t (g d)", t=TT)
            tt(vt, vt, bc1(LVG[:, :], TT), MUL)
            dve.drain()
            tt(vt, vt, bc1(LVB[:, :], TT), ADD).then_inc(v_ready, 1)
            dve.wait_ge(wsp_t, 1)
            for a in range(2):
                dve.tensor_copy(WSPT[:, 4 * a:4 * a + 4, :].rearrange("p g t -> p (g t)"), PB[2 + a][:, :])
            after(wsp_r)
            dve.wait_ge(x_read, KT)
            dve.memset(PR[:, :, 0:1], 0.0)
            after(p_free, 2)

            def mix(s, dst, mu):
                tt(TMP[4 + s][:, :], PR[:, s, 0:T], PR[:, s, 1:T + 1], SUB)
                dve.drain()
                stt(dst, TMP[4 + s][:, :], mu, PR[:, s, 1:T + 1], MUL, ADD)
                dve.drain()
                dve.sem_inc(p_free, 1)
                dve.sem_inc(p_mixed, 1)

            for i in range(4 * JA):
                dve.wait_ge(p_copied, i + 1)
                mix(i % 2, RKVG[:, i, :], col("mu", i))
            dve.wait_ge(p_copied, 4 * JA + 1)
            mix(0, WAD[:, :], col("mu", 4 * JA))
            dve.wait_ge(u_ready, 1)
            for j in range(JA):
                dve.wait_ge(sp_done, j + 1)
                t = TMP[4 + j % 2]
                tt(t[:, :].rearrange("p (c t) -> p c t", c=TT), PB[2 + j][:, :].rearrange("p (c t) -> p c t", c=TT),
                   bc1(BSP[:, j, :], TT), ADD)
                tt(U[:, j, :], U[:, j, :], SG[:, j, :], MUL)
                dve.drain()
                tt(U[:, j, :], U[:, j, :], t[:, :], MUL)
                dve.drain()
            dve.sem_inc(oa_ready, 1)
            R_, K_, V_, G_ = (RKVG[:, n * JA:(n + 1) * JA, :] for n in range(4))
            for j in range(JA):
                dve.tensor_scalar(KKN[:, j, :], K_[:, j, :], col("k_k", j), None, MUL)
            dve.drain()
            tt(SQB[:, :, :], KKN[:, :, :], KKN[:, :, :], MUL).then_inc(kk_sq, 1)
            dve.wait_ge(lr_sig, 1)
            for j in range(JA):
                dve.tensor_tensor_scan(CS[:, j, :], RSET[:, :], SIG[:, j, :], 0.0, MUL, ADD)
            dve.drain()
            tt(SIG[:, :, :], CS[:, :, :], SIG[:, :, :], SUB)
            dve.wait_ge(lr_sig, 2)
            for j in range(JA):
                t = TMP[4 + j % 2]
                dve.tensor_scalar(t[:, :], ICL[:, j, :], 1.0, col("k_a", j), SUB, MUL)
                dve.drain()
                stt(K_[:, j, :], t[:, :], 1.0, K_[:, j, :], ADD, MUL)
            dve.drain()
            dve.wait_ge(kk_sd, 1)
            dve.reciprocal(YT[:, :, :], YT[:, :, :])
            for j in range(JA):
                stt(SQB[:, j, :], R_[:, j, :], col("r_k", j), K_[:, j, :], MUL, MUL)
            after(rk_ready)
            tt(KKN[:, :, :], KKN[:, :, :], YT[:, :, :], MUL)
            dve.drain()
            tt(ICL[:, :, :], KKN[:, :, :], ICL[:, :, :], MUL)
            dve.wait_ge(rk_done, 1)
            for j in range(JA):
                tt(BON[:, j, :], PB[2 + j][:, :], V_[:, j, :], MUL)
            dve.memset(S[:, :, :], 0.0)
            tt(ID2[:, :], IDENT[:, 0:CH], IDENT[:, CH:P], ADD)
            dve.wait_ge(g_silu, 1)
            dve.wait_ge(const_pool, 1)
            dve.drain()
            dve.sem_inc(bulk_ready, 1)
            dve.sem_inc(s_new, 1)
            flat = "p h s -> p (h s)"

            def operands(k, slot):
                t0 = bass.ds(k * CH, CH)
                stt(AR[slot][:, :, 0:CH], KKN[:, :, t0], -1.0, EX[:, :, :], MUL, MUL)
                tt(AR[slot][:, :, CH:P], R_[:, :, t0], EL[:, :, :], MUL)
                for p in (0, CH):
                    tt(BK[p:p + CH, :, p:p + CH], ICL[p:p + CH, :, t0], ENL[p:p + CH, :, :], MUL)
                    tt(BK[p:p + CH, :, CH - p:P - p], K_[p:p + CH, :, t0], ENL[p:p + CH, :, :], MUL)

            def copied(dst, bank, signal):
                dve.tensor_copy(dst[:, :, :].rearrange(flat), PB[bank][:, 0:JA * CH]).then_inc(signal, 1)

            def added(dst, bank, plus, signal):
                tt(dst[:, :, :].rearrange(flat), PB[bank][:, 0:JA * CH], plus[:, :, :].rearrange(flat), ADD)\
                    .then_inc(signal, 1)

            def step(k1, s1, k2, s2, k3, s3):
                if k2 is not None:
                    dve.wait_ge(pw_pe, k2 * 4 + 4)
                    added(TDF, 0, TD, pw_dve)
                    dve.drain()
                if k1 is not None:
                    dve.wait_ge(ch_g, k1 + 1)
                    for a in range(2):
                        g = PB[1 + a][:, :].rearrange("p (h s) -> p h s", s=P)
                        tt(GA[:, a::2, :], g[:, :, 0:CH], bc1(MSKG[:, 0:CH], JA), MUL)
                    tt(ND[:, :, :], PB[3][:, 0:JA * CH].rearrange("p (h s) -> p h s", s=CH), bc1(MSKSD[:, :], JA),
                       MUL)
                    dve.drain()
                    for a in range(2):
                        half = slice(a * CH, (a + 1) * CH)
                        tt(NDT[half, :, :], GA[half, a::2, :], bc1(MSKD[half, :], JA), MUL)
                    tt(TD[:, :, :], ND[:, :, :], bc1(ID2[:, :], JA), ADD)
                    for a in range(2):
                        g = PB[1 + a][:, :].rearrange("p (h s) -> p h s", s=P)
                        tt(GR[s1][:, a::2, :], g[:, :, CH:P], bc1(MSKG[:, CH:P], JA), MUL)
                    after(ch_nd)
                if k2 is not None:
                    dve.wait_ge(in_pe, k2 * 4 + 1)
                    copied(FM, 0, in_dve)
                if k3 is not None:
                    dve.wait_ge(mv_read, k3 + 1)
                    dve.wait_ge(z_done, k3 + 1)
                    added(ZS[s3], 4, ZS[s3], z_read)
                if k1 is not None:
                    dve.wait_ge(pw_pe, k1 * 4 + 1)
                    copied(X1, 1, pw_dve)
                if k3 is not None:
                    dve.wait_ge(u_done, k3 + 1)
                    for a in range(2):
                        half = slice(a * CH, (a + 1) * CH)
                        dve.tensor_copy(UV[s3][half, a::2, :],
                                        PB[4][half, 0:JA * CH].rearrange("p (j d) -> p j d", d=HB))
                    after(u_read)
                if k1 is not None:
                    dve.wait_ge(ch_exp, following(k1, 0) + 1)
                    operands(following(k1), (s1 + 1) % 3)
                if k1 is not None:
                    dve.wait_ge(pw_pe, k1 * 4 + 2)
                    dve.tensor_copy(X1[:, :, :].rearrange(flat), PB[1][:, 0:JA * CH])
                    added(TD, 3, TD, pw_dve)
                    for a in range(2):
                        half = slice(a * CH, (a + 1) * CH)
                        tt(NOT[half, :, :], GA[half, a::2, :], NDT[half, :, :], SUB)
                if k2 is not None:
                    dve.wait_ge(in_pe, k2 * 4 + 3)
                    added(Y1, 0, TDT, in_dve)
                if k3 is not None:
                    dve.wait_ge(y_done, k3 + 1)
                    sv = S[:, :, :].rearrange("p j i -> p (j i)")
                    tt(sv, PB[7][:, JA * CH:], sv, ADD)
                    dve.drain()
                    tt(S[:, :, :], S[:, :, :], bc(FS[:, s3, :], CH), MUL)
                    after(s_new)
                if k1 is not None:
                    dve.tensor_copy(FS[:, (s1 + 1) % 3, :], EL[:, :, CH - 1])
                    after(ch_ops)
                if k1 is not None:
                    dve.wait_ge(pw_pe, k1 * 4 + 3)
                    added(TD, 3, TD, pw_dve)
                if k2 is not None:
                    dve.drain()
                    dve.wait_ge(in_pe, k2 * 4 + 4)
                    added(TTM, 5, Y1, in_dve)

            dve.wait_ge(ch_exp, 1)
            operands(0, 0)
            dve.tensor_copy(FS[:, 0, :], EL[:, :, CH - 1])
            after(ch_ops)
            rwkv_pipeline(dve, step)
            dve.wait_ge(gn_pe, 1)
            for j in range(JA):
                stt(YT[:, j, :], PB[2 + j][:, :], -1.0 / HB, YT[:, j, :], MUL, ADD)
            dve.drain()
            tt(SQB[:, :, :], YT[:, :, :], YT[:, :, :], MUL)
            after(gn_dve)
            dve.wait_ge(gn_act, 1)
            dve.reciprocal(KKN[:, :, :], KKN[:, :, :])
            dve.drain()
            tt(YT[:, :, :], YT[:, :, :], KKN[:, :, :], MUL)
            dve.drain()
            for j in range(JA):
                dve.tensor_scalar(YT[:, j, :], YT[:, j, :], col("gn_g", j), col("gn_b", j), MUL, ADD)
            dve.drain()
            tt(YT[:, :, :], YT[:, :, :], BON[:, :, :], ADD)
            dve.drain()
            tt(CS[:, :, :], YT[:, :, :], G_, MUL)
            after(ob_ready)
            for k in range(KT):
                src = U[:, k, :] if k < JA else CS[:, k - JA, :]
                dve.wait_ge(act_hi, 8 * USE["out"] + k + 1)
                tt(AL[:, k, :], src, AH[:, k, :].bitcast(F32), SUB).then_inc(act_lo, 1)
            dve.sem_inc(free["o"], 2)
            for k in range(KT):
                dve.wait_ge(job_done, O0 + k + 1)
                stt(M[:, k, :], PB[(O0 + k) % 2][:, :], MOD[:, 2 * KT + k:2 * KT + k + 1], XH[:, k, :], MUL, ADD)\
                    .then_inc(free["o"], 1)
                dve.drain()
                if k == 0:
                    dve.tensor_copy(SQA[:, :], M[:, k, :])
                else:
                    tt(SQA[:, :], SQA[:, :], M[:, k, :], ADD)
            after(ln_dve)
            dve.wait_ge(ln_act, 1)
            for k in range(KT):
                tt(M[:, k, :], M[:, k, :], R2[:, :], SUB)
                dve.drain()
                if k == 0:
                    tt(SQA[:, :], M[:, k, :], M[:, k, :], MUL)
                else:
                    tt(TMP[4][:, :], M[:, k, :], M[:, k, :], MUL)
                    dve.drain()
                    tt(SQA[:, :], SQA[:, :], TMP[4][:, :], ADD)
            after(ln_dve)
            dve.wait_ge(ln_act, 2)
            dve.reciprocal(R1[:, :], R2[:, :])
            dve.drain()
            for k in range(KT):
                tt(M[:, k, :], M[:, k, :], R1[:, :], MUL)
            dve.drain()
            for k in range(KT):
                dve.tensor_scalar(XH[:, k, :], M[:, k, :], col("ln_g", k), col("ln_b", k), MUL, ADD)
            after(x1_ready)

            squares, devs, his = [0], [0], [8 * USE["mla"]]

            def add_squares(n):
                for k in range(n):
                    squares[0] += 1
                    dve.wait_ge(nm_act, squares[0])
                    t = TMP[(squares[0] - 1) % 2]
                    if k == 0:
                        dve.tensor_copy(SQA[:, :], t[:, :]).then_inc(nm_sq, 1)
                    else:
                        tt(SQA[:, :], SQA[:, :], t[:, :], ADD).then_inc(nm_sq, 1)
                    dve.drain()
                dve.sem_inc(nm_dve, 1)

            def inverse(dst):
                devs[0] += 1
                dve.wait_ge(nm_dev, devs[0])
                dve.reciprocal(dst[:, :], R2[:, :])
                dve.drain()

            def low_of_gained(layer, which):
                for k in range(KT):
                    his[0] += 1
                    dve.wait_ge(act_hi, his[0])
                    stt(AL[:, k, :], XH[:, k, :], gain(layer, which, k), AH[:, k, :].bitcast(F32), MUL, SUB)\
                        .then_inc(act_lo, 1)

            def add_to_residual(layer, which):
                inverse(R2)
                for k in range(KT):
                    tt(M[:, k, :], M[:, k, :], R2[:, :], MUL)
                dve.drain()
                for k in range(KT):
                    stt(XH[:, k, :], M[:, k, :], gain(layer, which, k), XH[:, k, :], MUL, ADD)
                after(resid_ready)

            dve.wait_ge(pos_loaded, 32)
            dve.tensor_copy(ANG[:, :], PIX[:, :])
            dve.drain()
            dve.tensor_scalar(ANG[:, :], ANG[:, :], FC[:, 0:1], None, MUL)
            dve.drain()
            dve.tensor_scalar(ANGK[:, :], ANG[:, :], float(1 / (2 * np.pi)), None, MUL)
            dve.drain()
            dve.tensor_copy(SIN[:, :], ANGK[:, :])
            dve.drain()
            hi1 = 6.28125
            hi2 = float(np.float32(2 * np.pi - hi1))
            hi2 = float(np.frombuffer((np.frombuffer(np.float32(hi2).tobytes(), np.uint32) & np.uint32(0xFFFFF000))
                                      .tobytes(), np.float32)[0])
            for part in (hi1, hi2, float(2 * np.pi - hi1 - hi2)):
                stt(ANG[:, :], SIN[:, :], -part, ANG[:, :], MUL, ADD)
                dve.drain()
            dve.tensor_scalar(ANG[:, :], ANG[:, :], -3.1415925, 3.1415925, ALU.max, ALU.min)
            after(rp_ang)
            dve.wait_ge(rp_sin, 1)
            dve.tensor_scalar(ANG[:, :], ANG[:, :], float(np.pi / 2), None, ADD)
            dve.drain()
            dve.tensor_scalar(COS[:, :], ANG[:, :], float(np.pi), float(-2 * np.pi), ALU.is_gt, MUL)
            dve.drain()
            tt(ANG[:, :], ANG[:, :], COS[:, :], ADD)
            dve.drain()
            dve.tensor_scalar(ANG[:, :], ANG[:, :], -3.1415925, 3.1415925, ALU.max, ALU.min)
            after(rp_ang)
            dve.tensor_scalar(SIN[ROPE // 2:ROPE, :], SIN[ROPE // 2:ROPE, :], -1.0, None, MUL)
            dve.wait_ge(rp_sin, 2)

            def rope(dst, src, a, b):
                hf = ROPE // 2
                tt(a[0:ROPE, :], src, COS[:, :], MUL)
                tt(b[0:hf, :], src[hf:ROPE, :], SIN[hf:ROPE, :], MUL)
                tt(b[hf:ROPE, :], src[0:hf, :], SIN[0:hf, :], MUL)
                dve.drain()
                return tt(dst, a[0:ROPE, :], b[0:ROPE, :], ADD)

            dve.sem_inc(nm_sq, 2)
            low_of_gained(0, 0)
            add_squares(KT)
            inverse(R1)
            dve.sem_inc(free["mi"], 2)
            for k in range(QL + KVL):
                dve.wait_ge(job_done, I0 + k + 1)
                tt(CQ[:, k, :], PB[(I0 + k) % 2][:, :], R1[:, :], MUL)
                dve.drain()
                dve.sem_inc(free["mi"], 1)
                dve.sem_inc(cq_ready, 1)
            dve.wait_ge(job_done, H0)
            tt(TMP[2][0:ROPE, :], PB[(H0 - 1) % 2][0:ROPE, :], R1[0:ROPE, :], MUL)
            dve.drain()
            rope(KR[:, :], TMP[2][0:ROPE, :], TMP[4], TMP[5])
            after(kr_ready)
            add_squares(QL)
            inverse(R1)
            add_squares(KVL)
            for k in range(QL):
                tt(CQ[:, k, :], CQ[:, k, :], R1[:, :], MUL)
            dve.drain()
            inverse(R1)
            for k in range(KVL):
                tt(CQ[:, QL + k, :], CQ[:, QL + k, :], R1[:, :], MUL)
            after(cq_hi, QL + KVL)
            dve.wait_ge(cqh_ready, 1)
            for k in range(QL + KVL):
                g = col("q_norm", k) if k < QL else col("kv_norm", k - QL)
                stt(CQL[:, k, :], CQ[:, k, :], g, CQH[:, k, :].bitcast(F32), MUL, SUB)
            after(cq_lo)
            dve.sem_inc(h_or, 1)
            dve.wait_ge(const_pool, 2)
            with dve.Fori(0, HEADS) as h:
                dve.wait_ge(job_done, h * 4 + H0 + 2)
                rope(QR[:, :], PB[(H0 + 1) % 2][0:ROPE, :], TMP[4], TMP[5])
                after(h_r)

                def row_max(q):
                    n = (q + 1) * P
                    ps = PB[2 + q % 2]
                    dve.wait_ge(h_s, h * TT + q + 1)
                    tt(ps[:, q * P:n], ps[:, q * P:n], CMASK[:, :], ADD)
                    dve.drain()
                    dve.tensor_reduce(SMALL[:, q:q + 1], ps[:, 0:n], AX, ALU.max)
                    dve.drain()
                    dve.tensor_scalar(SMALL[:, 8 + q:9 + q], SMALL[:, q:q + 1], -SCALE, None, MUL).then_inc(h_mx, 1)

                def normalise(q):
                    n = (q + 1) * P
                    dve.wait_ge(h_exp, h * TT + q + 1)
                    dve.reciprocal(SMALL[:, 24 + q:25 + q], SMALL[:, 16 + q:17 + q])
                    dve.drain()
                    dve.tensor_scalar(PRB[:, q % 2, 0:n], PRB[:, q % 2, 0:n], SMALL[:, 24 + q:25 + q], None, MUL)\
                        .then_inc(h_pn, 1)

                for q in range(TT):
                    row_max(q)
                    if q:
                        normalise(q - 1)
                normalise(TT - 1)
                dve.wait_ge(act_hi, h + 8 * USE["mla_o"] + 1)
                tt(AL[:, bass.ds(h, 1), :], PB[6][:, :].rearrange("p (a t) -> p a t", a=1),
                   AH[:, bass.ds(h, 1), :].bitcast(F32), SUB)
                dve.drain()
                dve.sem_inc(act_lo, 1)
                dve.sem_inc(h_or, 1)
            his[0] += 8

            def read_mixer(c0, fr):
                dve.sem_inc(fr, 2)
                for k in range(KT):
                    dve.wait_ge(job_done, c0 + k + 1)
                    dve.tensor_copy(M[:, k, :], PB[(c0 + k) % 2][:, :])
                    dve.drain()
                    dve.sem_inc(fr, 1)
                    dve.sem_inc(mx_out, 1)
                    if k:
                        one_square(k - 1)
                one_square(KT - 1)
                dve.sem_inc(nm_dve, 1)

            def one_square(k):
                squares[0] += 1
                dve.wait_ge(nm_act, squares[0])
                t = TMP[(squares[0] - 1) % 2]
                if k == 0:
                    dve.tensor_copy(SQA[:, :], t[:, :]).then_inc(nm_sq, 1)
                else:
                    tt(SQA[:, :], SQA[:, :], t[:, :], ADD).then_inc(nm_sq, 1)
                dve.drain()

            read_mixer(V0, free["mo"])
            add_to_residual(0, 1)

            def mlp(l, j0):
                if l == 0:
                    dve.sem_inc(m_hid, 2)
                dve.sem_inc(f_dn[l], 2)
                low_of_gained(l, 2)
                add_squares(KT)
                inverse(R1)
                tt(R1[:, :], R1[:, :], R1[:, :], MUL)
                dve.drain()

                def up(q):
                    with dve.Fori(0, KT // 2) as i:
                        for s in range(2):
                            n = l * NQ * KT + q * KT + i * 2 + s
                            dve.wait_ge(m_relu, n * 2 + 1)
                            tt(TMP[4 + s][:, :], TMP[2 + s][:, :], TMP[2 + s][:, :], MUL)
                            after(m_hid)
                            dve.wait_ge(m_relu, n * 2 + 2)
                            tt(HL[:, bass.ds(i * 2 + s, 1), :], TMP[4 + s][:, :].rearrange("p (a t) -> p a t", a=1),
                               HH[:, bass.ds(i * 2 + s, 1), :].bitcast(F32), SUB).then_inc(m_hidlo, 1)

                def down(q, first):
                    with dve.Fori(0, KT // 2) as i:
                        for s in range(2):
                            dve.wait_ge(job_done, q * 2 * KT + i * 2 + j0 + KT + s + 1)
                            m = M[:, bass.ds(i * 2 + s, 1), :]
                            ps = PB[(j0 + s) % 2][:, :].rearrange("p (a t) -> p a t", a=1)
                            if first:
                                dve.tensor_copy(m, ps).then_inc(f_dn[l], 1)
                            else:
                                tt(m, ps, m, ADD).then_inc(f_dn[l], 1)
                            dve.drain()

                up(0)
                down(0, True)
                with dve.Fori(1, NQ - 1) as q:
                    up(q)
                    down(q, False)
                up(NQ - 1)
                for k in range(KT):
                    dve.wait_ge(job_done, j0 + 2 * KT * NQ - KT + k + 1)
                    tt(M[:, k, :], PB[(j0 + k) % 2][:, :], M[:, k, :], ADD).then_inc(f_dn[l], 1)
                    dve.drain()
                    tt(M[:, k, :], M[:, k, :], R1[:, :], MUL)
                    after(mx_out)
                    if k:
                        one_square(k - 1)
                one_square(KT - 1)
                dve.sem_inc(nm_dve, 1)
                add_to_residual(l, 3)

            mlp(0, F0)
            n = HEADS
            l0, l1 = col("lb", 0, n), col("lb", n, n)
            tt(LBS[:, 0:n], l0, l1, ALU.max)
            dve.drain()
            tt(LBS[:, n:2 * n], l0, LBS[:, 0:n], SUB)
            tt(LBS[:, 2 * n:3 * n], l1, LBS[:, 0:n], SUB)
            after(lb_diff)
            low_of_gained(1, 0)
            add_squares(KT)
            inverse(R1)
            dve.wait_ge(lb_exp, 1)
            tt(LBS[:, 0:n], LBS[:, n:2 * n], LBS[:, 2 * n:3 * n], ADD)
            dve.drain()
            dve.reciprocal(LBS[:, 0:n], LBS[:, 0:n])
            dve.drain()
            tt(LBS[:, n:2 * n], LBS[:, n:2 * n], LBS[:, 0:n], MUL)
            tt(LBS[:, 2 * n:3 * n], LBS[:, 2 * n:3 * n], LBS[:, 0:n], MUL)
            dve.drain()
            tt(LBS[:, 2 * n:3 * n], LBS[:, n:2 * n], LBS[:, 2 * n:3 * n], ADD)
            dve.drain()
            tt(LBS[:, 0:n], LBS[:, 2 * n:3 * n], LBS[:, n:2 * n], SUB)
            dve.drain()
            dve.tensor_scalar(LBS[:, n:2 * n], LBS[:, 0:n], -1.0, 1.0, MUL, ADD)
            dve.drain()
            dve.wait_ge(const_pool, 3)
            dve.sem_inc(free["g"], 2)

            def hgrn(n, o):
                def scaled(j, dst):
                    dve.wait_ge(job_done, n * 4 + G0 + j + 1)
                    tt(dst[:, :], PB[(G0 + j) % 2][:, :], R1[:, :], MUL).then_inc(free["g"], 1)

                if o is not None:
                    dve.wait_ge(const_pool, 3)
                    dve.wait_ge(g_sc, o + 1)
                    dve.copy_predicated(AT[:, :, :].rearrange("p t s -> p (t s)"),
                                        HMSK[:, :, :].rearrange("p t s -> p (t s)"), PB[2][:, :]).then_inc(g_at, 1)
                if n is not None:
                    scaled(0, TG[2])
                    dve.tensor_copy(LBH[:, 0:1], LBS[:, bass.ds(n, 1)])
                    dve.tensor_copy(LBH[:, 1:2], LBS[:, bass.ds(n + HEADS, 1)])
                    dve.drain()
                    dve.wait_ge(g_silu3, n * 3 + 1)
                    dve.tensor_scalar(FG[:, :], FG[:, :], LBH[:, 1:2], LBH[:, 0:1], MUL, ADD)
                    after(g_f)
                    dve.tensor_scalar(KG[:, :], FG[:, :], -1.0, 1.0, MUL, ADD)
                if o is not None:
                    dve.wait_ge(g_inc, o + 1)
                    for k in range(T // HC - 1):
                        ps = PB[2 + k % (P // HC)][:, k // (P // HC) * P:(k // (P // HC) + 1) * P]
                        if k == 0:
                            dve.tensor_copy(ST[:, 1, :], ps).then_inc(g_st, 1)
                        else:
                            stt(ST[:, k + 1, :], ST[:, k, :], EBL[:, k:k + 1], ps, MUL, ADD).then_inc(g_st, 1)
                        dve.drain()
                if n is not None:
                    dve.wait_ge(g_ln, n + 1)
                    dve.tensor_tensor_scan(BG[:, :], HRST[:, :], TG[2][:, :], 0.0, MUL, ADD)
                    scaled(1, TG[1])
                    dve.drain()
                    b3 = BG[:, :].rearrange("p (c t) -> p c t", t=HC)
                    tt(LREL[:, :].rearrange("p (c t) -> p c t", t=HC), b3, bc(b3[:, :, HC // 2], HC), SUB)
                    tt(TG[0][:, :].rearrange("p (c t) -> p c t", t=HC), bc(b3[:, :, HC - 1], HC), b3, SUB)
                    after(g_diff)
                    dve.wait_ge(g_exp, n + 1)
                    for a, b in ((QREL, QG), (KREL, KG), (QDEC, QG), (KDEC, KG)):
                        tt(a[:, :], a[:, :], b[:, :], MUL)
                    after(g_ops)
                    scaled(2, VF)
                if o is not None:
                    dve.wait_ge(g_sd, o + 1)
                    dve.reciprocal(OSD[:, :], OSD[:, :])
                    dve.drain()
                    stt(OG[:, :], OG[:, :], col("o_norm"), OSD[:, :], MUL, MUL)
                    dve.drain()
                    dve.wait_ge(g_silu3, o * 3 + 3)
                    tt(OG[:, :], OG[:, :], GG[:, :], MUL)
                    after(g_fin)
                if n is not None:
                    scaled(3, TG[3])
                if o is not None:
                    dve.wait_ge(act_hi, o + 8 * USE["hgrn_o"] + 1)
                    tt(HL[:, bass.ds(o, 1), :], OG[:, :].rearrange("p (a t) -> p a t", a=1),
                       HH[:, bass.ds(o, 1), :].bitcast(F32), SUB).then_inc(act_lo, 1)

            hgrn(0, None)
            with dve.Fori(1, HEADS) as h:
                hgrn(h, h - 1)
            hgrn(None, HEADS - 1)
            his[0] += 8
            dve.drain()
            read_mixer(W0, free["go"])
            add_to_residual(1, 1)
            mlp(1, E0)
            for t in range(TT):
                dve.wait_ge(out_t, t + 1)
                for a in range(2):
                    dve.tensor_copy(OTOK[:, t, a * T:(a + 1) * T], PB[2 + a][:, :]).then_inc(out_r, 1)
    return nc


INS = ['x', 'c', 'w_ada', 'b_ada', 'w_in', 'mu_b', 'ln_v_g', 'ln_v_b', 'w_spatial', 'b_spatial', 'w0', 'w_up', 'a0',
       'a_up', 'k_k', 'k_a', 'r_k', 'gn_g', 'gn_b', 'w_out', 'ln_g', 'ln_b', 'positions_2', 'norm_gains_2',
       'mla_w_in_2', 'mla_q_norm_2', 'mla_kv_norm_2', 'mla_w_uq_2', 'mla_w_ukv_2', 'mla_w_o_2', 'hgrn_w_in_2',
       'hgrn_lb_logits_2', 'hgrn_o_norm_2', 'hgrn_w_o_2', 'mlp_w1_2', 'mlp_w2_2']


def kernel(**inputs):
    import concourse.bacc as bacc
    from concourse.bass_utils import run_bass_kernel_spmd

    nc = bacc.Bacc("TRN2", target_bir_lowering=False, num_devices=1)
    arrays = {f"in_{name}": np.ascontiguousarray(inputs[name]) for name in INS}
    half = 32
    freq = (10000.0 ** (-np.arange(half, dtype=np.float64) / half)).astype(np.float32)
    arrays["inv_freq"] = np.concatenate([freq, freq]).reshape(2 * half, 1)
    aps = [nc.dram_tensor(name, a.shape, mybir.dt.from_np(a.dtype), kind="ExternalInput").ap()
           for name, a in arrays.items()]
    out = nc.dram_tensor("out", inputs["x"].shape, F32, kind="ExternalOutput").ap()
    block_kernel(nc, *aps, out)
    r = run_bass_kernel_spmd(nc, [arrays], core_ids=[0])
    return r.results[0]["out"]
```

```python
from contextlib import ExitStack

import numpy as np
import concourse.bass as bass
from concourse import mybir

F32 = mybir.dt.float32
F32R = mybir.dt.float32r
I32 = mybir.dt.int32
ALU = mybir.AluOpType
ACT = mybir.ActivationFunctionType
AX = mybir.AxisListType.X
P = 128


def block_kernel(nc, x, c, w_ada, b_ada, w_in, mu_b, ln_v_g, ln_v_b, w_spatial, b_spatial, w0, w_up, a0, a_up,
                 k_k, k_a, r_k, gn_g, gn_b, w_out, ln_g, ln_b, positions, norm_gains, mla_w_in, mla_q_norm,
                 mla_kv_norm, mla_w_uq, mla_w_ukv, mla_w_o, hgrn_w_in, hgrn_lb, hgrn_o_norm, hgrn_w_o,
                 mlp_w1, mlp_w2, inv_freq, out):
    T, D = x.shape[1], x.shape[2]
    KT = D // P
    TT = T // P
    DA = D // 2
    JA = DA // P
    HB = 64
    NH = DA // HB
    CH = 64
    NCH = T // CH
    FF = mlp_w1.shape[2]
    NQ = FF // D
    HEADS = 8
    NOPE, ROPE = 128, 64
    QL = mla_q_norm.shape[1] // P
    KVL = mla_kv_norm.shape[1] // P
    HC = 32
    ALPHA = 2.0 ** 0.25
    KAPPA = float(np.exp(-0.5))
    SCALE = float(NOPE + ROPE) ** -0.5
    NEG = -3.0e38

    ctx = ExitStack()
    with ctx:
        base = -(-nc.sbuf_base // 32) * 32
        ctx.enter_context(nc.sbuf_tensor("arena", [P, 206 * 256], F32))
        placed = {}

        def at(name, kb, shape, dt=F32):
            placed[name] = nc.alloc_sbuf_tensor_at(name, shape, dt, offset=base + int(kb * 1024))
            return placed[name]

        def sem(name):
            return ctx.enter_context(nc.semaphore(name))

        WR = at("w_raw", 0, [P, 2, 8, P])
        WH = at("w_high", 8, [P, 2, 8, P], F32R)
        WL = at("w_low", 16, [P, 2, 8, P], F32R)
        XH = at("resid", 24, [P, KT, T])
        AH = at("act_high", 40, [P, KT, T], F32R)
        AL = at("act_low", 56, [P, KT, T], F32R)
        M = at("mix_out", 72, [P, KT, T])
        HH = at("hid_high", 88, [P, KT, T], F32R)
        HL = at("hid_low", 104, [P, KT, T], F32R)
        TMP = [at(f"tmp{n}", 120 + 2 * n, [P, T]) for n in range(6)]
        R1 = at("rstd_a", 132, [P, T])
        R2 = at("rstd_b", 134, [P, T])
        SQA = at("sum_sq", 136, [P, T])
        ONES = at("ones", 138, [P, P])
        IDENT = at("ident", 138.5, [P, P])
        BONES = at("head_ones", 139, [P, P])
        COL = at("cols", 139.5, [P, 192])
        MOD = at("mod", 140.25, [P, 24])
        SMALL = at("small", 140.375, [P, 96])
        CST = at("consts", 140.75, [P, 8])
        XTOK = at("x_tok", 72, [P, TT, D])
        ROWS = at("param_rows", 199, [P, 2, P])
        CSIL = at("c_act", 200, [P, 2 * KT])
        ADA = at("w_ada_piece", 88, [P, 2, KT, T])
        VTOK = at("v_tok", 173, [P, TT * NH, HB])
        VC = at("v_centred", 181, [P, TT * NH, HB])
        VFM = at("v_feature", 181, [P, JA, T])
        VSQ = at("v_sq", 191, [P, TT * NH, HB])
        U = at("u_act", 141, [P, JA, T])
        SG = at("gate_a", 149, [P, JA, T])
        WSP = at("w_spatial_sb", 157, [P, NH, P])
        WSPT = at("w_spatial_t", 161, [P, NH, P])
        LVG = at("ln_v_gain", 165, [P, DA])
        LVB = at("ln_v_bias", 167, [P, DA])
        BSP = at("b_spatial_sb", 169, [P, JA, P])
        WUA = at("w_up_a_up", 171, [P, DA])
        RKVG = at("rkvg", 72, [P, 4 * JA, T])
        WAD = at("wd_ad", 104, [P, T])
        PR = at("p_shift", 106, [P, 2, T + 2])
        CS = at("decay_sum", 149, [P, JA, T])
        SIG = at("decay_sig", 157, [P, JA, T])
        ICL = at("iclr_a", 173, [P, JA, T])
        KKN = at("kk_norm", 181, [P, JA, T])
        SQB = at("sq_bulk", 40, [P, JA, T])
        RSET = at("scan_reset", 189, [P, T])
        YT = at("y_rwkv", 48, [P, JA, T])
        AR = [at(f"ar_ops{n}", 40 + 2 * n, [P, JA, 2 * CH]) for n in range(3)]
        BK = at("bk_ops", 46, [P, JA, 2 * CH])
        BKT = [at(f"bk_tok{n}", 56 + 2 * n, [P, JA, P]) for n in range(3)]
        UV = [at(f"uv{n}", 62 + 2 * n, [P, NH, CH]) for n in range(3)]
        VS = at("v_ops", 68, [P, JA, 2 * CH])
        GA = at("g_masked_a", 70, [P, NH, CH])
        ZS = [at(f"z_sb{n}", 104 + 2 * n, [P, JA, CH]) for n in range(3)]
        GR = [at(f"g_masked_r{n}", 189 + 2 * n, [P, NH, CH]) for n in range(3)]
        MSKG = at("mask_g", 112.25, [P, 2 * CH])
        MSKS = at("mask_s", 112.75, [P, CH])
        MSKD = at("mask_d", 113, [P, CH])
        S = at("state", 113.25, [P, JA, CH])
        FS = at("state_decay", 114.25, [P, 3, JA])
        MSKSD = at("mask_sd", 114.5, [P, CH])
        SEL = at("head_select", 201, [P, JA, NH])
        SELT = at("head_spread", 201.5, [NH, JA, P])
        HST = at("head_stats", 203.5, [NH, T])
        ID2 = at("ident_halves", 114.75, [P, CH])
        EL = at("e_incl", 115, [P, JA, CH])
        ENL = at("e_neg", 116, [P, JA, CH])
        EX = at("e_excl", 117, [P, JA, CH])
        ND = at("n_diag", 118, [P, JA, CH])
        NDT = at("n_diag_t", 128, [P, JA, CH])
        NOT = at("n_off_t", 130, [P, JA, CH])
        X1 = at("pow_1", 132, [P, JA, CH])
        X1T = at("pow_1t", 134, [P, JA, CH])
        TD = at("inv_diag", 136, [P, JA, CH])
        TDF = at("inv_diag_full", 165, [P, JA, CH])
        FM = at("f_mat", 167, [P, JA, CH])
        FMT = at("f_mat_t", 169, [P, JA, CH])
        TDT = at("inv_diag_t", 171, [P, JA, CH])
        Y1 = at("inv_part_t", 195, [P, JA, CH])
        F2 = at("f_sq", 197, [P, JA, CH])
        TTM = at("inv_full_t", 199, [P, JA, CH])
        CQ = at("latents", 141, [P, QL + KVL, T])
        CQH = at("latents_high", 153, [P, QL + KVL, T], F32R)
        CQL = at("latents_low", 165, [P, QL + KVL, T], F32R)
        R3 = at("rstd_kv", 187, [P, T])
        SQK = at("sum_sq_kv", 189, [P, T])
        KR = at("k_rope", 177, [ROPE, T])
        QR = [at(f"q_rope{n}", (179, 141)[n], [ROPE, T]) for n in range(2)]
        QN = [at(f"q_nope{n}", (181, 143)[n], [P, T]) for n in range(2)]
        KN = [at(f"k_nope{n}", (183, 145)[n], [P, T]) for n in range(2)]
        VM = [at(f"v_mla{n}", (185, 147)[n], [P, TT, P]) for n in range(2)]
        PRB = [at(f"probs{n}", (187, 189, 149, 151)[n], [P, T]) for n in range(TT)]
        PT = at("probs_t", 191, [P, 2, TT, P])
        COS = at("cos", 195, [ROPE, T])
        SIN = at("sin", 197, [ROPE, T])
        ANG = at("angle", 199, [ROPE, T])
        ANGK = at("angle_k", 201, [ROPE, T], I32)
        PIX = at("positions_sb", 141, [ROPE, T], I32)
        CMASK = at("causal_mask", 203, [P, P])
        QG = at("hg_q", 141, [P, T])
        FG = at("hg_f", 143, [P, T])
        KG = at("hg_k", 145, [P, T])
        BG = at("hg_b", 147, [P, T])
        GG = at("hg_gate", 149, [P, T])
        VG = at("hg_v", 151, [P, TT, P])
        QREL = at("hg_q_rel", 153, [P, T])
        KREL = at("hg_k_rel", 155, [P, T])
        QDEC = at("hg_q_dec", 157, [P, T])
        KDEC = at("hg_k_dec", 159, [P, T])
        EBL = at("hg_decay", 161, [P, T // HC])
        KDT = at("hg_k_dec_t", 162, [P, TT, P])
        AT = at("hg_scores", 164, [P, TT, P])
        ST = at("hg_state", 182, [P, T // HC, P])
        OG = at("hg_out", 168, [P, T])
        HMSK = at("hg_mask", 170, [P, TT, P], I32)
        HRST = at("hg_reset", 172, [P, T])
        TG = [at(f"hg_t{n}", 174 + 2 * n, [P, T]) for n in range(4)]
        OSQ = at("hg_out_sq", 190, [P, T])
        OSD = at("hg_out_dev", 192, [P, T])
        VF = at("hg_v_feature", 194, [P, T])
        LREL = at("hg_b_less_ref", 196, [P, T])
        LBS = at("hg_bounds", 204.5, [P, 3 * HEADS])
        LBH = at("hg_bound", 204.75, [P, 2])
        LNSQ = at("ln_squares", 88, [P, KT, T])
        BON = at("bonus", 120, [P, JA, T])
        FC = at("inv_freq_sb", 205, [ROPE, 1])
        OTOK = at("out_tok", 88, [P, TT, D])

        PB = [ctx.enter_context(nc.psum_tensor(f"bank{n}", [P, 512], F32)) for n in range(8)]

        rows, col_of = [], {}
        for name, src, n in (("gains", norm_gains.rearrange("l a (k p) -> (l a k) p", p=P), 8 * KT),
                             ("b_ada", b_ada.rearrange("(k p) -> k p", p=P), 3 * KT),
                             ("mu", mu_b.rearrange("(k p) -> k p", p=P), 17),
                             ("lb", hgrn_lb.rearrange("l (k p) -> (l k) p", p=P), 2 * HEADS),
                             ("ln_g", ln_g.rearrange("(k p) -> k p", p=P), KT),
                             ("ln_b", ln_b.rearrange("(k p) -> k p", p=P), KT),
                             ("w0", w0.rearrange("(k p) -> k p", p=P), JA),
                             ("a0", a0.rearrange("(k p) -> k p", p=P), JA),
                             ("k_k", k_k.rearrange("(k p) -> k p", p=P), JA),
                             ("k_a", k_a.rearrange("(k p) -> k p", p=P), JA),
                             ("r_k", r_k.rearrange("(k a) d -> k (a d)", a=2), JA),
                             ("gn_g", gn_g.rearrange("(k a) d -> k (a d)", a=2), JA),
                             ("gn_b", gn_b.rearrange("(k a) d -> k (a d)", a=2), JA),
                             ("q_norm", mla_q_norm.rearrange("l (k p) -> (l k) p", p=P), QL),
                             ("kv_norm", mla_kv_norm.rearrange("l (k p) -> (l k) p", p=P), KVL),
                             ("o_norm", hgrn_o_norm, 1)):
            start = sum(r[2] for r in rows)
            if start < P < start + n:
                rows.append((None, None, P - start))
                start = P
            col_of[name] = start
            rows.append((name, src, n))
        n_rows = sum(r[2] for r in rows)

        def col(name, j=0, n=1, p0=0, p1=P):
            return COL[p0:p1, col_of[name] + j:col_of[name] + j + n]

        def gain(layer, which, k):
            return col("gains", (layer * 4 + which) * KT + k)

        A0 = 0
        B0 = A0 + 3 * JA
        O0 = B0 + 4 * JA + 1
        I0 = O0 + KT
        H0 = I0 + QL + KVL + 1
        V0 = H0 + 4 * HEADS
        F0 = V0 + KT
        G0 = F0 + 2 * KT * NQ
        W0 = G0 + 4 * HEADS
        E0 = W0 + KT
        NJ = E0 + 2 * KT * NQ
        USE = {n: k for k, n in enumerate(("in", "out", "mla", "mla_o", "mlp0", "hgrn", "hgrn_o", "mlp1"))}

        x_loaded, c_loaded, par_loaded = sem("x_loaded"), sem("c_loaded"), sem("par_loaded")
        bc_loaded = sem("bc_loaded")
        pos_loaded = sem("pos_loaded")
        ada_loaded = [sem("ada_loaded0"), sem("ada_loaded1")]
        w_loaded = [sem("w_loaded0"), sem("w_loaded1")]
        w_hi, w_lo = sem("w_hi"), sem("w_lo")
        job_done = sem("job_done")
        act_hi, act_lo = sem("act_hi"), sem("act_lo")
        const_ready, const_pool = sem("const_ready"), sem("const_pool")
        x_turned, x_read, par_turned = sem("x_turned"), sem("x_read"), sem("par_turned")
        ada_used, ada_part = sem("ada_used"), sem("ada_part")
        c_ready, ada_done, mod_ready = sem("c_ready"), sem("ada_done"), sem("mod_ready")
        gate_ready = sem("gate_ready")
        free = {n: sem("free_" + n) for n in ("a", "b", "o", "mi", "h", "mo", "f0", "g", "go", "f1")}
        v_turned = sem("v_turned")
        v_gelu, v_ms, v_sd, v_ready = sem("v_gelu"), sem("v_ms"), sem("v_sd"), sem("v_ready")
        wsp_t, wsp_r, sp_done, u_ready, oa_ready = (sem("wsp_t"), sem("wsp_r"), sem("sp_done"), sem("u_ready"),
                                                    sem("oa_ready"))
        wsp_masked = sem("wsp_masked")
        p_copied, p_free, p_mixed = sem("p_copied"), sem("p_free"), sem("p_mixed")
        lr_tanh, lr_done, lr_sig = sem("lr_tanh"), sem("lr_done"), sem("lr_sig")
        sel_ready, kk_rs, kk_sp, gn_rs, gn_sp = (sem(n) for n in ("sel_ready", "kk_rs", "kk_sp", "gn_rs", "gn_sp"))
        decay_ready = sem("decay_ready")
        kk_sq, kk_ss, kk_sd, rk_ready, rk_done, bulk_ready = (sem("kk_sq"), sem("kk_ss"), sem("kk_sd"),
                                                              sem("rk_ready"), sem("rk_done"), sem("bulk_ready"))
        g_silu = sem("g_silu")
        ch_exp, ch_vs, ch_ops, ch_g, ch_t, ch_nd, ch_tok = (sem("ch_" + n) for n in ("exp", "vs", "ops", "g", "t",
                                                                                     "nd", "tok"))
        pw_pe, pw_dve, pw_act, in_pe, in_dve, in_act = (sem(n) for n in ("pw_pe", "pw_dve", "pw_act", "in_pe",
                                                                         "in_dve", "in_act"))
        mv_done, mv_read = sem("mv_done"), sem("mv_read")
        z_done, z_read, u_done, u_read, s_new, y_done, y_read = (
            sem("z_done"), sem("z_read"), sem("u_done"), sem("u_read"), sem("s_new"), sem("y_done"), sem("y_read"))
        gn_pe, gn_dve, gn_act, ob_ready = sem("gn_pe"), sem("gn_dve"), sem("gn_act"), sem("ob_ready")
        ln_sq, ln_sub = sem("ln_sq"), sem("ln_sub")
        ln_pe, ln_dve, ln_act = sem("ln_pe"), sem("ln_dve"), sem("ln_act")
        nm_dve, nm_pe, nm_act, nm_sq = sem("nm_dve"), sem("nm_pe"), sem("nm_act"), sem("nm_sq")
        rp_ang, rp_sin = sem("rp_ang"), sem("rp_sin")
        cq_ready, kr_ready = sem("cq_ready"), sem("kr_ready")
        cq_hi, cqh_ready, cq_lo = sem("cq_normed"), sem("cq_high"), sem("cq_low")
        lb_diff, lb_exp = sem("lb_diff"), sem("lb_exp")
        h_q, h_r, h_s, h_mx, h_exp, h_pn, h_pt, h_ptr, h_o, h_or = (
            sem("h_q"), sem("h_r"), sem("h_s"), sem("h_mx"), sem("h_exp"), sem("h_pn"), sem("h_pt"), sem("h_ptr"),
            sem("h_o"), sem("h_or"))
        mx_out, resid_ready = sem("mx_out"), sem("resid_ready")
        m_relu, m_hid, m_hidlo = sem("m_relu"), sem("m_hid"), sem("m_hidlo")
        nm_dev, pre_sq, gained = sem("nm_dev"), sem("pre_sq"), sem("gained")
        f_up, f_dn = [sem("free_up0"), sem("free_up1")], [sem("free_dn0"), sem("free_dn1")]
        g_vt, g_vc = sem("g_vt"), sem("g_vc")
        g_silu3, g_f, g_ln, g_diff, g_exp, g_ops, g_sc, g_at, g_kt, g_inc, g_st, g_out, g_sq, g_ss, g_sd, g_fin = (
            sem("g_" + n) for n in ("silu3", "f", "ln", "diff", "exp", "ops", "sc", "at", "kt", "inc", "st", "out",
                                    "sq", "ss", "sd", "fin"))
        out_h = sem("out_h")
        out_t, out_r, stored = sem("out_t"), sem("out_r"), sem("stored")
        block = ctx.enter_context(nc.Block())

        def mla_pipeline(engine, step):
            step(0, 0, None, None)
            with engine.Fori(0, HEADS // 2 - 1) as g:
                for s in range(2):
                    step(g * 2 + 1 + s, 1 - s, g * 2 + s, s)
            step(HEADS - 1, 1, HEADS - 2, 0, last=True)
            step(None, None, HEADS - 1, 1)

        def add_tile_squares(engine, use):
            for k in range(1, KT):
                engine.wait_ge(pre_sq, use * KT + k + 1)
                engine.tensor_tensor(SQA[:, :], (M[:, 0, :] if k == 1 else SQA[:, :]), M[:, k, :], ALU.add)
                engine.drain()
            engine.sem_inc(nm_dve, 1)

        SBANK = (2, 3, 7, 2)

        def following(k):
            return (k + 1) & (NCH - 1)

        def rwkv_pipeline(engine, step):
            step(0, 0, None, None, None, None)
            step(1, 1, 0, 0, None, None)
            with engine.Fori(0, (NCH - 2) // 3) as g:
                for n in range(3):
                    step(g * 3 + 2 + n, (2 + n) % 3, g * 3 + 1 + n, (1 + n) % 3, g * 3 + n, n)
            step(None, None, NCH - 1, (NCH - 1) % 3, NCH - 2, (NCH - 2) % 3)
            step(None, None, None, None, NCH - 1, (NCH - 1) % 3)

        w_in_v = w_in.rearrange("(k p) n -> p k n", p=P)
        w_out_v = w_out.rearrange("(k p) n -> p k n", p=P)
        mla_in_v = mla_w_in[0].rearrange("(k p) n -> p k n", p=P)
        uq_v = mla_w_uq[0].rearrange("(k p) n -> p k n", p=P)
        ukv_v = mla_w_ukv[0].rearrange("(k p) n -> p k n", p=P)
        mla_o_v = mla_w_o[0].rearrange("(k p) n -> p k n", p=P)
        hg_in_v = hgrn_w_in[0].rearrange("(k p) n -> p k n", p=P)
        hg_o_v = hgrn_w_o[0].rearrange("(k p) n -> p k n", p=P)
        w1_v = [mlp_w1[l].rearrange("(k p) n -> p k n", p=P) for l in range(2)]
        w2_v = [mlp_w2[l].rearrange("(q k p) n -> p (q k) n", p=P, k=KT) for l in range(2)]
        ada_v = w_ada.rearrange("(p j) n -> p j n", j=KT)

        @block.sync
        def _(sp):
            sp.dma_start(CSIL[:, 0:KT], c.rearrange("a (p j) -> (a p) j", j=KT)).then_inc(c_loaded, 16)
            for n in range(6):
                if n >= 2:
                    sp.wait_ge(ada_used, n - 1)
                if n == 4:
                    for j in range(2):
                        sp.dma_start(WR[:, j, :, :], w_in_v[:, :, j * P:(j + 1) * P]).then_inc(w_loaded[j], 16)
                sp.dma_start(ADA[:, n % 2], ada_v[:, :, n * T:(n + 1) * T]).then_inc(ada_loaded[n % 2], 16)

            def load(c0, src, r=0, kt=8, m=P):
                if c0 >= 2:
                    sp.wait_ge(w_lo, c0 - 1 + r)
                sp.dma_start(WR[:, c0 % 2, 0:kt, 0:m], src).then_inc(w_loaded[c0 % 2], 16)

            with sp.Fori(1, (O0 - 1) // 2) as i:
                for s in range(2):
                    load(A0 + 2 + s, w_in_v[:, :, bass.ds(i * 2 * P + s * P, P)], (i - 1) * 2)
            load(O0 - 1, w_in_v[:, :, (O0 - 1) * P:O0 * P])
            with sp.Fori(0, KT // 2) as i:
                for s in range(2):
                    load(O0 + s, w_out_v[:, :, bass.ds(i * 2 * P + s * P, P)], i * 2)
            for j in range(QL + KVL):
                load(I0 + j, mla_in_v[:, :, j * P:(j + 1) * P])
            load(H0 - 1, mla_in_v[:, :, (QL + KVL) * P:(QL + KVL) * P + ROPE], m=ROPE)
            with sp.Fori(0, HEADS) as h:
                load(H0, uq_v[:, :, bass.ds(h * (NOPE + ROPE), NOPE)], h * 4, kt=QL)
                load(H0 + 1, uq_v[:, :, bass.ds(h * (NOPE + ROPE) + NOPE, ROPE)], h * 4, kt=QL, m=ROPE)
                load(H0 + 2, ukv_v[:, :, bass.ds(h * 2 * P, P)], h * 4, kt=KVL)
                load(H0 + 3, ukv_v[:, :, bass.ds(h * 2 * P + P, P)], h * 4, kt=KVL)
            with sp.Fori(0, KT // 2) as i:
                for s in range(2):
                    load(V0 + s, mla_o_v[:, :, bass.ds(i * 2 * P + s * P, P)], i * 2)

            def load_mlp(l, j0):
                with sp.Fori(0, NQ) as q:
                    with sp.Fori(0, KT // 2) as i:
                        for s in range(2):
                            load(j0 + s, w1_v[l][:, :, bass.ds(q * D + i * 2 * P + s * P, P)], q * 2 * KT + i * 2)
                    with sp.Fori(0, KT // 2) as i:
                        for s in range(2):
                            load(j0 + KT + s, w2_v[l][:, bass.ds(q * KT, KT), bass.ds(i * 2 * P + s * P, P)],
                                 q * 2 * KT + i * 2)

            load_mlp(0, F0)
            with sp.Fori(1, HEADS + 1) as h1:
                for j, part in enumerate((1, 0, 2, 3)):
                    load(G0 + j, hg_in_v[:, :, bass.ds(h1 * P + (part * D - P), P)], h1 * 4 - 4)
            with sp.Fori(0, KT // 2) as i:
                for s in range(2):
                    load(W0 + s, hg_o_v[:, :, bass.ds(i * 2 * P + s * P, P)], i * 2)
            load_mlp(1, E0)
            out_v = out[0].rearrange("(t p) d -> p t d", p=P)
            sp.wait_ge(out_h, TT)
            sp.dma_start(out_v[:, :, 0:T], OTOK[:, :, 0:T]).then_inc(stored, 16)
            sp.wait_ge(out_r, TT)
            sp.dma_start(out_v[:, :, T:2 * T], OTOK[:, :, T:2 * T]).then_inc(stored, 16)
            sp.wait_ge(stored, 32)

        @block.gpsimd
        def _(gp):
            gp.memset(ONES[:, :], 1.0)
            gp.memset(IDENT[:, :], 0.0)
            gp.memset(BONES[:, :], 0.0)
            gp.memset(CST[:, 0:1], 1e-5)
            gp.memset(CST[:, 1:2], 1e-12)
            gp.memset(CST[:, 2:3], 64e-5)
            gp.memset(CST[:, 3:4], 1e-6)
            gp.memset(CST[:, 4:5], float(np.pi / 2))
            gp.memset(RSET[:, :], 1.0)
            gp.drain()
            gp.affine_select(out=IDENT[:, :], in_=IDENT[:, :], compare_op=ALU.not_equal, fill=1.0, base=0,
                             pattern=[[-1, P]], channel_multiplier=1)
            gp.drain()
            gp.memset(BONES[0:HB, 0:HB], 1.0)
            gp.drain()
            gp.memset(BONES[HB:P, HB:P], 1.0)
            gp.drain()
            gp.memset(RSET[:, :].rearrange("p (c t) -> p c t", t=CH)[:, :, 0:1], 0.0)
            gp.drain()
            gp.nop().then_inc(const_ready, 1)
            at_row = 0
            gp.memset(ROWS[:, :, :], 0.0)
            gp.drain()
            n_dma = 0
            for name, src, n in rows:
                if name:
                    t, r = divmod(at_row, P)
                    gp.dma_start(ROWS[r:r + n, t, :], src).then_inc(par_loaded, 16)
                    n_dma += 1
                at_row += n
            gp.dma_start(WSP[:, :, :], w_spatial.rearrange("g t s -> t g s")).then_inc(bc_loaded, 16)
            gp.dma_start(LVG[:, :], ln_v_g.rearrange("g d -> (g d)").partition_broadcast(P)).then_inc(bc_loaded, 16)
            gp.dma_start(LVB[:, :], ln_v_b.rearrange("g d -> (g d)").partition_broadcast(P)).then_inc(bc_loaded, 16)
            for a in range(2):
                gp.dma_start(BSP[a * HB:(a + 1) * HB, :, :],
                             b_spatial.rearrange("(j a) t -> a j t", a=2)[a].partition_broadcast(HB))\
                    .then_inc(bc_loaded, 16)
            gp.dma_start(WUA[0:64, :], w_up).then_inc(bc_loaded, 16)
            gp.dma_start(WUA[64:128, :], a_up).then_inc(bc_loaded, 16)
            gp.wait_ge(bc_loaded, 16 * 7)
            gp.affine_select(out=WSP[:, :, :], in_=WSP[:, :, :], compare_op=ALU.is_ge, fill=0.0, base=0,
                             pattern=[[0, NH], [-1, P]], channel_multiplier=1).then_inc(wsp_masked, 1)

            def low(c0, r=0, kt=8, m=P):
                gp.wait_ge(w_hi, c0 + 1 + r)
                gp.tensor_tensor(WL[:, c0 % 2, 0:kt, 0:m], WR[:, c0 % 2, 0:kt, 0:m],
                                 WH[:, c0 % 2, 0:kt, 0:m].bitcast(F32), ALU.subtract).then_inc(w_lo, 1)

            def low_of_gained(norm, use):
                for k in range(KT):
                    gp.wait_ge(gained, KT * norm + k + 1)
                    gp.wait_ge(act_hi, KT * USE[use] + k + 1)
                    gp.tensor_tensor(AL[:, k, :], M[:, k, :], AH[:, k, :].bitcast(F32), ALU.subtract)\
                        .then_inc(act_lo, 1)

            with gp.Fori(0, O0 // 2) as i:
                for s in range(2):
                    low(s, i * 2)
            low(O0 - 1)
            gp.memset(SEL[:, :, :], 0.0)
            gp.memset(SELT[:, :, :], 1.0)
            gp.drain()
            for j in range(JA):
                for a in range(2):
                    gp.memset(SEL[a * HB:(a + 1) * HB, j, 2 * j + a:2 * j + a + 1], 1.0)
                    gp.drain()
            sel_f = SELT[:, :, :].rearrange("h j p -> h (j p)")
            gp.affine_select(out=sel_f, in_=sel_f, compare_op=ALU.is_ge, fill=0.0, base=0,
                             pattern=[[1, JA * P]], channel_multiplier=-HB)
            gp.drain()
            gp.affine_select(out=sel_f, in_=sel_f, compare_op=ALU.is_gt, fill=0.0, base=HB,
                             pattern=[[-1, JA * P]], channel_multiplier=HB).then_inc(sel_ready, 1)
            gp.wait_ge(p_mixed, 4 * JA + 1)
            gp.memset(MSKG[:, :], 1.0)
            gp.memset(MSKS[:, :], 1.0)
            gp.memset(MSKD[:, :], 0.0)
            gp.drain()
            for half in range(2):
                rows_ = MSKG[half * CH:(half + 1) * CH, :]
                gp.affine_select(out=rows_[:, 0:CH], in_=rows_[:, 0:CH], compare_op=ALU.is_gt, fill=0.0,
                                 base=0, pattern=[[1, CH]], channel_multiplier=-1)
                gp.affine_select(out=rows_[:, CH:2 * CH], in_=rows_[:, CH:2 * CH], compare_op=ALU.is_ge,
                                 fill=0.0, base=0, pattern=[[1, CH]], channel_multiplier=-1)
                gp.drain()
            for half in range(2):
                ms = MSKS[half * CH:(half + 1) * CH, :]
                gp.affine_select(out=ms, in_=ms, compare_op=ALU.is_gt, fill=0.0, base=0,
                                 pattern=[[-1, CH]], channel_multiplier=1)
                md = MSKD[half * CH:(half + 1) * CH, :].rearrange("p (b t) -> p b t", t=16)
                gp.affine_select(out=md, in_=md, compare_op=ALU.is_gt, fill=1.0, base=0,
                                 pattern=[[16, CH // 16], [0, 16]], channel_multiplier=-1)
                gp.drain()
                gp.affine_select(out=md, in_=md, compare_op=ALU.is_ge, fill=0.0, base=15,
                                 pattern=[[16, CH // 16], [0, 16]], channel_multiplier=-1)
                gp.drain()
            gp.tensor_tensor(MSKSD[:, :], MSKS[:, :], MSKD[:, :], ALU.mult).then_inc(const_pool, 1)
            with gp.Fori(0, KT // 2) as i:
                for s in range(2):
                    low(O0 + s, i * 2)
            gp.memset(CMASK[:, :], 0.0)
            gp.drain()
            gp.affine_select(out=CMASK[:, :], in_=CMASK[:, :], compare_op=ALU.is_ge, fill=NEG, base=0,
                             pattern=[[-1, P]], channel_multiplier=1).then_inc(const_pool, 1)
            for j in range(QL + KVL):
                low(I0 + j)
                if j == 1:
                    low_of_gained(0, "mla")
            low(H0 - 1, m=ROPE)
            with gp.Fori(0, HEADS) as h:
                low(H0, h * 4, kt=QL)
                low(H0 + 1, h * 4, kt=QL, m=ROPE)
                low(H0 + 2, h * 4, kt=KVL)
                low(H0 + 3, h * 4, kt=KVL)
            with gp.Fori(0, KT // 2) as i:
                for s in range(2):
                    low(V0 + s, i * 2)
            for s in range(2):
                low(F0 + s)
            low_of_gained(1, "mlp0")
            with gp.Fori(1, NQ * KT) as i:
                for s in range(2):
                    low(F0 + s, i * 2)
            gp.memset(TG[0][:, :], 1.0)
            gp.memset(HRST[:, :], 1.0)
            gp.drain()
            gp.memset(HRST[:, :].rearrange("p (c t) -> p c t", t=HC)[:, :, 0:1], 0.0)
            hm = TG[0][:, :].rearrange("p (a b t) -> p a b t", a=TT, t=HC)
            gp.affine_select(out=hm, in_=hm, compare_op=ALU.is_ge, fill=0.0, base=0,
                             pattern=[[0, TT], [HC, P // HC], [1, HC]], channel_multiplier=-1)
            gp.drain()
            gp.affine_select(out=hm, in_=hm, compare_op=ALU.is_ge, fill=0.0, base=0,
                             pattern=[[0, TT], [-HC, P // HC], [0, HC]], channel_multiplier=1)
            gp.drain()
            gp.tensor_copy(HMSK[:, :, :].rearrange("p a t -> p (a t)"), TG[0][:, :])
            gp.memset(AT[:, :, :], 0.0)
            gp.drain()
            gp.nop().then_inc(const_pool, 1)
            for s in range(2):
                low(G0 + s)
            low_of_gained(2, "hgrn")
            with gp.Fori(1, HEADS * 2) as i:
                for s in range(2):
                    low(G0 + s, i * 2)
            with gp.Fori(0, KT // 2) as i:
                for s in range(2):
                    low(W0 + s, i * 2)
            for s in range(2):
                low(E0 + s)
            low_of_gained(3, "mlp1")
            with gp.Fori(1, NQ * KT) as i:
                for s in range(2):
                    low(E0 + s, i * 2)

        @block.tensor
        def _(pe):
            def job(c0, r, fr, n, kt=8, m=P, hi=AH, lo=AL, k0=0, token_major=False, ready=None):
                s = c0 % 2
                pe.wait_ge(w_lo, c0 + 1 + r)
                pe.wait_ge(fr, n)
                if not token_major:
                    for k in range(kt):
                        if ready is not None:
                            pe.wait_ge(ready[0], ready[1] + k + 1)
                        for w, a in ((WH, hi), (WH, lo), (WL, hi)):
                            mm = pe.matmul(PB[s][0:m, :], w[:, s, k, 0:m], a[:, k0 + k, :],
                                           start=(k == 0 and w is WH and a is hi), stop=(k == kt - 1 and w is WL))
                else:
                    for t in range(TT):
                        for k in range(kt):
                            for w, a in ((WH, hi), (WH, lo), (WL, hi)):
                                mm = pe.matmul(PB[s][:, t * P:(t + 1) * P], a[:, k0 + k, t * P:(t + 1) * P],
                                               w[:, s, k, :], start=(k == 0 and w is WH and a is hi),
                                               stop=(k == kt - 1 and w is WL))
                mm.then_inc(job_done, 1)

            def hold(*waits):
                waits = [(signal, pe.to_reg(n)) for signal, n in waits]
                pe.wait_ge(const_ready, 1)
                for signal, n in waits:
                    pe.wait_ge(signal, n)

            pe.wait_ge(const_ready, 1)

            def modulation(n):
                pe.wait_ge(ada_part, n + 1)
                for b in range(4):
                    for a in range(2):
                        mm = pe.matmul(PB[6][:, 4 * n + b:4 * n + b + 1], TMP[n % 2 * 2 + a][:, b * P:(b + 1) * P],
                                       ONES[:, 0:1], start=(a == 0), stop=(a == 1))
                mm.then_inc(ada_done, 1)

            modulation(0)
            modulation(1)
            pe.wait_ge(par_loaded, 16 * sum(1 for r in rows if r[0]))
            for t in range(2):
                mm = pe.transpose(PB[7][:, t * P:(t + 1) * P], ROWS[:, t, :], IDENT[:, :])
            mm.then_inc(par_turned, 1)
            pe.wait_ge(x_loaded, 16)
            for k in range(KT):
                if k >= 6:
                    pe.wait_ge(x_read, k - 5)
                for t in range(TT):
                    mm = pe.transpose(PB[k % 6][:, t * P:(t + 1) * P], XTOK[:, t, k * P:(k + 1) * P], IDENT[:, :])
                mm.then_inc(x_turned, 1)
            modulation(2)
            modulation(3)
            pe.wait_ge(x_read, KT)

            def part(c, bank_credit, use, k0, k1, hi=AH, lo=AL):
                if k0 == 0:
                    pe.wait_ge(w_lo, c + 1)
                    pe.wait_ge(*bank_credit)
                for k in range(k0, k1):
                    pe.wait_ge(act_lo, KT * USE[use] + k + 1)
                    for w, a in ((WH, hi), (WH, lo), (WL, hi)):
                        mm = pe.matmul(PB[c % 2][:, :], w[:, c % 2, k, :], a[:, k, :],
                                       start=(k == 0 and w is WH and a is hi), stop=(k == KT - 1 and w is WL))
                if k1 == KT:
                    mm.then_inc(job_done, 1)

            LAG = 5

            def two_jobs(c0, fr, use):
                for k in range(KT + LAG):
                    if k < KT:
                        part(c0, (fr, 1), use, k, k + 1)
                    if k >= LAG:
                        part(c0 + 1, (fr, 2), use, k - LAG, k - LAG + 1)

            two_jobs(A0, free["a"], "in")
            for i in range(2, 2 * JA):
                job(A0 + i, 0, free["a"], i + 1)
                if i in (3, 4):
                    modulation(i + 1)
            with pe.Fori(0, JA // 2) as i:
                for s in range(2):
                    job(A0 + 2 * JA + s, i * 2, free["a"], i * 2 + s + 1 + 2 * JA)
            pe.wait_ge(v_gelu, 1)
            pe.wait_ge(gate_ready, 1)
            for j in range(JA):
                for t in range(TT):
                    mm = pe.transpose(PB[4 + j][:, t * P:(t + 1) * P], VFM[:, j, t * P:(t + 1) * P], IDENT[:, :])
                mm.then_inc(v_turned, 1)
            pe.wait_ge(wsp_masked, 1)
            for g in range(NH):
                mm = pe.transpose(PB[2 + g // 4][:, (g % 4) * P:(g % 4 + 1) * P], WSP[:, g, :], IDENT[:, :])
            mm.then_inc(wsp_t, 1)
            with pe.Fori(0, 2 * JA) as i:
                for s in range(2):
                    job(B0 + s, i * 2, free["b"], i * 2 + s + 1)
            job(O0 - 1, 0, free["b"], 4 * JA + 1)
            pe.wait_ge(wsp_r, 1)
            pe.wait_ge(v_ready, 1)
            for j in range(JA):
                for t in range(TT):
                    for a in range(2):
                        g = 2 * j + a
                        mm = pe.matmul(PB[2 + j][a * HB:(a + 1) * HB, t * P:(t + 1) * P],
                                       VC[:, t * NH + g, :], WSPT[:, g, :], start=True, stop=True)
                mm.then_inc(sp_done, 1)
            pe.wait_ge(lr_tanh, 1)
            for j in range(JA):
                mm = pe.matmul(PB[(6 + j) % 8][:, :], WUA[0:64, j * P:(j + 1) * P], WAD[0:64, :],
                               start=True, stop=True)
                mm.then_inc(lr_done, 1)
            pe.wait_ge(oa_ready, 1)
            for j in range(JA):
                mm = pe.matmul(PB[2 + j][:, :], WUA[64:128, j * P:(j + 1) * P], WAD[64:128, :],
                               start=True, stop=True)
                mm.then_inc(lr_done, 1)
            pe.wait_ge(kk_sq, 1)
            pe.wait_ge(lr_sig, 2)
            pe.wait_ge(sel_ready, 1)
            for j in range(JA):
                mm = pe.matmul(PB[6][0:NH, :], SEL[:, j, :], SQB[:, j, :], start=(j == 0), stop=(j == JA - 1))
            mm.then_inc(kk_ss, 1)
            pe.wait_ge(rk_ready, 1)
            for j in range(JA):
                mm = pe.matmul(PB[2 + j][:, :], BONES[:, :], SQB[:, j, :], start=True, stop=True)
            mm.then_inc(rk_done, 1)
            pe.wait_ge(kk_rs, 1)
            for j in range(JA):
                pe.matmul(PB[(6 + j) % 8][:, :], SELT[:, j, :], HST[:, :], start=True, stop=True).then_inc(kk_sp, 1)
            pe.wait_ge(bulk_ready, 1)

            def heads():
                return [(h, h // 2, (h % 2) * HB) for h in range(NH)]

            def hs(h, bank):
                return PB[bank][h % 2 * HB:h % 2 * HB + HB, h // 2 * HB:(h // 2 + 1) * HB]

            def each(bank, left, right):
                for h, j, p in heads():
                    mm = pe.matmul(hs(h, bank), left[p:p + HB, j, :], right[p:p + HB, j, :], start=True, stop=True)
                return mm

            def step(k1, s1, k2, s2, k3, s3):
                if k1 is not None:
                    hold((ch_ops, k1 + 1), (ch_vs, k1 + 1))
                    for j in range(JA):
                        pe.transpose(PB[6][:, j * P:(j + 1) * P], VS[:, j, :], IDENT[:, :])
                if k2 is not None:
                    hold((pw_dve, k2 * 4 + 3), (pw_act, k2 * 3 + 3))
                    each(0, X1T, TD).then_inc(pw_pe, 1)
                if k1 is not None:
                    for h, j, p in heads():
                        pe.matmul(PB[1 + h % 2][:, j * P:(j + 1) * P], BK[p:p + HB, j, :], AR[s1][p:p + HB, j, :],
                                  start=True, stop=True)
                    for h, j, p in heads():
                        mm = pe.matmul(hs(h, 3), AR[s1][p:p + HB, j, 0:CH], BK[p:p + HB, j, p:p + CH],
                                       start=True, stop=True)
                    mm.then_inc(ch_g, 1)
                    if k3 is not None:
                        hold((in_dve, k3 * 3 + 3))
                    for j in range(JA):
                        mm = pe.transpose(PB[5][:, j * P:(j + 1) * P], BK[:, j, :], IDENT[:, :])
                    mm.then_inc(ch_t, 1)
                if k2 is not None:
                    hold((pw_dve, k2 * 4 + 4))
                    each(0, NOT, TDF).then_inc(in_pe, 1)
                if k3 is not None:
                    hold((s_new, k3 + 1), (y_read, k3 + 1))
                    for h, j, p in heads():
                        mm = pe.matmul(hs(h, 4), AR[s3][p:p + HB, j, 0:CH], S[p:p + HB, j, :],
                                       start=True, stop=True)
                    mm.then_inc(z_done, 1)
                    for h, j, p in heads():
                        pe.matmul(PB[7][p:p + HB, j * HB:(j + 1) * HB], S[p:p + HB, j, :],
                                  AR[s3][p:p + HB, j, CH:P], start=(j == 0), stop=False)
                if k1 is not None:
                    hold((ch_nd, k1 + 1))
                    each(1, NDT, ND)
                    each(2, ND, NDT).then_inc(pw_pe, 1)
                    hold((ch_tok, k1 + 1))
                if k2 is not None:
                    each(5, TDF, NOT)
                    for h, j, p in heads():
                        mm = pe.matmul(hs(h, 6), TDF[p:p + HB, j, :], ID2[p:p + HB, :], start=True, stop=True)
                    mm.then_inc(in_pe, 1)
                if k3 is not None:
                    hold((z_read, k3 + 1), (in_dve, k3 * 3 + 3))
                    each(4, TTM, ZS[s3]).then_inc(u_done, 1)
                if k1 is not None:
                    if k2 is not None:
                        hold((in_dve, k2 * 3 + 1))
                    for h, j, p in heads():
                        mm = pe.matmul(hs(h, 0), GA[CH - p:P - p, h, :], UV[s1][CH - p:P - p, h, :], start=True,
                                       stop=True)
                    mm.then_inc(mv_done, 1)
                if k1 is not None:
                    hold((pw_dve, k1 * 4 + 1), (pw_act, k1 * 3 + 1))
                    each(3, X1T, TD)
                    each(1, X1T, X1)
                    each(2, X1, X1T).then_inc(pw_pe, 1)
                if k2 is not None:
                    hold((in_dve, k2 * 3 + 1), (in_act, k2 * 2 + 1))
                    if k1 is not None:
                        hold((mv_read, k1 + 1))
                    each(0, FM, TDT)
                    each(5, FMT, FM).then_inc(in_pe, 1)
                if k3 is not None:
                    hold((u_read, k3 + 1))
                    for h, j, p in heads():
                        pe.matmul(PB[7][p:p + HB, (JA + j) * HB:(JA + j + 1) * HB], BKT[s3][:, j, p:p + HB],
                                  UV[s3][:, h, :], start=False, stop=False)
                    for h, j, p in heads():
                        mm = pe.matmul(PB[7][p:p + HB, j * HB:(j + 1) * HB], UV[s3][:, h, :], GR[s3][:, h, :],
                                       start=False, stop=(j == JA - 1))
                    mm.then_inc(y_done, 1)
                if k1 is not None:
                    hold((pw_dve, k1 * 4 + 2), (pw_act, k1 * 3 + 2))
                    each(3, X1T, TD)
                    each(2, X1, X1T).then_inc(pw_pe, 1)
                if k2 is not None:
                    hold((in_dve, k2 * 3 + 2), (in_act, k2 * 2 + 2))
                    each(5, F2, Y1).then_inc(in_pe, 1)

            rwkv_pipeline(pe, step)
            pe.wait_ge(y_read, NCH + 1)
            for j in range(JA):
                mm = pe.matmul(PB[2 + j][:, :], BONES[:, :], YT[:, j, :], start=True, stop=True)
            mm.then_inc(gn_pe, 1)
            pe.wait_ge(gn_dve, 1)
            for j in range(JA):
                mm = pe.matmul(PB[6][0:NH, :], SEL[:, j, :], SQB[:, j, :], start=(j == 0), stop=(j == JA - 1))
            mm.then_inc(gn_pe, 1)
            pe.wait_ge(gn_rs, 1)
            for j in range(JA):
                pe.matmul(PB[2 + j][:, :], SELT[:, j, :], HST[:, :], start=True, stop=True).then_inc(gn_sp, 1)

            def six_jobs(c0, fr, hi=AH, lo=AL):
                with pe.Fori(1, KT // 2) as i:
                    for s in range(2):
                        job(c0 + s, i * 2, fr, i * 2 + s + 1, hi=hi, lo=lo)

            two_jobs(O0, free["o"], "out")
            six_jobs(O0, free["o"])
            pe.wait_ge(ln_dve, 1)
            mm = pe.matmul(PB[2][:, :], ONES[:, :], SQA[:, :], start=True, stop=True)
            mm.then_inc(ln_pe, 1)
            for k in range(KT):
                pe.wait_ge(ln_sq, k + 1)
                mm = pe.matmul(PB[3][:, :], ONES[:, :], LNSQ[:, k, :], start=(k == 0), stop=(k == KT - 1))
            mm.then_inc(ln_pe, 1)

            norms = [0]

            def norm_sum(src=SQA, bank=2):
                norms[0] += 1
                pe.wait_ge(nm_dve, norms[0])
                pe.matmul(PB[bank][:, :], ONES[:, :], src[:, :], start=True, stop=True).then_inc(nm_pe, 1)

            two_jobs(I0, free["mi"], "mla")
            norm_sum()
            for j in range(2, QL + KVL):
                job(I0 + j, 0, free["mi"], j + 1)
            norm_sum()
            job(H0 - 1, 0, free["mi"], QL + KVL + 1, m=ROPE)
            norm_sum(SQK, 3)
            pe.wait_ge(const_pool, 2)

            def step(n, sn, o, so, last=False):
                def scores(q):
                    w = (q + 1) * P
                    if q == 3:
                        pe.wait_ge(h_exp, o * TT + 1)
                    ps = PB[SBANK[q]][:, 0:w]
                    pe.matmul(ps, QN[so][:, q * P:w], KN[so][:, 0:w], start=True, stop=False)
                    pe.matmul(ps, QR[so][:, q * P:w], KR[:, 0:w], start=False, stop=True).then_inc(h_s, 1)

                def turn(q):
                    pe.wait_ge(h_pn, o * TT + q + 1)
                    for b in range(q + 1):
                        mm = pe.transpose(PB[4 + q % 2][:, b * P:(b + 1) * P], PRB[q][:, b * P:(b + 1) * P],
                                          IDENT[:, :])
                    mm.then_inc(h_pt, 1)

                def values(q):
                    pe.wait_ge(h_ptr, o * TT + q + 1)
                    for b in range(q + 1):
                        mm = pe.matmul(PB[6][:, q * P:(q + 1) * P], VM[so][:, b, :], PT[:, q % 2, b, :],
                                       start=(b == 0), stop=(b == q))
                    if q == TT - 1:
                        mm.then_inc(h_o, 1)

                if o is not None:
                    pe.wait_ge(h_q, o * 3 + 3)
                    pe.wait_ge(h_r, o + 1)
                    scores(0)
                    scores(1)
                    scores(2)
                if n is None:
                    pe.wait_ge(h_q, HEADS * 3 + 1)
                    part(V0, (free["mo"], 1), "mla_o", 0, 3)
                if n is not None:
                    job(H0, n * 4, h_q, n * 3 + 1, kt=QL, hi=CQH, lo=CQL, ready=(cq_lo, 0) if o is None else None)
                if o is not None:
                    turn(0)
                    scores(3)
                    turn(1)
                    pe.wait_ge(h_q, o * 3 + 4)
                    pe.wait_ge(h_or, o + 1)
                    values(0)
                if o is None:
                    pe.wait_ge(kr_ready, 1)
                if n is not None:
                    job(H0 + 1, n * 4, h_q, n * 3 + 1, kt=QL, m=ROPE, hi=CQH, lo=CQL)
                if n is None:
                    part(V0, (free["mo"], 1), "mla_o", 3, 7)
                if o is not None:
                    turn(2)
                    values(1)
                if o is None:
                    pe.wait_ge(cq_lo, QL + KVL)
                if n is not None:
                    job(H0 + 2, n * 4, h_q, n * 3 + 2, kt=KVL, hi=CQH, lo=CQL, k0=QL)
                if n is None:
                    part(V0 + 1, (free["mo"], 2), "mla_o", 0, 2)
                if o is not None:
                    turn(3)
                    values(2)
                if n is None:
                    part(V0 + 1, (free["mo"], 2), "mla_o", 2, 4)
                if n is not None:
                    job(H0 + 3, n * 4, h_r, n + 1, kt=KVL, hi=CQH, lo=CQL, k0=QL, token_major=True)
                if o is not None:
                    values(3)

            mla_pipeline(pe, step)
            part(V0, (free["mo"], 1), "mla_o", KT - 1, KT)
            part(V0 + 1, (free["mo"], 2), "mla_o", 4, KT)
            six_jobs(V0, free["mo"])
            norm_sum()

            def mlp(l, j0, use):
                def up(q, i0):
                    with pe.Fori(i0, KT // 2) as i:
                        for s in range(2):
                            job(j0 + s, q * 2 * KT + i * 2, f_up[l], q * KT + i * 2 + s + 1)

                def down(q):
                    hold((f_up[l], q * KT + KT + 1))
                    for s in range(2):
                        job(j0 + KT + s, q * 2 * KT, f_dn[l], q * KT + s + 1, hi=HH, lo=HL,
                            ready=(m_hidlo, q * KT + l * NQ * KT) if s == 0 else None)
                    with pe.Fori(1, KT // 2) as i:
                        for s in range(2):
                            job(j0 + KT + s, q * 2 * KT + i * 2, f_dn[l], q * KT + i * 2 + s + 1, hi=HH, lo=HL)

                two_jobs(j0, f_up[l], use)
                up(0, 1)
                down(0)
                norm_sum()
                with pe.Fori(1, NQ) as q:
                    for s in range(2):
                        hold((f_dn[l], q * KT + s + 1))
                        job(j0 + s, q * 2 * KT, f_up[l], q * KT + s + 1)
                    up(q, 1)
                    down(q)
                norm_sum()

            mlp(0, F0, "mlp0")
            NC = T // HC

            def hgrn(n, o):
                if o is not None:
                    pe.wait_ge(g_ops, o + 1)
                    for t in range(TT):
                        pe.matmul(PB[2][:, t * P:(t + 1) * P], KREL[:, t * P:(t + 1) * P],
                                  QREL[:, t * P:(t + 1) * P], start=True, stop=True)
                    for t in range(TT):
                        mm = pe.transpose(PB[3][:, t * P:(t + 1) * P], KDEC[:, t * P:(t + 1) * P], IDENT[:, :])
                    mm.then_inc(g_sc, 1)
                if o is None:
                    two_jobs(G0, free["g"], "hgrn")
                    norm_sum()
                elif n is not None:
                    job(G0, n * 4, free["g"], n * 4 + 1)
                else:
                    pe.wait_ge(free["g"], HEADS * 4 + 2)
                    part(W0, (free["go"], 1), "hgrn_o", 0, 3, HH, HL)
                if o is not None:
                    pe.wait_ge(g_at, o + 1)
                    pe.wait_ge(g_kt, o + 1)
                    pe.wait_ge(g_vc, o + 1)
                    for c_ in range(NC - 1):
                        t, b = divmod(c_, P // HC)
                        mm = pe.matmul(PB[2 + b][:, t * P:(t + 1) * P], KDT[b * HC:(b + 1) * HC, t, :],
                                       VG[b * HC:(b + 1) * HC, t, :], start=True, stop=True)
                    mm.then_inc(g_inc, 1)
                if n is not None and o is not None:
                    job(G0 + 1, n * 4, free["g"], n * 4 + 2)
                if n is None:
                    part(W0, (free["go"], 1), "hgrn_o", 3, 7, HH, HL)
                if o is not None:
                    for t in range(TT):
                        pe.matmul(PB[6][:, t * P:(t + 1) * P], VG[:, t, :], AT[:, t, :], start=True, stop=False)
                        for b in range(P // HC):
                            c_ = t * (P // HC) + b
                            if c_:
                                pe.wait_ge(g_st, o * (NC - 1) + c_)
                                mm = pe.matmul(PB[6][:, c_ * HC:(c_ + 1) * HC], ST[:, c_, :],
                                               QDEC[:, c_ * HC:(c_ + 1) * HC], start=False,
                                               stop=(b == P // HC - 1))
                    mm.then_inc(g_out, 1)
                if n is not None:
                    job(G0 + 2, n * 4, free["g"], n * 4 + 3)
                else:
                    part(W0 + 1, (free["go"], 2), "hgrn_o", 0, 2, HH, HL)
                if o is not None:
                    pe.wait_ge(g_sq, o + 1)
                    pe.matmul(PB[7][:, :], ONES[:, :], OSQ[:, :], start=True, stop=True).then_inc(g_ss, 1)
                if n is None:
                    part(W0 + 1, (free["go"], 2), "hgrn_o", 2, 4, HH, HL)
                if n is not None:
                    job(G0 + 3, n * 4, free["g"], n * 4 + 4)
                    if o is not None:
                        pe.wait_ge(g_sd, o + 1)
                    pe.wait_ge(free["g"], n * 4 + 5)
                    for t in range(TT):
                        mm = pe.transpose(PB[7][:, t * P:(t + 1) * P], VF[:, t * P:(t + 1) * P], IDENT[:, :])
                    mm.then_inc(g_vt, 1)

            hgrn(0, None)
            with pe.Fori(1, HEADS) as h:
                hgrn(h, h - 1)
            hgrn(None, HEADS - 1)
            part(W0, (free["go"], 1), "hgrn_o", KT - 1, KT, HH, HL)
            part(W0 + 1, (free["go"], 2), "hgrn_o", 4, KT, HH, HL)
            six_jobs(W0, free["go"], hi=HH, lo=HL)
            norm_sum()
            mlp(1, E0, "mlp1")
            for k in range(KT):
                pe.wait_ge(resid_ready, 4 * KT + k + 1)
                for t in range(TT):
                    mm = pe.transpose(PB[2 * t + k // 4][:, (k % 4) * P:(k % 4 + 1) * P],
                                      XH[:, k, t * P:(t + 1) * P], IDENT[:, :])
                mm.then_inc(out_t, 1)

        @block.scalar
        def _(act):
            act.wait_ge(ada_loaded[0], 16)
            act.dma_start(XTOK[:, :, :], x[0].rearrange("(t p) d -> p t d", p=P)).then_inc(x_loaded, 16)
            act.wait_ge(c_loaded, 16)
            act.activation(CSIL[:, KT:2 * KT], CSIL[:, 0:KT], ACT.Silu).then_inc(c_ready, 1)

            def high(c0, r=0, kt=8, m=P):
                act.wait_ge(w_loaded[c0 % 2], (c0 // 2 + 1) * 16 + r * 8)
                if c0 >= 2:
                    act.wait_ge(job_done, c0 - 1 + r)
                act.activation(WH[:, c0 % 2, 0:kt, 0:m], WR[:, c0 % 2, 0:kt, 0:m], ACT.Copy).then_inc(w_hi, 1)

            for k in range(KT):
                act.wait_ge(x_turned, k + 1)
                act.activation(XH[:, k, :], PB[k % 6][:, :], ACT.Copy).then_inc(x_read, 1)
            high(0)
            high(1)
            act.drain()
            act.wait_ge(mod_ready, 1)
            act.sem_inc(free["a"], 2)
            for k in range(KT):
                act.activation(AH[:, k, :], XH[:, k, :], ACT.Identity, scale=MOD[:, KT + k:KT + k + 1],
                               bias=MOD[:, k:k + 1]).then_inc(act_hi, 1)
            for i in range(3 * JA):
                if i:
                    high(A0 + i + 1)
                act.wait_ge(job_done, A0 + i + 1)
                if i < JA:
                    act.activation(U[:, i, :], PB[(A0 + i) % 2][:, :], ACT.Gelu_apprx_tanh).then_inc(free["a"], 1)
                elif i < 2 * JA:
                    j = i - JA
                    act.activation(VFM[:, j, :], PB[(A0 + i) % 2][:, :], ACT.Gelu_apprx_tanh)\
                        .then_inc(free["a"], 1)
                    if j == JA - 1:
                        act.drain()
                        act.sem_inc(v_gelu, 1)
                else:
                    act.activation(SG[:, i - 2 * JA, :], PB[(A0 + i) % 2][:, :], ACT.Silu).then_inc(free["a"], 1)
            act.drain()
            act.sem_inc(u_ready, 1)
            act.sem_inc(free["b"], 2)

            def shifted(i, s):
                high(B0 + 1 + s, i * 2)
                act.wait_ge(job_done, B0 + 1 + s + i * 2)
                act.wait_ge(p_free, i * 2 + s + 1)
                act.activation(PR[:, s, 1:T + 1], PB[(B0 + s) % 2][:, :], ACT.Copy).then_inc(p_copied, 1)
                act.drain()
                act.sem_inc(free["b"], 1)

            shifted(0, 0)
            act.wait_ge(v_ms, 1)
            act.activation(SMALL[:, 64:96], SMALL[:, 32:64], ACT.Sqrt, scale=1.0 / HB, bias=CST[:, 0:1])\
                .then_inc(v_sd, 1)
            shifted(0, 1)
            with act.Fori(1, 2 * JA) as i:
                for s in range(2):
                    shifted(i, s)
            high(O0)
            act.wait_ge(job_done, O0)
            act.wait_ge(p_free, 4 * JA + 1)
            act.activation(PR[:, 0, 1:T + 1], PB[(O0 - 1) % 2][:, :], ACT.Copy).then_inc(p_copied, 1)
            act.wait_ge(p_mixed, 4 * JA + 1)
            act.activation(WAD[0:64, :], WAD[0:64, :], ACT.Tanh).then_inc(lr_tanh, 1)
            for j in range(JA):
                act.wait_ge(lr_done, j + 1)
                act.activation(SIG[:, j, :], PB[(6 + j) % 8][:, :], ACT.Sigmoid, bias=col("w0", j))
            act.drain()
            act.sem_inc(lr_sig, 1)
            for j in range(JA):
                act.wait_ge(lr_done, JA + j + 1)
                act.activation(ICL[:, j, :], PB[2 + j][:, :], ACT.Sigmoid, bias=col("a0", j))
            act.drain()
            act.sem_inc(lr_sig, 1)
            act.activation(RKVG[:, 3 * JA:4 * JA, :], RKVG[:, 3 * JA:4 * JA, :], ACT.Silu).then_inc(g_silu, 1)
            act.wait_ge(kk_ss, 1)
            act.activation(HST[:, :], PB[6][0:NH, :], ACT.Sqrt, bias=CST[0:NH, 1:2]).then_inc(kk_sd, 1)
            act.wait_ge(decay_ready, 1)
            act.sem_inc(y_read, 1)
            flat = "p h s -> p (h s)"

            def prepare(k):
                t0 = bass.ds(k * CH, CH)
                act.activation(EL[:, :, :], CS[:, :, t0], ACT.Exp, scale=-KAPPA)
                act.activation(ENL[:, :, :], CS[:, :, t0], ACT.Exp, scale=KAPPA)
                act.activation(EX[:, :, :], SIG[:, :, t0], ACT.Exp, scale=-KAPPA)
                act.drain()
                act.sem_inc(ch_exp, 1)

            def values(k):
                for half in range(2):
                    act.activation(VS[:, :, half * CH:(half + 1) * CH],
                                   RKVG[:, 2 * JA:3 * JA, bass.ds(k * CH, CH)], ACT.Copy)
                act.drain()
                act.sem_inc(ch_vs, 1)

            def step(k1, s1, k2, s2, k3, s3):
                if k1 is not None:
                    act.wait_ge(ch_ops, k1 + 1)
                    prepare(following(k1))
                    act.wait_ge(ch_t, k1 + 1)
                    for a in range(2):
                        rows_ = slice((1 - a) * CH, (2 - a) * CH)
                        act.activation(UV[s1][rows_, a::2, :],
                                       PB[6][rows_, :].rearrange("p (h d) -> p h d", d=HB)[:, a::2, :], ACT.Copy)
                    act.activation(BKT[s1][:, :, :].rearrange(flat), PB[5][:, :], ACT.Copy)
                    act.drain()
                    act.sem_inc(ch_tok, 1)
                    act.wait_ge(pw_pe, k1 * 4 + 1)
                    act.activation(X1T[:, :, :].rearrange(flat), PB[2][:, 0:JA * CH], ACT.Copy).then_inc(pw_act, 1)
                    values(following(k1))
                if k2 is not None:
                    act.wait_ge(in_pe, k2 * 4 + 2)
                    act.activation(FMT[:, :, :].rearrange(flat), PB[5][:, 0:JA * CH], ACT.Copy)
                    act.activation(TDT[:, :, :].rearrange(flat), PB[6][:, 0:JA * CH], ACT.Copy)
                    act.drain()
                    act.sem_inc(in_act, 1)
                if k1 is not None:
                    act.wait_ge(mv_done, k1 + 1)
                    act.activation(ZS[s1][:, :, :].rearrange(flat), PB[0][:, 0:JA * CH], ACT.Copy).then_inc(mv_read, 1)
                if k1 is not None:
                    act.wait_ge(pw_pe, k1 * 4 + 2)
                    act.activation(X1T[:, :, :].rearrange(flat), PB[2][:, 0:JA * CH], ACT.Copy).then_inc(pw_act, 1)
                if k2 is not None:
                    act.wait_ge(in_pe, k2 * 4 + 3)
                    act.activation(F2[:, :, :].rearrange(flat), PB[5][:, 0:JA * CH], ACT.Copy).then_inc(in_act, 1)
                if k3 is not None:
                    act.wait_ge(s_new, k3 + 2)
                    act.activation(YT[:, :, bass.ds(k3 * CH, CH)],
                                   PB[7][:, 0:JA * CH].rearrange("p (j t) -> p j t", j=JA), ACT.Copy)\
                        .then_inc(y_read, 1)
                if k1 is not None:
                    act.wait_ge(pw_pe, k1 * 4 + 3)
                    act.activation(X1T[:, :, :].rearrange(flat), PB[2][:, 0:JA * CH], ACT.Copy).then_inc(pw_act, 1)

            prepare(0)
            values(0)
            rwkv_pipeline(act, step)
            act.wait_ge(gn_pe, 2)
            act.activation(HST[:, :], PB[6][0:NH, :], ACT.Sqrt, scale=1.0 / HB, bias=CST[0:NH, 2:3])\
                .then_inc(gn_act, 1)
            high(O0 + 1)
            act.wait_ge(gn_rs, 1)
            for k in range(KT):
                if k >= JA:
                    act.wait_ge(ob_ready, k - JA + 1)
                src = U[:, k, :] if k < JA else CS[:, k - JA, :]
                act.activation(AH[:, k, :], src, ACT.Copy).then_inc(act_hi, 1)

            act.wait_ge(act_lo, 8 * (USE["out"] + 1))
            act.dma_start(PIX[:, :], positions[0].partition_broadcast(ROPE)).then_inc(pos_loaded, 16)
            act.dma_start(FC[:, :], inv_freq).then_inc(pos_loaded, 16)
            high(O0 + 2)
            with act.Fori(1, KT // 2) as i:
                for s in range(2):
                    high(O0 + 1 + s, i * 2)
            act.wait_ge(ln_pe, 1)
            act.activation(R2[:, :], PB[2][:, :], ACT.Copy, scale=1.0 / D).then_inc(ln_act, 1)
            for k in range(KT):
                act.wait_ge(ln_sub, k + 1)
                act.activation(LNSQ[:, k, :], M[:, k, :], ACT.Square).then_inc(ln_sq, 1)
            act.wait_ge(ln_pe, 2)
            act.activation(R2[:, :], PB[3][:, :], ACT.Sqrt, scale=1.0 / D, bias=CST[:, 0:1]).then_inc(ln_act, 1)

            norms, squares = [0], [0]

            def squares_of(src, n, ready, first):
                for k in range(n):
                    squares[0] += 1
                    if ready is not None:
                        act.wait_ge(ready, first + k)
                    act.wait_ge(nm_sq, squares[0])
                    act.activation(TMP[(squares[0] - 1) % 2][:, :], src[:, k, :], ACT.Square).then_inc(nm_act, 1)

            def deviation(n, eps=3, dst=R2, bank=2):
                norms[0] += 1
                act.wait_ge(nm_pe, norms[0])
                act.activation(dst[:, :], PB[bank][:, :], ACT.Sqrt, scale=1.0 / n, bias=CST[:, eps:eps + 1])\
                    .then_inc(nm_dev, 1)

            def pre_norm(layer, which, norm, use, c_next):
                high(c_next + 1)
                for k in range(KT):
                    act.wait_ge(resid_ready, norm * KT + k + 1)
                    act.activation(M[:, k, :], XH[:, k, :], ACT.Copy, scale=gain(layer, which, k))\
                        .then_inc(gained, 1)
                    act.activation(AH[:, k, :], XH[:, k, :], ACT.Copy, scale=gain(layer, which, k))\
                        .then_inc(act_hi, 1)
                for k in range(KT):
                    act.wait_ge(act_lo, KT * USE[use] + k + 1)
                    act.activation(M[:, k, :], XH[:, k, :], ACT.Square).then_inc(pre_sq, 1)

            pre_norm(0, 0, 0, "mla", I0)
            deviation(D)
            act.wait_ge(rp_ang, 1)
            act.activation(SIN[:, :], ANG[:, :], ACT.Sin).then_inc(rp_sin, 1)
            for j in range(1, QL + KVL):
                high(I0 + j + 1)
                squares_of(CQ[:, j - 1:j, :], 1, cq_ready, j)
                if j == 4:
                    act.wait_ge(rp_ang, 2)
                    act.activation(COS[:, :], ANG[:, :], ACT.Sin).then_inc(rp_sin, 1)
            high(H0, kt=QL)
            squares_of(CQ[:, QL + KVL - 1:QL + KVL, :], 1, cq_ready, QL + KVL)
            deviation(QL * P)
            deviation(KVL * P, dst=R3, bank=3)
            act.sem_inc(h_q, 1)
            for k in range(QL + KVL):
                if k == QL:
                    high(H0 + 1, kt=QL, m=ROPE)
                act.wait_ge(cq_hi, k + 1)
                g = col("q_norm", k) if k < QL else col("kv_norm", k - QL)
                act.activation(CQH[:, k, :], CQ[:, k, :], ACT.Copy, scale=g).then_inc(cqh_ready, 1)

            def step(n, sn, o, so, last=False):
                def exponentials(q):
                    w = (q + 1) * P
                    act.wait_ge(h_mx, o * TT + q + 1)
                    act.activation(PRB[q][:, 0:w], PB[SBANK[q]][:, 0:w], ACT.Exp, scale=SCALE,
                                   bias=SMALL[:, 8 + q:9 + q], accum_out=SMALL[:, 16 + q:17 + q])
                    act.drain()
                    act.sem_inc(h_exp, 1)

                def turned(q):
                    act.wait_ge(h_pt, o * TT + q + 1)
                    act.activation(PT[:, q % 2, 0:q + 1, :].rearrange("p b s -> p (b s)"),
                                   PB[4 + q % 2][:, 0:(q + 1) * P], ACT.Copy).then_inc(h_ptr, 1)

                if n is None:
                    high(V0 + 1)
                elif o is not None:
                    high(H0 + 1, n * 4, kt=QL, m=ROPE)
                if o is not None:
                    exponentials(0)
                    exponentials(1)
                    exponentials(2)
                if n is not None:
                    act.wait_ge(job_done, n * 4 + H0 + 1)
                    act.activation(QN[sn][:, :], PB[H0 % 2][:, :], ACT.Copy).then_inc(h_q, 1)
                    high(H0 + 2, n * 4, kt=KVL)
                if o is not None:
                    turned(0)
                    turned(1)
                    exponentials(3)
                if n is not None:
                    high(H0 + 3, n * 4, kt=KVL)
                if o is not None:
                    turned(2)
                if n is not None:
                    act.wait_ge(job_done, n * 4 + H0 + 3)
                    act.activation(KN[sn][:, :], PB[H0 % 2][:, :], ACT.Copy).then_inc(h_q, 1)
                    high(H0 + 4, n * 4, kt=KT if last else QL)
                if o is not None:
                    turned(3)
                if n is not None:
                    act.wait_ge(job_done, n * 4 + H0 + 4)
                    act.activation(VM[sn][:, :, :].rearrange("p t d -> p (t d)"), PB[(H0 + 1) % 2][:, :], ACT.Copy)\
                        .then_inc(h_q, 1)
                if o is not None:
                    act.wait_ge(h_o, o + 1)
                    act.activation(AH[:, bass.ds(o, 1), :], PB[6][:, :].rearrange("p (a t) -> p a t", a=1), ACT.Copy)\
                        .then_inc(act_hi, 1)

            mla_pipeline(act, step)

            def mixer_out(c0, fr_count):
                for k in range(KT):
                    if k:
                        high(c0 + 1 + k)
                    squares[0] += 1
                    act.wait_ge(mx_out, fr_count + k + 1)
                    act.wait_ge(nm_sq, squares[0])
                    act.activation(TMP[(squares[0] - 1) % 2][:, :], M[:, k, :], ACT.Square).then_inc(nm_act, 1)
                deviation(D)

            mixer_out(V0, 0)

            def mlp(l, j0, norm):
                act.sem_inc(f_up[l], 2)
                pre_norm(l, 2, norm, f"mlp{l}", j0)

                def up(q, first=False):
                    if first:
                        hidden(0, 0, 0)
                        high(j0 + 2)
                        hidden(0, 0, 1)
                    with act.Fori(1 if first else 0, KT // 2) as i:
                        for s in range(2):
                            high(j0 + 1 + s, q * 2 * KT + i * 2)
                            hidden(q, i, s)

                def hidden(q, i, s):
                    act.wait_ge(job_done, j0 + 1 + s + q * 2 * KT + i * 2)
                    act.wait_ge(m_hid, l * NQ * KT + q * KT + i * 2 + s + 1)
                    act.activation(TMP[2 + s][:, :], PB[(j0 + s) % 2][:, :], ACT.Relu)
                    act.drain()
                    act.sem_inc(f_up[l], 1)
                    act.sem_inc(m_relu, 1)
                    act.activation(HH[:, bass.ds(i * 2 + s, 1), :],
                                   TMP[2 + s][:, :].rearrange("p (a t) -> p a t", a=1), ACT.Square)\
                        .then_inc(m_relu, 1)

                def down(q):
                    with act.Fori(0, KT // 2) as i:
                        for s in range(2):
                            high(j0 + KT + 1 + s, q * 2 * KT + i * 2)

                up(0, first=True)
                down(0)
                deviation(D)
                with act.Fori(1, NQ - 1) as q:
                    up(q)
                    down(q)
                up(NQ - 1)
                for k in range(KT):
                    c_next = j0 + 2 * KT * NQ - KT + k + 1
                    if c_next < NJ:
                        high(c_next)
                    squares[0] += 1
                    act.wait_ge(mx_out, KT * (1 + 2 * l) + k + 1)
                    act.wait_ge(nm_sq, squares[0])
                    act.activation(TMP[(squares[0] - 1) % 2][:, :], M[:, k, :], ACT.Square).then_inc(nm_act, 1)
                deviation(D)

            act.wait_ge(lb_diff, 1)
            act.activation(LBS[:, HEADS:3 * HEADS], LBS[:, HEADS:3 * HEADS], ACT.Exp).then_inc(lb_exp, 1)
            mlp(0, F0, 1)
            pre_norm(1, 0, 2, "hgrn", G0)
            deviation(D)

            def hgrn(n, o):
                if n is None:
                    high(W0 + 1)
                elif o is None:
                    high(G0 + 2)
                    high(G0 + 3)
                else:
                    high(G0 + 1, n * 4)
                if o is not None:
                    act.wait_ge(g_sc, o + 1)
                    act.activation(KDT[:, :, :].rearrange("p t d -> p (t d)"), PB[3][:, :], ACT.Copy)\
                        .then_inc(g_kt, 1)
                if n is not None:
                    act.wait_ge(free["g"], n * 4 + 3)
                    act.activation(FG[:, :], TG[2][:, :], ACT.Sigmoid).then_inc(g_silu3, 1)
                    if o is not None:
                        high(G0 + 2, n * 4)
                    act.wait_ge(g_f, n + 1)
                    act.activation(TG[2][:, :], FG[:, :], ACT.Ln).then_inc(g_ln, 1)
                    if o is not None:
                        high(G0 + 3, n * 4)
                    act.wait_ge(free["g"], n * 4 + 4)
                    act.activation(QG[:, :], TG[1][:, :], ACT.Silu).then_inc(g_silu3, 1)
                    act.wait_ge(g_diff, n + 1)
                    act.activation(QREL[:, :], LREL[:, :], ACT.Exp)
                    act.activation(KREL[:, :], LREL[:, :], ACT.Exp, scale=-1.0)
                    act.activation(KDEC[:, :], TG[0][:, :], ACT.Exp)
                    if o is not None:
                        act.wait_ge(g_out, o + 1)
                    act.activation(QDEC[:, :], BG[:, :], ACT.Exp)
                    act.activation(EBL[:, :], BG[:, :].rearrange("p (c t) -> p c t", t=HC)[:, :, HC - 1], ACT.Exp)
                    act.drain()
                    act.sem_inc(g_exp, 1)
                if o is not None:
                    act.wait_ge(g_out, o + 1)
                    act.activation(OG[:, :], PB[6][:, :], ACT.Copy)
                    act.activation(OSQ[:, :], PB[6][:, :], ACT.Square)
                    act.drain()
                    act.sem_inc(g_sq, 1)
                if n is not None:
                    high(G0 + 4, n * 4)
                if o is not None:
                    act.wait_ge(g_ss, o + 1)
                    act.activation(OSD[:, :], PB[7][:, :], ACT.Sqrt, scale=1.0 / P, bias=CST[:, 3:4])\
                        .then_inc(g_sd, 1)
                if n is not None:
                    act.wait_ge(free["g"], n * 4 + 6)
                    if o is not None:
                        act.wait_ge(g_fin, o + 1)
                    act.activation(GG[:, :], TG[3][:, :], ACT.Silu).then_inc(g_silu3, 1)
                if o is not None:
                    act.wait_ge(g_fin, o + 1)
                    act.activation(HH[:, bass.ds(o, 1), :], OG[:, :].rearrange("p (a t) -> p a t", a=1), ACT.Copy)\
                        .then_inc(act_hi, 1)
                if n is not None:
                    act.wait_ge(g_vt, n + 1)
                    act.activation(VG[:, :, :].rearrange("p t d -> p (t d)"), PB[7][:, :], ACT.Copy)\
                        .then_inc(g_vc, 1)

            hgrn(0, None)
            with act.Fori(1, HEADS) as h:
                hgrn(h, h - 1)
            hgrn(None, HEADS - 1)
            mixer_out(W0, 2 * KT)
            mlp(1, E0, 3)
            for a in range(2):
                act.wait_ge(out_t, KT // 2 * (a + 1))
                for t in range(TT if a == 0 else TT // 2):
                    act.activation(OTOK[:, t, a * T:(a + 1) * T], PB[2 * t + a][:, :], ACT.Copy)\
                        .then_inc(out_h if a == 0 else out_r, 1)

        @block.vector
        def _(dve):
            def bc(ap, n):
                return ap.unsqueeze(2).broadcast_to([ap.shape[0], ap.shape[1], n])

            def bc1(ap, n):
                return ap.unsqueeze(1).broadcast_to([ap.shape[0], n, ap.shape[1]])

            def tt(out_, a, b, op):
                return dve.tensor_tensor(out_, a, b, op)

            def stt(out_, a, sc, b, op0, op1):
                return dve.scalar_tensor_tensor(out=out_, in0=a, scalar=sc, in1=b, op0=op0, op1=op1)

            def after(signal, n=1):
                dve.drain()
                dve.sem_inc(signal, n)

            MUL, ADD, SUB = ALU.mult, ALU.add, ALU.subtract
            dve.wait_ge(c_ready, 1)

            def weigh(n):
                dve.wait_ge(ada_loaded[n % 2], 16 * (n // 2 + 1))
                if n >= 2:
                    dve.wait_ge(ada_done, n - 1)
                for j in range(KT):
                    acc, w, cj = TMP[n % 2 * 2 + j % 2], ADA[:, n % 2, j, :], CSIL[:, KT + j:KT + j + 1]
                    if j < 2:
                        dve.tensor_scalar(acc[:, :], w, cj, None, MUL)
                    else:
                        if j % 2 == 0:
                            dve.drain()
                        stt(acc[:, :], w, cj, acc[:, :], MUL, ADD)
                dve.drain()
                dve.sem_inc(ada_used, 1)
                dve.sem_inc(ada_part, 1)

            weigh(0)
            weigh(1)
            dve.wait_ge(par_turned, 1)
            dve.tensor_copy(COL[:, 0:n_rows], PB[7][:, 0:n_rows])
            weigh(2)
            weigh(3)
            dve.wait_ge(ada_done, 4)
            tt(MOD[:, 0:2 * KT], PB[6][:, 0:2 * KT], col("b_ada", 0, 2 * KT), ADD)
            dve.drain()
            dve.tensor_scalar(MOD[:, KT:2 * KT], MOD[:, KT:2 * KT], 1.0, None, ADD).then_inc(mod_ready, 1)
            dve.drain()
            dve.wait_ge(x_read, KT)
            for k in range(KT):
                t = TMP[4 + k % 2]
                dve.tensor_scalar(t[:, :], XH[:, k, :], MOD[:, KT + k:KT + k + 1], MOD[:, k:k + 1], MUL, ADD)
                dve.drain()
                dve.wait_ge(act_hi, k + 1)
                tt(AL[:, k, :], t[:, :], AH[:, k, :].bitcast(F32), SUB).then_inc(act_lo, 1)
            weigh(4)
            weigh(5)
            dve.wait_ge(ada_done, 6)
            tt(MOD[:, 2 * KT:3 * KT], PB[6][:, 2 * KT:3 * KT], col("b_ada", 2 * KT, KT), ADD).then_inc(gate_ready, 1)
            dve.tensor_scalar(XH[:, :, :], XH[:, :, :], ALPHA, None, MUL)
            dve.memset(PR[:, :, 0:1], 0.0)
            after(p_free, 2)
            for j in range(JA):
                dve.wait_ge(v_turned, j + 1)
                dve.tensor_copy(VTOK[:, :, :].rearrange("p (t g) d -> p t (g d)", t=TT)[:, :, j * P:(j + 1) * P],
                                PB[4 + j][:, :].rearrange("p (t f) -> p t f", t=TT))
            dve.drain()
            dve.tensor_reduce(SMALL[:, 0:32], VTOK[:, :, :], AX, ADD)
            dve.drain()
            dve.tensor_scalar(SMALL[:, 0:32], SMALL[:, 0:32], 1.0 / HB, None, MUL)
            dve.drain()
            tt(VC[:, :, :], VTOK[:, :, :], bc(SMALL[:, 0:32], HB), SUB)
            dve.drain()
            tt(VSQ[:, :, :], VC[:, :, :], VC[:, :, :], MUL)
            dve.drain()
            dve.tensor_reduce(SMALL[:, 32:64], VSQ[:, :, :], AX, ADD).then_inc(v_ms, 1)
            dve.wait_ge(v_sd, 1)
            dve.reciprocal(SMALL[:, 64:96], SMALL[:, 64:96])
            dve.drain()
            tt(VC[:, :, :], VC[:, :, :], bc(SMALL[:, 64:96], HB), MUL)
            dve.drain()
            dve.wait_ge(bc_loaded, 16 * 7)
            vt = VC[:, :, :].rearrange("p (t g) d -> p t (g d)", t=TT)
            tt(vt, vt, bc1(LVG[:, :], TT), MUL)
            dve.drain()
            tt(vt, vt, bc1(LVB[:, :], TT), ADD).then_inc(v_ready, 1)
            dve.wait_ge(wsp_t, 1)
            for a in range(2):
                dve.tensor_copy(WSPT[:, 4 * a:4 * a + 4, :].rearrange("p g t -> p (g t)"), PB[2 + a][:, :])
            after(wsp_r)

            def mix(s, dst, mu):
                tt(TMP[4 + s][:, :], PR[:, s, 0:T], PR[:, s, 1:T + 1], SUB)
                dve.drain()
                stt(dst, TMP[4 + s][:, :], mu, PR[:, s, 1:T + 1], MUL, ADD)
                dve.drain()
                dve.sem_inc(p_free, 1)
                dve.sem_inc(p_mixed, 1)

            for i in range(4 * JA):
                dve.wait_ge(p_copied, i + 1)
                mix(i % 2, RKVG[:, i, :], col("mu", i))
            dve.wait_ge(p_copied, 4 * JA + 1)
            mix(0, WAD[:, :], col("mu", 4 * JA))
            dve.wait_ge(u_ready, 1)
            for j in range(JA):
                dve.wait_ge(sp_done, j + 1)
                t = TMP[4 + j % 2]
                tt(t[:, :].rearrange("p (c t) -> p c t", c=TT), PB[2 + j][:, :].rearrange("p (c t) -> p c t", c=TT),
                   bc1(BSP[:, j, :], TT), ADD)
                tt(U[:, j, :], U[:, j, :], SG[:, j, :], MUL)
                dve.drain()
                tt(U[:, j, :], U[:, j, :], t[:, :], MUL)
                dve.drain()
            dve.sem_inc(oa_ready, 1)
            R_, K_, V_, G_ = (RKVG[:, n * JA:(n + 1) * JA, :] for n in range(4))
            for j in range(JA):
                dve.tensor_scalar(KKN[:, j, :], K_[:, j, :], col("k_k", j), None, MUL)
            dve.drain()
            tt(SQB[:, :, :], KKN[:, :, :], KKN[:, :, :], MUL).then_inc(kk_sq, 1)
            dve.wait_ge(lr_sig, 1)
            for j in range(JA):
                dve.tensor_tensor_scan(CS[:, j, :], RSET[:, :], SIG[:, j, :], 0.0, MUL, ADD)
            dve.drain()
            tt(SIG[:, :, :], CS[:, :, :], SIG[:, :, :], SUB).then_inc(decay_ready, 1)
            dve.wait_ge(lr_sig, 2)
            for j in range(JA):
                t = TMP[4 + j % 2]
                dve.tensor_scalar(t[:, :], ICL[:, j, :], 1.0, col("k_a", j), SUB, MUL)
                dve.drain()
                stt(K_[:, j, :], t[:, :], 1.0, K_[:, j, :], ADD, MUL)
            dve.drain()
            dve.wait_ge(kk_ss, 1)
            for j in range(JA):
                stt(SQB[:, j, :], R_[:, j, :], col("r_k", j), K_[:, j, :], MUL, MUL)
            after(rk_ready)
            dve.wait_ge(kk_sd, 1)
            dve.reciprocal(HST[:, :], HST[:, :])
            after(kk_rs)
            dve.wait_ge(rk_done, 1)
            for j in range(JA):
                tt(BON[:, j, :], PB[2 + j][:, :], V_[:, j, :], MUL)
            for j in range(JA):
                dve.wait_ge(kk_sp, j + 1)
                tt(KKN[:, j, :], KKN[:, j, :], PB[(6 + j) % 8][:, :], MUL)
            dve.drain()
            tt(ICL[:, :, :], KKN[:, :, :], ICL[:, :, :], MUL)
            dve.memset(S[:, :, :], 0.0)
            tt(ID2[:, :], IDENT[:, 0:CH], IDENT[:, CH:P], ADD)
            dve.wait_ge(g_silu, 1)
            dve.wait_ge(const_pool, 1)
            dve.drain()
            dve.sem_inc(bulk_ready, 1)
            dve.sem_inc(s_new, 1)
            flat = "p h s -> p (h s)"

            def operands(k, slot):
                t0 = bass.ds(k * CH, CH)
                stt(AR[slot][:, :, 0:CH], KKN[:, :, t0], -1.0, EX[:, :, :], MUL, MUL)
                tt(AR[slot][:, :, CH:P], R_[:, :, t0], EL[:, :, :], MUL)
                for p in (0, CH):
                    tt(BK[p:p + CH, :, p:p + CH], ICL[p:p + CH, :, t0], ENL[p:p + CH, :, :], MUL)
                    tt(BK[p:p + CH, :, CH - p:P - p], K_[p:p + CH, :, t0], ENL[p:p + CH, :, :], MUL)

            def copied(dst, bank, signal):
                dve.tensor_copy(dst[:, :, :].rearrange(flat), PB[bank][:, 0:JA * CH]).then_inc(signal, 1)

            def added(dst, bank, plus, signal):
                tt(dst[:, :, :].rearrange(flat), PB[bank][:, 0:JA * CH], plus[:, :, :].rearrange(flat), ADD)\
                    .then_inc(signal, 1)

            def step(k1, s1, k2, s2, k3, s3):
                if k2 is not None:
                    dve.wait_ge(pw_pe, k2 * 4 + 4)
                    added(TDF, 0, TD, pw_dve)
                    dve.drain()
                if k1 is not None:
                    dve.wait_ge(ch_g, k1 + 1)
                    for a in range(2):
                        g = PB[1 + a][:, :].rearrange("p (h s) -> p h s", s=P)
                        tt(GA[:, a::2, :], g[:, :, 0:CH], bc1(MSKG[:, 0:CH], JA), MUL)
                    tt(ND[:, :, :], PB[3][:, 0:JA * CH].rearrange("p (h s) -> p h s", s=CH), bc1(MSKSD[:, :], JA),
                       MUL)
                    dve.drain()
                    for a in range(2):
                        half = slice(a * CH, (a + 1) * CH)
                        tt(NDT[half, :, :], GA[half, a::2, :], bc1(MSKD[half, :], JA), MUL)
                    tt(TD[:, :, :], ND[:, :, :], bc1(ID2[:, :], JA), ADD)
                    for a in range(2):
                        g = PB[1 + a][:, :].rearrange("p (h s) -> p h s", s=P)
                        tt(GR[s1][:, a::2, :], g[:, :, CH:P], bc1(MSKG[:, CH:P], JA), MUL)
                    after(ch_nd)
                if k2 is not None:
                    dve.wait_ge(in_pe, k2 * 4 + 1)
                    copied(FM, 0, in_dve)
                if k3 is not None:
                    dve.wait_ge(mv_read, k3 + 1)
                    dve.wait_ge(z_done, k3 + 1)
                    added(ZS[s3], 4, ZS[s3], z_read)
                if k1 is not None:
                    dve.wait_ge(pw_pe, k1 * 4 + 1)
                    copied(X1, 1, pw_dve)
                if k3 is not None:
                    dve.wait_ge(u_done, k3 + 1)
                    for a in range(2):
                        half = slice(a * CH, (a + 1) * CH)
                        dve.tensor_copy(UV[s3][half, a::2, :],
                                        PB[4][half, 0:JA * CH].rearrange("p (j d) -> p j d", d=HB))
                    after(u_read)
                if k1 is not None:
                    dve.wait_ge(ch_exp, k1 + 2)
                    operands(following(k1), (s1 + 1) % 3)
                if k1 is not None:
                    dve.wait_ge(pw_pe, k1 * 4 + 2)
                    dve.tensor_copy(X1[:, :, :].rearrange(flat), PB[1][:, 0:JA * CH])
                    added(TD, 3, TD, pw_dve)
                    for a in range(2):
                        half = slice(a * CH, (a + 1) * CH)
                        tt(NOT[half, :, :], GA[half, a::2, :], NDT[half, :, :], SUB)
                if k2 is not None:
                    dve.wait_ge(in_pe, k2 * 4 + 3)
                    added(Y1, 0, TDT, in_dve)
                if k3 is not None:
                    dve.wait_ge(y_done, k3 + 1)
                    sv = S[:, :, :].rearrange("p j i -> p (j i)")
                    tt(sv, PB[7][:, JA * CH:], sv, ADD)
                    dve.drain()
                    tt(S[:, :, :], S[:, :, :], bc(FS[:, s3, :], CH), MUL)
                    after(s_new)
                if k1 is not None:
                    dve.tensor_copy(FS[:, (s1 + 1) % 3, :], EL[:, :, CH - 1])
                    after(ch_ops)
                if k1 is not None:
                    dve.wait_ge(pw_pe, k1 * 4 + 3)
                    added(TD, 3, TD, pw_dve)
                if k2 is not None:
                    dve.drain()
                    dve.wait_ge(in_pe, k2 * 4 + 4)
                    added(TTM, 5, Y1, in_dve)

            dve.wait_ge(ch_exp, 1)
            operands(0, 0)
            dve.tensor_copy(FS[:, 0, :], EL[:, :, CH - 1])
            after(ch_ops)
            rwkv_pipeline(dve, step)
            dve.wait_ge(gn_pe, 1)
            for j in range(JA):
                stt(YT[:, j, :], PB[2 + j][:, :], -1.0 / HB, YT[:, j, :], MUL, ADD)
            dve.drain()
            tt(SQB[:, :, :], YT[:, :, :], YT[:, :, :], MUL)
            after(gn_dve)
            dve.wait_ge(gn_act, 1)
            dve.reciprocal(HST[:, :], HST[:, :])
            after(gn_rs)

            def low_out(k):
                src = U[:, k, :] if k < JA else CS[:, k - JA, :]
                dve.wait_ge(act_hi, 8 * USE["out"] + k + 1)
                tt(AL[:, k, :], src, AH[:, k, :].bitcast(F32), SUB).then_inc(act_lo, 1)

            dve.sem_inc(free["o"], 2)
            for k in range(JA):
                low_out(k)
            for j in range(JA):
                dve.wait_ge(gn_sp, j + 1)
                tt(KKN[:, j, :], YT[:, j, :], PB[2 + j][:, :], MUL)
                dve.drain()
                dve.tensor_scalar(KKN[:, j, :], KKN[:, j, :], col("gn_g", j), col("gn_b", j), MUL, ADD)
                dve.drain()
                tt(KKN[:, j, :], KKN[:, j, :], BON[:, j, :], ADD)
                if j:
                    low_out(JA + j - 1)
                dve.drain()
                tt(CS[:, j, :], KKN[:, j, :], G_[:, j, :], MUL)
                after(ob_ready)
            low_out(2 * JA - 1)
            for k in range(KT):
                dve.wait_ge(job_done, O0 + k + 1)
                stt(M[:, k, :], PB[(O0 + k) % 2][:, :], MOD[:, 2 * KT + k:2 * KT + k + 1], XH[:, k, :], MUL, ADD)\
                    .then_inc(free["o"], 1)
                dve.drain()
                if k == 0:
                    dve.tensor_copy(SQA[:, :], M[:, k, :])
                else:
                    tt(SQA[:, :], SQA[:, :], M[:, k, :], ADD)
            after(ln_dve)
            dve.wait_ge(ln_act, 1)
            for k in range(KT):
                tt(M[:, k, :], M[:, k, :], R2[:, :], SUB).then_inc(ln_sub, 1)
            dve.drain()
            dve.wait_ge(ln_act, 2)
            dve.reciprocal(R1[:, :], R2[:, :])
            dve.drain()
            dve.sem_inc(free["mi"], 2)

            def residual_tiles(r, new_tile):
                for k in range(KT + 1):
                    if k < KT:
                        tt(M[:, k, :], M[:, k, :], r[:, :], MUL)
                    if k:
                        new_tile(k - 1)
                    dve.drain()
                    if k:
                        dve.sem_inc(resid_ready, 1)

            residual_tiles(R1, lambda k: dve.tensor_scalar(XH[:, k, :], M[:, k, :], col("ln_g", k), col("ln_b", k),
                                                           MUL, ADD))

            squares, devs = [0], [0]

            def inverse(dst, src=R2):
                devs[0] += 1
                dve.wait_ge(nm_dev, devs[0])
                dve.reciprocal(dst[:, :], src[:, :])
                dve.drain()

            def add_to_residual(layer, which):
                inverse(R2)
                residual_tiles(R2, lambda k: stt(XH[:, k, :], M[:, k, :], gain(layer, which, k), XH[:, k, :], MUL,
                                                 ADD))

            dve.wait_ge(pos_loaded, 32)
            dve.tensor_copy(ANG[:, :], PIX[:, :])
            dve.drain()
            dve.tensor_scalar(ANG[:, :], ANG[:, :], FC[:, 0:1], None, MUL)
            dve.drain()
            dve.tensor_scalar(ANGK[:, :], ANG[:, :], float(1 / (2 * np.pi)), None, MUL)
            dve.drain()
            dve.tensor_copy(SIN[:, :], ANGK[:, :])
            dve.drain()
            hi1 = 6.28125
            hi2 = float(np.float32(2 * np.pi - hi1))
            hi2 = float(np.frombuffer((np.frombuffer(np.float32(hi2).tobytes(), np.uint32) & np.uint32(0xFFFFF000))
                                      .tobytes(), np.float32)[0])
            for part in (hi1, hi2, float(2 * np.pi - hi1 - hi2)):
                stt(ANG[:, :], SIN[:, :], -part, ANG[:, :], MUL, ADD)
                dve.drain()
            dve.tensor_scalar(ANG[:, :], ANG[:, :], -3.1415925, 3.1415925, ALU.max, ALU.min)
            after(rp_ang)
            def rope(dst, src, a, b):
                hf = ROPE // 2
                tt(a[0:ROPE, :], src, COS[:, :], MUL)
                tt(b[0:hf, :], src[hf:ROPE, :], SIN[hf:ROPE, :], MUL)
                tt(b[hf:ROPE, :], src[0:hf, :], SIN[0:hf, :], MUL)
                dve.drain()
                return tt(dst, a[0:ROPE, :], b[0:ROPE, :], ADD)

            dve.sem_inc(nm_sq, 2)
            add_tile_squares(dve, 0)
            inverse(R1)

            def latent_square(k):
                squares[0] += 1
                dve.wait_ge(nm_act, squares[0])
                t, total = TMP[(squares[0] - 1) % 2], (SQA if k < QL else SQK)
                if k in (0, QL):
                    dve.tensor_copy(total[:, :], t[:, :]).then_inc(nm_sq, 1)
                else:
                    tt(total[:, :], total[:, :], t[:, :], ADD).then_inc(nm_sq, 1)
                dve.drain()
                if k in (QL - 1, QL + KVL - 1):
                    dve.sem_inc(nm_dve, 1)

            for k in range(QL + KVL):
                if k == 3:
                    dve.wait_ge(rp_sin, 1)
                    dve.tensor_scalar(ANG[:, :], ANG[:, :], float(np.pi / 2), None, ADD)
                    dve.drain()
                    dve.tensor_scalar(COS[:, :], ANG[:, :], float(np.pi), float(-2 * np.pi), ALU.is_gt, MUL)
                    dve.drain()
                    tt(ANG[:, :], ANG[:, :], COS[:, :], ADD)
                    dve.drain()
                    dve.tensor_scalar(ANG[:, :], ANG[:, :], -3.1415925, 3.1415925, ALU.max, ALU.min)
                    after(rp_ang)

                dve.wait_ge(job_done, I0 + k + 1)
                tt(CQ[:, k, :], PB[(I0 + k) % 2][:, :], R1[:, :], MUL)
                dve.drain()
                dve.sem_inc(free["mi"], 1)
                dve.sem_inc(cq_ready, 1)
                if k:
                    latent_square(k - 1)
            latent_square(QL + KVL - 1)
            dve.tensor_scalar(SIN[ROPE // 2:ROPE, :], SIN[ROPE // 2:ROPE, :], -1.0, None, MUL)
            dve.wait_ge(rp_sin, 2)

            def latents(k0, n, norm, r):
                for k in range(n + 1):
                    if k < n:
                        tt(CQ[:, k0 + k, :], CQ[:, k0 + k, :], r[:, :], MUL)
                        after(cq_hi)
                    if k:
                        dve.wait_ge(cqh_ready, k0 + k)
                        stt(CQL[:, k0 + k - 1, :], CQ[:, k0 + k - 1, :], col(norm, k - 1),
                            CQH[:, k0 + k - 1, :].bitcast(F32), MUL, SUB).then_inc(cq_lo, 1)

            inverse(TMP[3])
            latents(0, QL, "q_norm", TMP[3])
            dve.wait_ge(job_done, H0)
            tt(TMP[2][0:ROPE, :], PB[(H0 - 1) % 2][0:ROPE, :], R1[0:ROPE, :], MUL)
            dve.drain()
            rope(KR[:, :], TMP[2][0:ROPE, :], TMP[4], TMP[5])
            after(kr_ready)
            inverse(R3, R3)
            latents(QL, KVL, "kv_norm", R3)
            dve.sem_inc(h_or, 1)
            dve.wait_ge(const_pool, 2)

            def step(n, sn, o, so, last=False):
                def row_max(q):
                    w = (q + 1) * P
                    ps = PB[SBANK[q]]
                    dve.wait_ge(h_s, o * TT + q + 1)
                    tt(ps[:, q * P:w], ps[:, q * P:w], CMASK[:, :], ADD)
                    dve.drain()
                    dve.tensor_reduce(SMALL[:, q:q + 1], ps[:, 0:w], AX, ALU.max)
                    dve.drain()
                    dve.tensor_scalar(SMALL[:, 8 + q:9 + q], SMALL[:, q:q + 1], -SCALE, None, MUL).then_inc(h_mx, 1)

                def normalise(q):
                    w = (q + 1) * P
                    dve.wait_ge(h_exp, o * TT + q + 1)
                    dve.reciprocal(SMALL[:, 24 + q:25 + q], SMALL[:, 16 + q:17 + q])
                    dve.drain()
                    dve.tensor_scalar(PRB[q][:, 0:w], PRB[q][:, 0:w], SMALL[:, 24 + q:25 + q], None, MUL)\
                        .then_inc(h_pn, 1)

                if o is not None:
                    row_max(0)
                    row_max(1)
                    normalise(0)
                    row_max(2)
                    normalise(1)
                    row_max(3)
                    normalise(2)
                    normalise(3)
                if n is not None:
                    dve.wait_ge(job_done, n * 4 + H0 + 2)
                    rope(QR[sn][:, :], PB[(H0 + 1) % 2][0:ROPE, :], TMP[4], TMP[5])
                    after(h_r)
                if o is not None:
                    dve.wait_ge(act_hi, o + 8 * USE["mla_o"] + 1)
                    tt(AL[:, bass.ds(o, 1), :], PB[6][:, :].rearrange("p (a t) -> p a t", a=1),
                       AH[:, bass.ds(o, 1), :].bitcast(F32), SUB)
                    dve.drain()
                    dve.sem_inc(act_lo, 1)
                    dve.sem_inc(h_or, 1)

            dve.sem_inc(free["mo"], 2)
            mla_pipeline(dve, step)

            def read_mixer(c0, fr):
                for k in range(KT):
                    dve.wait_ge(job_done, c0 + k + 1)
                    dve.tensor_copy(M[:, k, :], PB[(c0 + k) % 2][:, :])
                    dve.drain()
                    dve.sem_inc(fr, 1)
                    dve.sem_inc(mx_out, 1)
                    if k:
                        one_square(k - 1)
                one_square(KT - 1)
                dve.sem_inc(nm_dve, 1)

            def one_square(k):
                squares[0] += 1
                dve.wait_ge(nm_act, squares[0])
                t = TMP[(squares[0] - 1) % 2]
                if k == 0:
                    dve.tensor_copy(SQA[:, :], t[:, :]).then_inc(nm_sq, 1)
                else:
                    tt(SQA[:, :], SQA[:, :], t[:, :], ADD).then_inc(nm_sq, 1)
                dve.drain()

            read_mixer(V0, free["mo"])
            n = HEADS
            l0, l1 = col("lb", 0, n), col("lb", n, n)
            tt(LBS[:, 0:n], l0, l1, ALU.max)
            dve.drain()
            tt(LBS[:, n:2 * n], l0, LBS[:, 0:n], SUB)
            tt(LBS[:, 2 * n:3 * n], l1, LBS[:, 0:n], SUB)
            after(lb_diff)
            add_to_residual(0, 1)

            def mlp(l, j0):
                if l == 0:
                    dve.sem_inc(m_hid, 2)
                dve.sem_inc(f_dn[l], 2)

                def up(q):
                    with dve.Fori(0, KT // 2) as i:
                        for s in range(2):
                            n = l * NQ * KT + q * KT + i * 2 + s
                            dve.wait_ge(m_relu, n * 2 + 1)
                            tt(TMP[4 + s][:, :], TMP[2 + s][:, :], TMP[2 + s][:, :], MUL)
                            after(m_hid)
                            dve.wait_ge(m_relu, n * 2 + 2)
                            tt(HL[:, bass.ds(i * 2 + s, 1), :], TMP[4 + s][:, :].rearrange("p (a t) -> p a t", a=1),
                               HH[:, bass.ds(i * 2 + s, 1), :].bitcast(F32), SUB).then_inc(m_hidlo, 1)

                def down(q, first):
                    with dve.Fori(0, KT // 2) as i:
                        for s in range(2):
                            dve.wait_ge(job_done, q * 2 * KT + i * 2 + j0 + KT + s + 1)
                            m = M[:, bass.ds(i * 2 + s, 1), :]
                            ps = PB[(j0 + s) % 2][:, :].rearrange("p (a t) -> p a t", a=1)
                            if first:
                                dve.tensor_copy(m, ps).then_inc(f_dn[l], 1)
                            else:
                                tt(m, ps, m, ADD).then_inc(f_dn[l], 1)
                            dve.drain()

                up(0)
                add_tile_squares(dve, 1 + 2 * l)
                down(0, True)
                inverse(R1)
                tt(R1[:, :], R1[:, :], R1[:, :], MUL)
                dve.drain()
                with dve.Fori(1, NQ - 1) as q:
                    up(q)
                    down(q, False)
                up(NQ - 1)
                for k in range(KT):
                    dve.wait_ge(job_done, j0 + 2 * KT * NQ - KT + k + 1)
                    tt(M[:, k, :], PB[(j0 + k) % 2][:, :], M[:, k, :], ADD).then_inc(f_dn[l], 1)
                    dve.drain()
                    tt(M[:, k, :], M[:, k, :], R1[:, :], MUL)
                    after(mx_out)
                    if k:
                        one_square(k - 1)
                one_square(KT - 1)
                dve.sem_inc(nm_dve, 1)
                if l == 0:
                    dve.sem_inc(free["g"], 2)
                    add_to_residual(0, 3)
                else:
                    add_to_residual(1, 3)

            mlp(0, F0)
            dve.wait_ge(lb_exp, 1)
            tt(LBS[:, 0:n], LBS[:, n:2 * n], LBS[:, 2 * n:3 * n], ADD)
            dve.drain()
            dve.reciprocal(LBS[:, 0:n], LBS[:, 0:n])
            dve.drain()
            tt(LBS[:, n:2 * n], LBS[:, n:2 * n], LBS[:, 0:n], MUL)
            tt(LBS[:, 2 * n:3 * n], LBS[:, 2 * n:3 * n], LBS[:, 0:n], MUL)
            dve.drain()
            tt(LBS[:, 2 * n:3 * n], LBS[:, n:2 * n], LBS[:, 2 * n:3 * n], ADD)
            dve.drain()
            tt(LBS[:, 0:n], LBS[:, 2 * n:3 * n], LBS[:, n:2 * n], SUB)
            dve.drain()
            dve.tensor_scalar(LBS[:, n:2 * n], LBS[:, 0:n], -1.0, 1.0, MUL, ADD)
            add_tile_squares(dve, 2)
            inverse(R1)
            dve.wait_ge(const_pool, 3)

            def hgrn(n, o):
                def scaled(j, dst):
                    dve.wait_ge(job_done, n * 4 + G0 + j + 1)
                    tt(dst[:, :], PB[(G0 + j) % 2][:, :], R1[:, :], MUL).then_inc(free["g"], 1)

                if o is not None:
                    dve.wait_ge(const_pool, 3)
                    dve.wait_ge(g_sc, o + 1)
                    dve.copy_predicated(AT[:, :, :].rearrange("p t s -> p (t s)"),
                                        HMSK[:, :, :].rearrange("p t s -> p (t s)"), PB[2][:, :]).then_inc(g_at, 1)
                if n is not None:
                    scaled(0, TG[2])
                    dve.tensor_copy(LBH[:, 0:1], LBS[:, bass.ds(n, 1)])
                    dve.tensor_copy(LBH[:, 1:2], LBS[:, bass.ds(n + HEADS, 1)])
                    dve.drain()
                    dve.wait_ge(g_silu3, n * 3 + 1)
                    dve.tensor_scalar(FG[:, :], FG[:, :], LBH[:, 1:2], LBH[:, 0:1], MUL, ADD)
                    after(g_f)
                    dve.tensor_scalar(KG[:, :], FG[:, :], -1.0, 1.0, MUL, ADD)
                if o is not None:
                    dve.wait_ge(g_inc, o + 1)
                    for k in range(T // HC - 1):
                        ps = PB[2 + k % (P // HC)][:, k // (P // HC) * P:(k // (P // HC) + 1) * P]
                        if k == 0:
                            dve.tensor_copy(ST[:, 1, :], ps).then_inc(g_st, 1)
                        else:
                            stt(ST[:, k + 1, :], ST[:, k, :], EBL[:, k:k + 1], ps, MUL, ADD).then_inc(g_st, 1)
                        dve.drain()
                if n is not None:
                    dve.wait_ge(g_ln, n + 1)
                    dve.tensor_tensor_scan(BG[:, :], HRST[:, :], TG[2][:, :], 0.0, MUL, ADD)
                    scaled(1, TG[1])
                    dve.drain()
                    b3 = BG[:, :].rearrange("p (c t) -> p c t", t=HC)
                    tt(LREL[:, :].rearrange("p (c t) -> p c t", t=HC), b3, bc(b3[:, :, HC // 2], HC), SUB)
                    tt(TG[0][:, :].rearrange("p (c t) -> p c t", t=HC), bc(b3[:, :, HC - 1], HC), b3, SUB)
                    after(g_diff)
                    dve.wait_ge(g_exp, n + 1)
                    for a, b in ((QREL, QG), (KREL, KG), (QDEC, QG), (KDEC, KG)):
                        tt(a[:, :], a[:, :], b[:, :], MUL)
                    after(g_ops)
                    scaled(2, VF)
                if o is not None:
                    dve.wait_ge(g_sd, o + 1)
                    dve.reciprocal(OSD[:, :], OSD[:, :])
                    dve.drain()
                    stt(OG[:, :], OG[:, :], col("o_norm"), OSD[:, :], MUL, MUL)
                    dve.drain()
                    dve.wait_ge(g_silu3, o * 3 + 3)
                    tt(OG[:, :], OG[:, :], GG[:, :], MUL)
                    after(g_fin)
                if n is not None:
                    scaled(3, TG[3])
                if o is not None:
                    dve.wait_ge(act_hi, o + 8 * USE["hgrn_o"] + 1)
                    tt(HL[:, bass.ds(o, 1), :], OG[:, :].rearrange("p (a t) -> p a t", a=1),
                       HH[:, bass.ds(o, 1), :].bitcast(F32), SUB).then_inc(act_lo, 1)

            dve.sem_inc(free["go"], 2)
            hgrn(0, None)
            with dve.Fori(1, HEADS) as h:
                hgrn(h, h - 1)
            hgrn(None, HEADS - 1)
            dve.drain()
            read_mixer(W0, free["go"])
            add_to_residual(1, 1)
            mlp(1, E0)
            dve.wait_ge(out_t, KT)
            for t in range(TT // 2, TT):
                dve.tensor_copy(OTOK[:, t, T:2 * T], PB[2 * t + 1][:, :]).then_inc(out_r, 1)
    return nc


INS = ['x', 'c', 'w_ada', 'b_ada', 'w_in', 'mu_b', 'ln_v_g', 'ln_v_b', 'w_spatial', 'b_spatial', 'w0', 'w_up', 'a0',
       'a_up', 'k_k', 'k_a', 'r_k', 'gn_g', 'gn_b', 'w_out', 'ln_g', 'ln_b', 'positions_2', 'norm_gains_2',
       'mla_w_in_2', 'mla_q_norm_2', 'mla_kv_norm_2', 'mla_w_uq_2', 'mla_w_ukv_2', 'mla_w_o_2', 'hgrn_w_in_2',
       'hgrn_lb_logits_2', 'hgrn_o_norm_2', 'hgrn_w_o_2', 'mlp_w1_2', 'mlp_w2_2']


def kernel(**inputs):
    import concourse.bacc as bacc
    from concourse.bass_utils import run_bass_kernel_spmd

    nc = bacc.Bacc("TRN2", target_bir_lowering=False, num_devices=1)
    arrays = {f"in_{name}": np.ascontiguousarray(inputs[name]) for name in INS}
    half = 32
    freq = (10000.0 ** (-np.arange(half, dtype=np.float64) / half)).astype(np.float32)
    arrays["inv_freq"] = np.concatenate([freq, freq]).reshape(2 * half, 1)
    aps = [nc.dram_tensor(name, a.shape, mybir.dt.from_np(a.dtype), kind="ExternalInput").ap()
           for name, a in arrays.items()]
    out = nc.dram_tensor("out", inputs["x"].shape, F32, kind="ExternalOutput").ap()
    block_kernel(nc, *aps, out)
    r = run_bass_kernel_spmd(nc, [arrays], core_ids=[0])
    return r.results[0]["out"]
```
